# Optimizing a Trainium2 kernel written in Bass

```python
import jax
import jax.numpy as jnp
from jax import lax
import numpy as np

D_MODEL = 1024
BATCH = 1
SEQ = 512
DEPTH = 2

GRID_W = 64
CTX_LEN = 256
N_MIXERS = 4
GROUP_W = D_MODEL // N_MIXERS
HEAD_DIM = 64
N_Q_HEADS = GROUP_W // HEAD_DIM
N_KV_HEADS = 2
Q_PER_KV = N_Q_HEADS // N_KV_HEADS
KV_W = N_KV_HEADS * HEAD_DIM
ATTN_SCALE = HEAD_DIM ** -0.5
Q_BLOCK = 128
WINDOW = 128
ROPE_THETA = 10000.0
ROPE_FREQS = HEAD_DIM // 4
CONV_WIDTH = 31
CONV_PAD = CONV_WIDTH // 2
HGRN_HEADS = 4
HGRN_KEY = GROUP_W // HGRN_HEADS
HGRN_VAL = GROUP_W // HGRN_HEADS
SCAN_CHUNK = 64
N_EXPERTS = 64
TOP_K = 8
N_EXPERT_GROUPS = 8
TOPK_GROUPS = 4
EXPERT_HIDDEN = 256
SHARED_HIDDEN = 256
ROUTED_SCALE = 2.5
MOE_BLOCK = 128
EPS = 1e-6
F32 = jnp.float32
IN_SPLITS = (GROUP_W, KV_W, KV_W, GROUP_W, KV_W, KV_W, GROUP_W, GROUP_W,
             GROUP_W, GROUP_W, GROUP_W, GROUP_W, GROUP_W)
D_IN = sum(IN_SPLITS)

kernel_name = 'hybrid_parallel_heads_dit_block'

def rms_norm(x, g):
    xf = x.astype(F32)
    y = xf * lax.rsqrt(jnp.mean(xf * xf, axis=-1, keepdims=True) + EPS)
    return (y * g.astype(F32)).astype(x.dtype)

def layer_norm(x, g, b):
    xf = x.astype(F32)
    xc = xf - jnp.mean(xf, axis=-1, keepdims=True)
    y = xc * lax.rsqrt(jnp.mean(xc * xc, axis=-1, keepdims=True) + EPS)
    return (y * g.astype(F32) + b.astype(F32)).astype(x.dtype)

def modulate(h, shift, scale):
    return h * (1.0 + scale) + shift

def split_cols(p):
    cuts = [int(v) for v in np.cumsum(IN_SPLITS)[:-1]]
    return jnp.split(p, cuts, axis=-1)

def split_heads(t, n_heads, dim):
    return t.reshape(t.shape[:-1] + (n_heads, dim))

def axial_rope(n):
    n_rows = n // GRID_W
    row = jnp.broadcast_to(jnp.arange(n_rows)[:, None], (n_rows, GRID_W)).reshape(n)
    col = jnp.broadcast_to(jnp.arange(GRID_W)[None, :], (n_rows, GRID_W)).reshape(n)
    inv_freq = jnp.power(ROPE_THETA, -jnp.arange(ROPE_FREQS, dtype=F32) / ROPE_FREQS)
    ang = jnp.stack([row.astype(F32)[:, None] * inv_freq,
                     col.astype(F32)[:, None] * inv_freq], axis=1)
    return jnp.cos(ang), jnp.sin(ang)

def apply_rope(x, rope):
    cos, sin = rope
    b, n, h, _ = x.shape
    xr = x.astype(F32).reshape(b, n, h, 2, 2, ROPE_FREQS)
    x1, x2 = xr[..., 0, :], xr[..., 1, :]
    cs, sn = cos[None, :, None], sin[None, :, None]
    out = jnp.stack([x1 * cs - x2 * sn, x1 * sn + x2 * cs], axis=-2)
    return out.reshape(b, n, h, HEAD_DIM).astype(x.dtype)

def attn_heads(qx, kx, vx, q_gain, k_gain, rope=None):
    q = rms_norm(split_heads(qx, N_Q_HEADS, HEAD_DIM), q_gain)
    k = rms_norm(split_heads(kx, N_KV_HEADS, HEAD_DIM), k_gain)
    if rope is not None:
        q, k = apply_rope(q, rope), apply_rope(k, rope)
    return q, k, split_heads(vx, N_KV_HEADS, HEAD_DIM)

def ctx_attention(q_c, k_c, v_c, sink=None):
    b, l = q_c.shape[:2]
    qg = q_c.reshape(b, l, N_KV_HEADS, Q_PER_KV, HEAD_DIM)
    s = jnp.einsum('bqkgd,bskd->bkgqs', qg, k_c, preferred_element_type=F32) * ATTN_SCALE
    if sink is not None:
        s_sink = jnp.broadcast_to(sink.astype(F32).reshape(1, N_KV_HEADS, Q_PER_KV, 1, 1), s.shape[:-1] + (1,))
        s = jnp.concatenate([s, s_sink], axis=-1)
    p = jax.nn.softmax(s, axis=-1)[..., :l].astype(v_c.dtype)
    return jnp.einsum('bkgqs,bskd->bqkgd', p, v_c).reshape(b, l, GROUP_W)

def global_attention(q, k, v, k_c, v_c):
    b, n = q.shape[:2]
    nb = n // Q_BLOCK
    k_all = jnp.concatenate([k, k_c], axis=1)
    v_all = jnp.concatenate([v, v_c], axis=1)
    q_blocks = q.reshape(b, nb, Q_BLOCK, N_KV_HEADS, Q_PER_KV, HEAD_DIM).transpose(1, 0, 2, 3, 4, 5)

    def block(qb):
        s = jnp.einsum('bqkgd,bskd->bkgqs', qb, k_all, preferred_element_type=F32) * ATTN_SCALE
        p = jax.nn.softmax(s, axis=-1).astype(v_all.dtype)
        return jnp.einsum('bkgqs,bskd->bqkgd', p, v_all)

    o = lax.map(block, q_blocks)
    return o.transpose(1, 0, 2, 3, 4, 5).reshape(b, n, GROUP_W)

def window_attention(q, k, v, k_c, v_c, sink):
    b, n = q.shape[:2]
    l = k_c.shape[1]
    nb = n // Q_BLOCK
    span = 3 * Q_BLOCK

    def band(t):
        tp = jnp.pad(t, ((0, 0), (WINDOW, WINDOW), (0, 0), (0, 0)))
        tp = tp.reshape(b, nb + 2, Q_BLOCK, N_KV_HEADS, HEAD_DIM)
        return jnp.concatenate([tp[:, :-2], tp[:, 1:-1], tp[:, 2:]], axis=2)

    kb, vb = band(k), band(v)
    qb = q.reshape(b, nb, Q_BLOCK, N_KV_HEADS, Q_PER_KV, HEAD_DIM)
    s_loc = jnp.einsum('bnqkgd,bnskd->bnkgqs', qb, kb, preferred_element_type=F32) * ATTN_SCALE
    q_pos = jnp.arange(nb)[:, None] * Q_BLOCK + jnp.arange(Q_BLOCK)[None, :]
    k_pos = jnp.arange(nb)[:, None] * Q_BLOCK - WINDOW + jnp.arange(span)[None, :]
    inside = ((jnp.abs(q_pos[:, :, None] - k_pos[:, None, :]) <= WINDOW)
              & (k_pos[:, None, :] >= 0) & (k_pos[:, None, :] < n))
    s_loc = jnp.where(inside[None, :, None, None], s_loc, -jnp.inf)
    s_ctx = jnp.einsum('bnqkgd,bskd->bnkgqs', qb, k_c, preferred_element_type=F32) * ATTN_SCALE
    s_sink = jnp.broadcast_to(sink.astype(F32).reshape(1, 1, N_KV_HEADS, Q_PER_KV, 1, 1), s_loc.shape[:-1] + (1,))
    p = jax.nn.softmax(jnp.concatenate([s_loc, s_ctx, s_sink], axis=-1), axis=-1).astype(v.dtype)
    o = (jnp.einsum('bnkgqs,bnskd->bnqkgd', p[..., :span], vb)
         + jnp.einsum('bnkgqs,bskd->bnqkgd', p[..., span:span + l], v_c))
    return o.reshape(b, n, GROUP_W)

def conformer_conv(val, gate, dw_w, dw_b, ln_g, ln_b, pw_w, pw_b):
    h = val * jax.nn.sigmoid(gate)
    h = lax.conv_general_dilated(h, dw_w[:, None, :].astype(h.dtype), window_strides=(1,),
                                 padding=[(CONV_PAD, CONV_PAD)],
                                 dimension_numbers=('NWC', 'WIO', 'NWC'),
                                 feature_group_count=GROUP_W) + dw_b
    h = jax.nn.silu(layer_norm(h, ln_g, ln_b))
    return h @ pw_w + pw_b

def gla_chunk_scan(q, k, v, logf, s0):
    b, n, h, _ = q.shape
    dv = v.shape[-1]
    nc = n // SCAN_CHUNK

    def chunks(t):
        return t.astype(F32).reshape(b, nc, SCAN_CHUNK, h, t.shape[-1]).transpose(1, 0, 3, 2, 4)

    lower = jnp.tril(jnp.ones((SCAN_CHUNK, SCAN_CHUNK), dtype=bool))[:, :, None]

    def step(state, inp):
        qc, kc, vc, gc = inp
        cum = jnp.cumsum(gc, axis=2)
        last = cum[:, :, -1:, :]
        rel = cum[:, :, :, None, :] - cum[:, :, None, :, :]
        decay = jnp.exp(jnp.where(lower, rel, -jnp.inf))
        scores = jnp.einsum('bhtd,bhsd,bhtsd->bhts', qc, kc, decay)
        out = (jnp.einsum('bhtd,bhde->bhte', qc * jnp.exp(cum), state)
               + jnp.einsum('bhts,bhse->bhte', scores, vc))
        new_state = (jnp.exp(last[:, :, 0, :])[..., None] * state
                     + jnp.einsum('bhsd,bhse->bhde', kc * jnp.exp(last - cum), vc))
        return new_state, out

    final, out = lax.scan(step, s0, (chunks(q), chunks(k), chunks(v), chunks(logf)))
    return out.transpose(1, 0, 3, 2, 4).reshape(b, n, h, dv), final

def hgrn_gates(f_logits, lb):
    z = f_logits.astype(F32)
    logf = jnp.logaddexp(jax.nn.log_sigmoid(z), jnp.log(lb) + jax.nn.log_sigmoid(-z))
    return (1.0 - lb) * jax.nn.sigmoid(-z), logf

def hgrn_out(o, g, onorm_g):
    y = rms_norm(o, onorm_g) * jax.nn.silu(split_heads(g, HGRN_HEADS, HGRN_VAL).astype(F32))
    return y.reshape(g.shape).astype(g.dtype)

def hgrn2_mixer(qx, ix, ffx, fbx, gx, qc, ic, ffc, fbc, gc, lb_fwd, lb_bwd, onorm_g, with_ctx):
    b = qx.shape[0]
    s0 = jnp.zeros((b, HGRN_HEADS, HGRN_KEY, HGRN_VAL), F32)
    o_lat, o_ctx = 0.0, 0.0
    for f_lat, f_ctx, lb, reverse in ((ffx, ffc, lb_fwd, False), (fbx, fbc, lb_bwd, True)):
        def orient(t):
            return jnp.flip(t, axis=1) if reverse else t
        k_c, logf_c = hgrn_gates(split_heads(orient(f_ctx), HGRN_HEADS, HGRN_KEY), lb)
        out_c, state = gla_chunk_scan(split_heads(orient(qc), HGRN_HEADS, HGRN_KEY), k_c,
                                      split_heads(orient(ic), HGRN_HEADS, HGRN_VAL), logf_c, s0)
        k_x, logf_x = hgrn_gates(split_heads(orient(f_lat), HGRN_HEADS, HGRN_KEY), lb)
        out_x, _ = gla_chunk_scan(split_heads(orient(qx), HGRN_HEADS, HGRN_KEY), k_x,
                                  split_heads(orient(ix), HGRN_HEADS, HGRN_VAL), logf_x, state)
        o_lat = o_lat + orient(out_x)
        if with_ctx:
            o_ctx = o_ctx + orient(out_c)
    y_lat = hgrn_out(o_lat, gx, onorm_g)
    y_ctx = hgrn_out(o_ctx, gc, onorm_g) if with_ctx else None
    return y_lat, y_ctx

def routed_experts(h, idx, w, w_gate, w_up, w_down):
    t, d = h.shape
    a = t * TOP_K
    flat_e = idx.reshape(a)
    order = jnp.argsort(flat_e)
    sorted_e = flat_e[order]
    counts = jnp.bincount(flat_e, length=N_EXPERTS)
    starts = jnp.cumsum(counts) - counts
    padded = (counts + MOE_BLOCK - 1) // MOE_BLOCK * MOE_BLOCK
    pad_ends = jnp.cumsum(padded)
    pad_starts = pad_ends - padded
    dest = pad_starts[sorted_e] + jnp.arange(a) - starts[sorted_e]
    n_blocks = -(-(a + N_EXPERTS * (MOE_BLOCK - 1)) // MOE_BLOCK)
    n_slots = n_blocks * MOE_BLOCK
    slot_src = jnp.full((n_slots,), a, jnp.int32).at[dest].set(order.astype(jnp.int32))
    valid = slot_src < a
    src = jnp.minimum(slot_src, a - 1)
    slot_tok = jnp.where(valid, src // TOP_K, 0)
    slot_w = jnp.where(valid, w.reshape(a)[src], 0.0).astype(h.dtype)
    block_e = jnp.minimum(jnp.searchsorted(pad_ends, jnp.arange(n_blocks) * MOE_BLOCK, side='right'), N_EXPERTS - 1)

    def run_block(args):
        tok, wt, e = args
        xb = h[tok]
        hid = jax.nn.silu(xb @ w_gate[e]) * (xb @ w_up[e])
        return (hid @ w_down[e]) * wt[:, None]

    y = lax.map(run_block, (slot_tok.reshape(n_blocks, MOE_BLOCK), slot_w.reshape(n_blocks, MOE_BLOCK), block_e))
    return jax.ops.segment_sum(y.reshape(n_slots, d), slot_tok, num_segments=t)

def moe_ffn(h, router_w, router_bias, w_gate, w_up, w_down, sh_gate, sh_up, sh_down):
    t = h.shape[0]
    scores = jax.nn.sigmoid(jnp.matmul(h, router_w, preferred_element_type=F32))
    sel = scores + router_bias.astype(F32)
    grouped = sel.reshape(t, N_EXPERT_GROUPS, N_EXPERTS // N_EXPERT_GROUPS)
    group_score = lax.top_k(grouped, 2)[0].sum(-1)
    _, top_groups = lax.top_k(group_score, TOPK_GROUPS)
    group_keep = (top_groups[..., None] == jnp.arange(N_EXPERT_GROUPS)).any(axis=1)
    expert_keep = jnp.repeat(group_keep, N_EXPERTS // N_EXPERT_GROUPS, axis=-1)
    _, idx = lax.top_k(jnp.where(expert_keep, sel, -jnp.inf), TOP_K)
    w = jnp.take_along_axis(scores, idx, axis=-1)
    w = w / jnp.sum(w, axis=-1, keepdims=True) * ROUTED_SCALE
    shared = (jax.nn.silu(h @ sh_gate) * (h @ sh_up)) @ sh_down
    return routed_experts(h, idx, w, w_gate, w_up, w_down) + shared

def hybrid_layer(x, cx, c, c_ctx, rope, w_mod, b_mod, norm1_g, norm2_g, w_in, w_out,
                 gqa_q_gain, gqa_k_gain, win_q_gain, win_k_gain, win_sink,
                 conv_dw_w, conv_dw_b, conv_ln_g, conv_ln_b, conv_pw_w, conv_pw_b,
                 lb_fwd, lb_bwd, hgrn_onorm_g, router_w, router_bias,
                 exp_w_gate, exp_w_up, exp_w_down, sh_w_gate, sh_w_up, sh_w_down, with_ctx):
    b, n, d = x.shape
    l = cx.shape[1]
    mx = (jax.nn.silu(c) @ w_mod + b_mod).reshape(b, 6, d).transpose(1, 0, 2)[:, :, None, :]
    mc = (jax.nn.silu(c_ctx) @ w_mod + b_mod).reshape(6, 1, 1, d)

    hx = modulate(rms_norm(x, norm1_g), mx[0], mx[1])
    hc = modulate(rms_norm(cx, norm1_g), mc[0], mc[1])
    (gq, gk, gv, wq, wk, wv, cv_val, cv_gate, rq, ri, rf_f, rf_b, rg) = split_cols(hx @ w_in)
    (gq_c, gk_c, gv_c, wq_c, wk_c, wv_c, cv_val_c, cv_gate_c,
     rq_c, ri_c, rf_f_c, rf_b_c, rg_c) = split_cols(hc @ w_in)

    q, k, v = attn_heads(gq, gk, gv, gqa_q_gain, gqa_k_gain, rope)
    gq_h, gk_h, gv_h = attn_heads(gq_c, gk_c, gv_c, gqa_q_gain, gqa_k_gain)
    y_glob = global_attention(q, k, v, gk_h, gv_h)

    y_conv = conformer_conv(cv_val, cv_gate, conv_dw_w, conv_dw_b, conv_ln_g, conv_ln_b, conv_pw_w, conv_pw_b)

    q, k, v = attn_heads(wq, wk, wv, win_q_gain, win_k_gain, rope)
    wq_h, wk_h, wv_h = attn_heads(wq_c, wk_c, wv_c, win_q_gain, win_k_gain)
    y_win = window_attention(q, k, v, wk_h, wv_h, win_sink)

    y_rec, yc_rec = hgrn2_mixer(rq, ri, rf_f, rf_b, rg, rq_c, ri_c, rf_f_c, rf_b_c, rg_c,
                                lb_fwd, lb_bwd, hgrn_onorm_g, with_ctx)

    x = x + mx[2] * (jnp.concatenate([y_glob, y_conv, y_win, y_rec], axis=-1) @ w_out)
    tokens = modulate(rms_norm(x, norm2_g), mx[3], mx[4]).reshape(b * n, d)
    if with_ctx:
        yc_glob = ctx_attention(gq_h, gk_h, gv_h)
        yc_conv = conformer_conv(cv_val_c, cv_gate_c, conv_dw_w, conv_dw_b, conv_ln_g, conv_ln_b, conv_pw_w, conv_pw_b)
        yc_win = ctx_attention(wq_h, wk_h, wv_h, win_sink)
        cx = cx + mc[2] * (jnp.concatenate([yc_glob, yc_conv, yc_win, yc_rec], axis=-1) @ w_out)
        hc2 = modulate(rms_norm(cx, norm2_g), mc[3], mc[4]).reshape(b * l, d)
        tokens = jnp.concatenate([tokens, hc2], axis=0)

    f = moe_ffn(tokens, router_w, router_bias, exp_w_gate, exp_w_up, exp_w_down, sh_w_gate, sh_w_up, sh_w_down)
    x = x + mx[5] * f[:b * n].reshape(b, n, d)
    if with_ctx:
        cx = cx + mc[5] * f[b * n:].reshape(b, l, d)
    return x, cx

def setup_inputs(seed: int = 0) -> dict:
    key = jax.random.key(seed)
    ks = jax.random.split(key, 31)
    d = D_MODEL

    def nrm(k, shape, s):
        return jax.random.normal(k, shape, F32) * s

    return {
        'x': nrm(ks[0], (BATCH, SEQ, d), 1.0),
        'c': nrm(ks[1], (BATCH, d), 1.0),
        'ctx': nrm(ks[2], (BATCH, CTX_LEN, d), 1.0),
        'c_ctx': nrm(ks[3], (d,), 1.0),
        'w_mod': nrm(ks[4], (DEPTH, d, 6 * d), 0.5 * d ** -0.5),
        'b_mod': nrm(ks[5], (DEPTH, 6 * d), 0.01),
        'norm1_g': 1.0 + nrm(ks[6], (DEPTH, d), 0.1),
        'norm2_g': 1.0 + nrm(ks[7], (DEPTH, d), 0.1),
        'w_in': nrm(ks[8], (DEPTH, d, D_IN), d ** -0.5),
        'w_out': nrm(ks[9], (DEPTH, N_MIXERS * GROUP_W, d), (N_MIXERS * GROUP_W) ** -0.5),
        'gqa_q_gain': 1.0 + nrm(ks[10], (DEPTH, HEAD_DIM), 0.1),
        'gqa_k_gain': 1.0 + nrm(ks[11], (DEPTH, HEAD_DIM), 0.1),
        'win_q_gain': 1.0 + nrm(ks[12], (DEPTH, HEAD_DIM), 0.1),
        'win_k_gain': 1.0 + nrm(ks[13], (DEPTH, HEAD_DIM), 0.1),
        'win_sink': nrm(ks[14], (DEPTH, N_Q_HEADS), 1.0),
        'conv_dw_w': nrm(ks[15], (DEPTH, CONV_WIDTH, GROUP_W), CONV_WIDTH ** -0.5),
        'conv_dw_b': nrm(ks[16], (DEPTH, GROUP_W), 0.01),
        'conv_ln_g': 1.0 + nrm(ks[17], (DEPTH, GROUP_W), 0.1),
        'conv_ln_b': nrm(ks[18], (DEPTH, GROUP_W), 0.01),
        'conv_pw_w': nrm(ks[19], (DEPTH, GROUP_W, GROUP_W), GROUP_W ** -0.5),
        'conv_pw_b': nrm(ks[20], (DEPTH, GROUP_W), 0.01),
        'hgrn_lb_logits': nrm(ks[21], (2, DEPTH, HGRN_HEADS * HGRN_KEY), 1.0),
        'hgrn_onorm_g': 1.0 + nrm(ks[22], (DEPTH, HGRN_VAL), 0.1),
        'router_w': nrm(ks[23], (DEPTH, d, N_EXPERTS), d ** -0.5),
        'router_bias': nrm(ks[24], (DEPTH, N_EXPERTS), 0.01),
        'exp_w_gate': nrm(ks[25], (DEPTH, N_EXPERTS, d, EXPERT_HIDDEN), d ** -0.5),
        'exp_w_up': nrm(ks[26], (DEPTH, N_EXPERTS, d, EXPERT_HIDDEN), d ** -0.5),
        'exp_w_down': nrm(ks[27], (DEPTH, N_EXPERTS, EXPERT_HIDDEN, d), EXPERT_HIDDEN ** -0.5),
        'sh_w_gate': nrm(ks[28], (DEPTH, d, SHARED_HIDDEN), d ** -0.5),
        'sh_w_up': nrm(ks[29], (DEPTH, d, SHARED_HIDDEN), d ** -0.5),
        'sh_w_down': nrm(ks[30], (DEPTH, SHARED_HIDDEN, d), SHARED_HIDDEN ** -0.5),
    }

def reference(x, c, ctx, c_ctx, w_mod, b_mod, norm1_g, norm2_g, w_in, w_out,
              gqa_q_gain, gqa_k_gain, win_q_gain, win_k_gain, win_sink,
              conv_dw_w, conv_dw_b, conv_ln_g, conv_ln_b, conv_pw_w, conv_pw_b,
              hgrn_lb_logits, hgrn_onorm_g, router_w, router_bias,
              exp_w_gate, exp_w_up, exp_w_down, sh_w_gate, sh_w_up, sh_w_down):
    rope = axial_rope(x.shape[1])
    lb = jnp.cumsum(jax.nn.softmax(hgrn_lb_logits.astype(F32), axis=1), axis=1)
    lb = (lb - lb[:, :1]).reshape(2, DEPTH, HGRN_HEADS, HGRN_KEY)
    cx = ctx
    for layer in range(DEPTH):
        x, cx = hybrid_layer(
            x, cx, c, c_ctx, rope, w_mod[layer], b_mod[layer], norm1_g[layer], norm2_g[layer],
            w_in[layer], w_out[layer], gqa_q_gain[layer], gqa_k_gain[layer],
            win_q_gain[layer], win_k_gain[layer], win_sink[layer],
            conv_dw_w[layer], conv_dw_b[layer], conv_ln_g[layer], conv_ln_b[layer],
            conv_pw_w[layer], conv_pw_b[layer], lb[0, layer], lb[1, layer], hgrn_onorm_g[layer],
            router_w[layer], router_bias[layer], exp_w_gate[layer], exp_w_up[layer], exp_w_down[layer],
            sh_w_gate[layer], sh_w_up[layer], sh_w_down[layer], layer < DEPTH - 1)
    return x


_drawn_inputs = setup_inputs


def setup_inputs(seed=0):
    import zlib

    import numpy as np

    out = dict(_drawn_inputs(seed))
    spreads = {}
    factors = {'gqa_q_gain': 3.933,
     'gqa_k_gain': 4.02,
     'win_q_gain': 4.404,
     'win_k_gain': 3.407,
     'win_sink': 64.0,
     'conv_dw_b': 3.75,
     'conv_ln_b': 6.407,
     'conv_pw_b': 3.665}
    for name, (base, spread) in spreads.items():
        noise = np.random.default_rng([zlib.crc32(name.encode()), seed]).standard_normal(out[name].shape)
        drawn = base * np.exp(spread * noise) if base else spread * noise
        out[name] = jnp.asarray(drawn.astype(out[name].dtype))
    for name, factor in factors.items():
        out[name] = (out[name] * factor).astype(out[name].dtype)
    return out
```

```python
import concourse.bass as bass
from concourse import mybir
from contextlib import ExitStack, contextmanager
import numpy as np

F32 = mybir.dt.float32
I32 = mybir.dt.int32
U32 = mybir.dt.uint32
ALU = mybir.AluOpType
ACT = mybir.ActivationFunctionType
AX = mybir.AxisListType

P = 128
D = 1024
KT = D // P
SEQ = 512
CTX = 256
TOK = SEQ + CTX
NT = TOK // P
NTX = SEQ // P
NTC = CTX // P
DEPTH = 2
GRID_W = 64
HEAD = 64
N_Q = 4
N_KV = 2
GROUP = 256
D_IN = 2816
SCALE = HEAD ** -0.5
CONV_W = 31
PAD = CONV_W // 2
N_EXP = 64
TOP_K = 8
N_GRP = 8
PER_GRP = N_EXP // N_GRP
HID = 256
ROUTED_SCALE = 2.5
EPS = 1e-6
LEVELS = 7
NEG = -1e30
BANK = 512

C_ID = 0
C_SEL = C_ID + P
C_PREV = C_SEL + 2 * P
C_NEXT = C_PREV + P
C_LEV = C_NEXT + P
C_LEVR = C_LEV + LEVELS * P
C_TRI = C_LEVR + LEVELS * P
C_IOTA = C_TRI + P
C_COL = C_IOTA + P
C_LOW = C_COL + 16
C_COS = C_LOW + 64
C_SIN = C_COS + NTX * HEAD
C_ALL = C_SIN + NTX * HEAD


def shape_constants():
    c = np.zeros((P, C_ALL), np.float32)
    r = np.arange(P)
    c[:, C_ID:C_ID + P] = np.eye(P)
    for j in range(4):
        for s in range(2):
            c[32 * j + s, C_SEL + s * P:C_SEL + (s + 1) * P] = 1.0
    c[:, C_PREV:C_PREV + P] = np.where(r[None, :] >= r[:, None], 0.0, NEG)
    c[:, C_NEXT:C_NEXT + P] = np.where(r[None, :] <= r[:, None], 0.0, NEG)
    for lev in range(LEVELS):
        n = 1 << lev
        same = (r[:, None] // (2 * n)) == (r[None, :] // (2 * n))
        fwd = same & (r[:, None] % (2 * n) < n) & (r[None, :] % (2 * n) >= n)
        c[:, C_LEV + lev * P:C_LEV + (lev + 1) * P] = fwd
        c[:, C_LEVR + lev * P:C_LEVR + (lev + 1) * P] = fwd.T
    c[:, C_TRI:C_TRI + P] = r[:, None] < r[None, :]
    c[:, C_IOTA:C_IOTA + P] = r[None, :]
    c[:, C_COL] = 1.0
    c[:, C_COL + 1] = r
    c[:, C_COL + 2] = TOK * TOP_K + r
    c[:, C_COL + 10:C_COL + 10 + DEPTH - 1] = 1.0
    k8 = np.arange(N_GRP)
    c[:, C_LOW:C_LOW + 64] = (k8[None, :] < k8[:, None]).reshape(1, 64)
    for i in range(NT):
        c[:, C_COL + 4 + i] = i * P + r
    freqs = HEAD // 4
    inv = np.power(10000.0, -np.arange(freqs, dtype=np.float32) / freqs).astype(np.float32)
    for i in range(NTX):
        t = i * P + r
        for ax, pos in enumerate((t // GRID_W, t % GRID_W)):
            ang = pos.astype(np.float32)[:, None] * inv[None, :]
            at = i * HEAD + ax * 2 * freqs
            c[:, C_COS + at:C_COS + at + freqs] = np.cos(ang)
            c[:, C_COS + at + freqs:C_COS + at + 2 * freqs] = np.cos(ang)
            c[:, C_SIN + at:C_SIN + at + freqs] = -np.sin(ang)
            c[:, C_SIN + at + freqs:C_SIN + at + 2 * freqs] = np.sin(ang)
    return c


@contextmanager
def stage(nc, name, sem_names, kept=()):
    sems = [nc.alloc_semaphore(name=f"{name}_{s}") for s in sem_names.split()]
    with nc.Block(name) as block:
        yield (block, *sems)
    for s in sems:
        nc.all_engine_barrier(sems_to_clear=s)
        nc.release_semaphore(s)
    for s in kept:
        nc.all_engine_barrier(sems_to_clear=s)


class Own:

    def __init__(self, eng, sem):
        self.eng, self.sem, self.n = eng, sem, 0

    def __call__(self, ins):
        ins.then_inc(self.sem, 1)
        self.n += 1
        return ins

    def settle(self):
        self.eng.wait_ge(self.sem, self.n)

    def then(self, ins):
        self(ins)
        self.settle()


def build(nc, A, out):
    with ExitStack() as es:
        def sb(name, shape, dt=F32, stack=es):
            return stack.enter_context(nc.sbuf_tensor(name, shape, dt))

        g = {}
        g["x"] = sb("x_res", [P, NT, D])
        g["cst"] = sb("cst", [P, C_ALL])
        g["cT"] = sb("cT", [P, KT, 2])
        g["lb"] = sb("lb", [P, DEPTH, 3, 4])
        g["mods"] = sb("mods", [P, 3, BANK])
        h_dram = nc.dram_tensor("h_rows", (TOK, D), F32).ap()
        y_dram = nc.dram_tensor("expert_rows", (TOK * TOP_K + P, D), F32).ap()
        g["rows_sems"] = [nc.alloc_semaphore(name=n) for n in ("gathered0", "gathered1", "scattered0", "scattered1")]
        prologue(nc, A, g)
        with nc.Fori(0, DEPTH) as layer:
            with ExitStack() as mix:
                g["pt"] = sb("p_tok", [P, NT, 1536], stack=mix)
                g["pf"] = sb("p_feat", [P, 10, TOK], stack=mix)
                modulation(nc, A, g, layer)
                with nc.sbuf_tensor("hT", [P, KT, TOK], F32) as hT:
                    norm_rows(nc, A, g, layer, 0, "norm1_g", hT, None)
                    projections(nc, A, g, layer, hT)
                g["yT"] = sb("yT", [P, KT, TOK], stack=mix)
                attention(nc, A, g, layer, 0)
                attention(nc, A, g, layer, 1)
                convolution(nc, A, g, layer)
                recurrence(nc, A, g, layer)
                out_projection(nc, A, g, layer)
            moe(nc, A, g, layer, h_dram, y_dram)
        with stage(nc, "store", "stored") as (block, stored):
            @block.sync
            def _(sp):
                sp.dma_start(out[0].rearrange("(t p) d -> p t d", p=P), g["x"][:, 0:NTX, :]).then_inc(stored, 16)
                sp.wait_ge(stored, 16)


def prologue(nc, A, g):
    x, cst, cT, lb = g["x"], g["cst"], g["cT"], g["lb"]
    with ExitStack() as es:
        craw = es.enter_context(nc.sbuf_tensor("craw", [P, KT, 2], F32))
        csig = es.enter_context(nc.sbuf_tensor("csig", [P, KT, 2], F32))
        lg = es.enter_context(nc.sbuf_tensor("lg", [P, DEPTH, 4], F32))
        mx = es.enter_context(nc.sbuf_tensor("lg_max", [P, 4], F32))
        den = es.enter_context(nc.sbuf_tensor("lg_den", [P, 4], F32))
        with stage(nc, "prologue", "loaded streams acted own ready") as (block, loaded, streams, acted, own, ready):
            @block.sync
            def _(sp):
                sp.dma_start(craw[:, :, 0], A["c"][0].rearrange("(k p) -> p k", p=P),
                             allow_slow_non_contiguous=True).then_inc(loaded, 16)
                sp.dma_start(craw[:, :, 1], A["c_ctx"].rearrange("(k p) -> p k", p=P),
                             allow_slow_non_contiguous=True).then_inc(loaded, 16)
                for l in range(DEPTH):
                    for d in range(2):
                        sp.dma_start(lg[:, l, 2 * d:2 * d + 2],
                                     A["hgrn_lb_logits"][d, l].rearrange("(g p) -> p g", p=P),
                                     allow_slow_non_contiguous=True).then_inc(loaded, 16)
                sp.dma_start(cst[:, :], A["consts"]).then_inc(streams, 16)
                sp.dma_start(x[:, 0:NTX, :], A["x"][0].rearrange("(t p) d -> p t d", p=P)).then_inc(streams, 16)
                sp.dma_start(x[:, NTX:NT, :], A["ctx"][0].rearrange("(t p) d -> p t d", p=P)).then_inc(streams, 16)
                sp.wait_ge(streams, 48)

            @block.scalar
            def _(act):
                act.wait_ge(loaded, 96)
                nc.scalar.activation(csig[:, :, :], craw[:, :, :], ACT.Sigmoid).then_inc(acted, 1)
                act.wait_ge(ready, 1)
                nc.scalar.activation(lg[:, :, :], lg[:, :, :], ACT.Exp).then_inc(acted, 1)
                act.wait_ge(ready, 2)
                nc.scalar.activation(lb[:, :, 1, :], lb[:, :, 1, :], ACT.Ln).then_inc(acted, 1)

            @block.vector
            def _(dve):
                o = Own(dve, own)
                dve.wait_ge(loaded, 96)
                o.then(nc.vector.tensor_tensor(mx[:, :], lg[:, 0, :], lg[:, 1, :], ALU.max))
                o(nc.vector.tensor_tensor(lg[:, 0, :], lg[:, 0, :], mx[:, :], ALU.subtract))
                nc.vector.tensor_tensor(lg[:, 1, :], lg[:, 1, :], mx[:, :], ALU.subtract).then_inc(ready, 1)
                dve.wait_ge(acted, 2)
                o(nc.vector.tensor_tensor(cT[:, :, :], craw[:, :, :], csig[:, :, :], ALU.mult))
                o.then(nc.vector.tensor_tensor(den[:, :], lg[:, 0, :], lg[:, 1, :], ALU.add))
                o.then(nc.vector.reciprocal(den[:, :], den[:, :]))
                o(nc.vector.tensor_tensor(lg[:, 0, :], lg[:, 0, :], den[:, :], ALU.mult))
                o.then(nc.vector.tensor_tensor(lg[:, 1, :], lg[:, 1, :], den[:, :], ALU.mult))
                o(nc.vector.memset(lb[:, 0, 0, :], 0.0))
                o.then(nc.vector.tensor_tensor(lb[:, 1, 0, :], lg[:, 0, :], lg[:, 1, :], ALU.add))
                o.then(nc.vector.tensor_tensor(lb[:, 1, 0, :], lb[:, 1, 0, :], lg[:, 0, :], ALU.subtract))
                o(nc.vector.tensor_scalar(lb[:, :, 2, :], lb[:, :, 0, :], -1.0, 1.0, ALU.mult, ALU.add))
                nc.vector.tensor_scalar(lb[:, :, 1, :], lb[:, :, 0, :], 1e-18, None, ALU.max).then_inc(ready, 1)
                o.then(nc.vector.tensor_scalar(lg[:, :, :], lb[:, :, 0, :], 0.0, NEG, ALU.is_equal, ALU.mult))
                dve.wait_ge(acted, 3)
                nc.vector.tensor_tensor(lb[:, :, 1, :], lb[:, :, 1, :], lg[:, :, :], ALU.add).then_inc(ready, 1)


def modulation(nc, A, g, layer):
    cT, cst, mods = g["cT"], g["cst"], g["mods"]
    NBUF, CH = 3, 12
    with ExitStack() as es:
        w = es.enter_context(nc.sbuf_tensor("w_mod_t", [P, NBUF, 6 * D], F32))
        b = es.enter_context(nc.sbuf_tensor("b_mod_t", [1, 6 * D], F32))
        one = es.enter_context(nc.sbuf_tensor("one_row", [1, 2], F32))
        ps = es.enter_context(nc.psum_tensor("mod_ps", [P, 3, BANK], F32))
        with stage(nc, "mod", "w0 w1 w2 bias w_used ones summed kept") as (block, w0, w1, w2, bias, w_used, ones, summed, kept):
            w_in = (w0, w1, w2)

            @block.sync
            def _(sp):
                sp.dma_start(b[:, :], A["b_mod"][bass.ds(layer, 1), :]).then_inc(bias, 16)
                for k in range(KT):
                    if k >= NBUF:
                        sp.wait_ge(w_used, k - NBUF + 1)
                    sp.dma_start(w[:, k % NBUF, :],
                                 A["w_mod"][bass.ds(layer, 1), k * P:(k + 1) * P, :].rearrange("a p n -> (a p) n")
                                 ).then_inc(w_in[k % NBUF], 16)

            @block.vector
            def _(dve):
                nc.vector.memset(one[:, :], 1.0).then_inc(ones, 1)
                dve.wait_ge(summed, 1)
                for j in range(4):
                    nc.vector.tensor_copy(mods[32 * j:32 * j + 2, :, :], ps[32 * j:32 * j + 2, :, :]).then_inc(kept, 1)

            @block.tensor
            def _(pe):
                for k in range(KT):
                    pe.wait_ge(w_in[k % NBUF], 16 * (k // NBUF + 1))
                    for c in range(CH):
                        last = nc.tensor.matmul(ps[32 * (c % 4):32 * (c % 4) + 2, c // 4, :], cT[:, k, :],
                                                w[:, k % NBUF, c * BANK:(c + 1) * BANK], start=(k == 0), stop=False)
                    last.then_inc(w_used, 1)
                pe.wait_ge(bias, 16)
                pe.wait_ge(ones, 1)
                for c in range(CH):
                    last = nc.tensor.matmul(ps[32 * (c % 4):32 * (c % 4) + 2, c // 4, :], one[0:1, :],
                                            b[0:1, c * BANK:(c + 1) * BANK], start=False, stop=True)
                last.then_inc(summed, 1)


def broadcast_row(nc, g, ps, kind, stream):
    cst, mods = g["cst"], g["mods"]
    for h in range(2):
        c = 2 * kind + h
        j = 32 * (c % 4)
        last = nc.tensor.matmul(ps[:, h * BANK:(h + 1) * BANK], cst[j:j + 2, C_SEL + stream * P:C_SEL + (stream + 1) * P],
                                mods[j:j + 2, c // 4, :], start=True, stop=True)
    return last


def norm_rows(nc, A, g, layer, kind, gain, hT, h_dram):
    x, cst = g["x"], g["cst"]
    with ExitStack() as es:
        gr = es.enter_context(nc.sbuf_tensor(f"gain_row{kind}", [P, D], F32))
        mul = es.enter_context(nc.sbuf_tensor(f"mul_row{kind}", [P, 2, D], F32))
        add = es.enter_context(nc.sbuf_tensor(f"add_row{kind}", [P, 2, D], F32))
        h = es.enter_context(nc.sbuf_tensor(f"h_tok{kind}", [P, 2, D], F32))
        sq = es.enter_context(nc.sbuf_tensor(f"h_sq{kind}", [P, D], F32))
        ss = es.enter_context(nc.sbuf_tensor(f"h_ss{kind}", [P, NT], F32))
        rs = es.enter_context(nc.sbuf_tensor(f"h_rstd{kind}", [P, NT], F32))
        pr = es.enter_context(nc.psum_tensor(f"row_ps{kind}", [P, 2, 2 * BANK], F32))
        pt = es.enter_context(nc.psum_tensor(f"hT_ps{kind}", [P, 2, 2 * BANK], F32))
        names = "gain_in spread rows own squared varied rooted h_ready turned kept stored0 stored1"
        with stage(nc, f"norm{kind}", names) as (block, gain_in, spread, rows, own, squared, varied, rooted, h_ready,
                                                 turned, kept, stored0, stored1):
            stored = (stored0, stored1)

            @block.sync
            def _(sp):
                sp.dma_start(gr[:, :], A[gain][bass.ds(layer, 1), :].broadcast_to([P, D])).then_inc(gain_in, 16)
                if h_dram is not None:
                    for i in range(NT):
                        sp.wait_ge(h_ready, i + 1)
                        sp.dma_start(h_dram[i * P:(i + 1) * P, :], h[:, i % 2, :]).then_inc(stored[i % 2], 16)
                    for a in range(2):
                        sp.wait_ge(stored[a], 16 * NT // 2)

            @block.tensor
            def _(pe):
                for n, (kd, s) in enumerate(((kind + 1, 0), (kind + 1, 1), (kind, 0), (kind, 1))):
                    if n >= 2:
                        pe.wait_ge(rows, n - 1)
                    broadcast_row(nc, g, pr[:, n % 2, :], kd, s).then_inc(spread, 1)
                for i in range(NT):
                    pe.wait_ge(h_ready, i + 1)
                    if i >= 2:
                        pe.wait_ge(kept, i - 1)
                    for k in range(KT):
                        last = nc.tensor.transpose(pt[:, i % 2, k * P:(k + 1) * P], h[:, i % 2, k * P:(k + 1) * P],
                                                   cst[:, C_ID:C_ID + P])
                    last.then_inc(turned, 1)

            @block.scalar
            def _(act):
                for i in range(NT):
                    if i:
                        act.wait_ge(squared, i)
                    nc.scalar.activation(sq[:, :], x[:, i, :], ACT.Square, accum_out=ss[:, i:i + 1]).then_inc(squared, 1)
                act.wait_ge(varied, 1)
                nc.scalar.activation(rs[:, :], rs[:, :], ACT.Sqrt).then_inc(rooted, 1)
                for i in range(NT):
                    act.wait_ge(turned, i + 1)
                    nc.scalar.activation(hT[:, :, i * P:(i + 1) * P],
                                         pt[:, i % 2, :].rearrange("p (k t) -> p k t", t=P), ACT.Copy).then_inc(kept, 1)

            @block.vector
            def _(dve):
                o = Own(dve, own)
                dve.wait_ge(gain_in, 16)
                for s in range(2):
                    dve.wait_ge(spread, s + 1)
                    nc.vector.scalar_tensor_tensor(mul[:, s, :], pr[:, s, :], 1.0, gr[:, :], ALU.add, ALU.mult).then_inc(rows, 1)
                for s in range(2):
                    dve.wait_ge(spread, s + 3)
                    nc.vector.tensor_copy(add[:, s, :], pr[:, s, :]).then_inc(rows, 1)
                dve.wait_ge(squared, NT)
                nc.vector.tensor_scalar(rs[:, :], ss[:, :], 1.0 / D, EPS, ALU.mult, ALU.add).then_inc(varied, 1)
                dve.wait_ge(rooted, 1)
                dve.wait_ge(rows, 4)
                o.then(nc.vector.reciprocal(rs[:, :], rs[:, :]))
                for i in range(NT):
                    s = 0 if i < NTX else 1
                    if i >= 2:
                        dve.wait_ge(turned, i - 1)
                        if h_dram is not None:
                            dve.wait_ge(stored[i % 2], 16 * (i // 2))
                    o.then(nc.vector.scalar_tensor_tensor(h[:, i % 2, :], x[:, i, :], rs[:, i:i + 1], mul[:, s, :], ALU.mult, ALU.mult))
                    nc.vector.tensor_tensor(h[:, i % 2, :], h[:, i % 2, :], add[:, s, :], ALU.add).then_inc(h_ready, 1)


def projections(nc, A, g, layer, hT):
    pt, pf = g["pt"], g["pf"]
    CHUNKS = [(0, 512, [("t", 0, 512, 0)]),
              (512, 512, [("t", 0, 512, 512)]),
              (1024, 512, [("f", 128 * j, j) for j in range(4)]),
              (1536, 512, [("f", 0, 4), ("f", 128, 5), ("t", 256, 256, 1024)]),
              (2048, 512, [("f", 128 * j, 6 + j) for j in range(4)]),
              (2560, 256, [("t", 0, 256, 1280)])]
    jobs = []
    for c, (c0, cw, js) in enumerate(CHUNKS):
        for job in js:
            if job[0] == "t":
                for i in range(NT):
                    jobs.append((c, "t", job[1], job[2], pt[:, i, job[3]:job[3] + job[2]], i * P, P))
            else:
                for t0, tw in ((0, SEQ), (SEQ, CTX)):
                    jobs.append((c, "f", job[1], tw, pf[:, job[2], t0:t0 + tw], t0, tw))
    with ExitStack() as es:
        w = es.enter_context(nc.sbuf_tensor("w_in_t", [P, 2, KT, BANK], F32))
        ps = es.enter_context(nc.psum_tensor("p_ps", [P, 8, BANK], F32))
        with stage(nc, "proj", "w0 w1 w_used done kept_a kept_v") as (block, w0, w1, w_used, done, kept_a, kept_v):
            w_in = (w0, w1)

            @block.sync
            def _(sp):
                for c, (c0, cw, _) in enumerate(CHUNKS):
                    if c >= 2:
                        sp.wait_ge(w_used, c - 1)
                    sp.dma_start(w[:, c % 2, :, 0:cw],
                                 A["w_in"][bass.ds(layer, 1), :, c0:c0 + cw].rearrange("a (k p) n -> p (a k) n", p=P)
                                 ).then_inc(w_in[c % 2], 16)

            @block.tensor
            def _(pe):
                for n, (c, kind, col, width, dst, t0, tw) in enumerate(jobs):
                    if n == 0 or jobs[n - 1][0] != c:
                        pe.wait_ge(w_in[c % 2], 16 * (c // 2 + 1))
                    if n >= 8:
                        pe.wait_ge((kept_a, kept_v)[n % 2], (n - 8) // 2 + 1)
                    for k in range(KT):
                        if kind == "t":
                            last = nc.tensor.matmul(ps[:, n % 8, 0:width], hT[:, k, t0:t0 + P], w[:, c % 2, k, col:col + width],
                                                    start=(k == 0), stop=(k == KT - 1))
                        else:
                            last = nc.tensor.matmul(ps[:, n % 8, 0:tw], w[:, c % 2, k, col:col + P], hT[:, k, t0:t0 + tw],
                                                    start=(k == 0), stop=(k == KT - 1))
                    last.then_inc(done, 1)
                    if n + 1 == len(jobs) or jobs[n + 1][0] != c:
                        pe.wait_ge(done, n + 1)
                        pe.sem_inc(w_used, 1)

            @block.scalar
            def _(act):
                for n, job in enumerate(jobs):
                    if n % 2 == 0:
                        act.wait_ge(done, n + 1)
                        nc.scalar.activation(job[4], ps[:, n % 8, 0:job[3]], ACT.Copy).then_inc(kept_a, 1)

            @block.vector
            def _(dve):
                for n, job in enumerate(jobs):
                    if n % 2 == 1:
                        dve.wait_ge(done, n + 1)
                        nc.vector.tensor_copy(job[4], ps[:, n % 8, 0:job[3]]).then_inc(kept_v, 1)


def attention(nc, A, g, layer, win):
    pt, cst, yT = g["pt"], g["cst"], g["yT"]
    name = ("glob", "win")[win]
    qg, kg = (("gqa_q_gain", "gqa_k_gain"), ("win_q_gain", "win_k_gain"))[win]
    c0 = 512 * win
    QK = (N_Q + N_KV) * HEAD
    NH = N_Q + N_KV
    qk = pt[:, :, c0:c0 + QK]

    def vals(j, kv):
        return pt[:, j, c0 + QK + kv * HEAD:c0 + QK + (kv + 1) * HEAD]

    units = []
    for i in range(NT):
        if i >= NTX:
            keys = list(range(NTX, NT))
        elif win:
            keys = list(range(max(0, i - 1), min(NTX, i + 2))) + list(range(NTX, NT))
        else:
            keys = list(range(NT))
        for h in (0, 2, 1, 3):
            units.append((i, h, keys))
    NU = len(units)

    def runs(keys):
        out = []
        for n, j in enumerate(keys):
            if out and out[-1][1] + out[-1][2] == j and (n * P) % BANK:
                out[-1][2] += 1
            else:
                out.append([n * P, j, 1])
        return out

    with ExitStack() as es:
        sb = lambda n, s: es.enter_context(nc.sbuf_tensor(f"{name}_{n}", s, F32))
        tmp = sb("tmp", [P, NT, QK])
        swp = sb("swp", [P, NTX, QK])
        gain = sb("gain", [P, NH, HEAD])
        rs = sb("rs", [P, NT * NH])
        qT = sb("qT", [P, 2, TOK])
        kT = sb("kT", [P, TOK])
        prob = sb("prob", [P, 2, NT, P])
        probT = sb("probT", [P, 2, NT, P])
        o_tok = sb("o", [P, 2, GROUP])
        top = sb("top", [P, NU])
        neg = sb("neg", [P, NU])
        den = sb("den", [P, NU])
        snk = sb("snk", [P, N_Q])
        esnk = sb("esnk", [P, NU])
        ps_s = es.enter_context(nc.psum_tensor(f"{name}_ps_s", [P, 2, 2 * BANK], F32))
        ps_t = es.enter_context(nc.psum_tensor(f"{name}_ps_t", [P, 2 * BANK], F32))
        ps_o = es.enter_context(nc.psum_tensor(f"{name}_ps_o", [P, 2, BANK], F32))
        names = ("gains varied rooted normed turned kept own own_a scored topped exped spread spread_kept "
                 "mixed scaled back back_kept")
        with stage(nc, name, names) as (block, gains, varied, rooted, normed, turned, kept, own, own_a, scored, topped,
                                        exped, spread, spread_kept, mixed, scaled, back, back_kept):
            @block.sync
            def _(sp):
                for h in range(NH):
                    sp.dma_start(gain[:, h, :], A[qg if h < N_Q else kg][bass.ds(layer, 1), :].broadcast_to([P, HEAD])
                                 ).then_inc(gains, 16)
                if win:
                    sp.dma_start(snk[:, :], A["win_sink"][bass.ds(layer, 1), :].broadcast_to([P, N_Q])).then_inc(gains, 16)

            @block.vector
            def _(dve):
                o = Own(dve, own)
                heads = lambda ap: ap.rearrange("p t (h d) -> p t h d", d=HEAD)
                o.then(nc.vector.tensor_tensor(tmp[:, :, :], qk, qk, ALU.mult))
                o.then(nc.vector.tensor_reduce(rs[:, :], tmp[:, :, :].rearrange("p t (h d) -> p (t h) d", d=HEAD), AX.X, ALU.add))
                nc.vector.tensor_scalar(rs[:, :], rs[:, :], 1.0 / HEAD, EPS, ALU.mult, ALU.add).then_inc(varied, 1)
                dve.wait_ge(rooted, 1)
                o.then(nc.vector.reciprocal(rs[:, :], rs[:, :]))
                by_head = rs[:, :].rearrange("p (t h o) -> p t h o", h=NH, o=1)
                for b in range(3):
                    pick = slice(b, N_Q, 2) if b < 2 else slice(N_Q, NH)
                    o(nc.vector.tensor_tensor(heads(tmp[:, :, :])[:, :, 2 * b:2 * b + 2, :], heads(qk)[:, :, pick, :],
                                              by_head[:, :, pick, :].broadcast_to([P, NT, 2, HEAD]), ALU.mult))
                o.settle()
                dve.wait_ge(gains, 16 * (NH + win))
                o.then(nc.vector.tensor_tensor(heads(tmp[:, :, :]), heads(tmp[:, :, :]),
                                               gain[:, :, :].rearrange("p (o h) d -> p o h d", o=1).broadcast_to([P, NT, NH, HEAD]), ALU.mult))
                half = HEAD // 4
                for i in range(NTX):
                    part = lambda ap, a: ap.rearrange("p (h x a f) -> p h x a f", x=2, a=2, f=half)[:, :, :, a, :]
                    sin = cst[:, C_SIN + i * HEAD:C_SIN + (i + 1) * HEAD].rearrange("p (o x a f) -> p o x a f", o=1, x=2, a=2)
                    for a in range(2):
                        o(nc.vector.tensor_tensor(part(swp[:, i, :], a), part(tmp[:, i, :], 1 - a),
                                                  sin[:, :, :, a, :].broadcast_to([P, NH, 2, half]), ALU.mult))
                o.settle()
                cos = cst[:, C_COS:C_COS + NTX * HEAD].rearrange("p (t o d) -> p t o d", t=NTX, o=1).broadcast_to([P, NTX, NH, HEAD])
                o.then(nc.vector.tensor_tensor(heads(tmp[:, 0:NTX, :]), heads(tmp[:, 0:NTX, :]), cos, ALU.mult))
                nc.vector.tensor_tensor(tmp[:, 0:NTX, :], tmp[:, 0:NTX, :], swp[:, :, :], ALU.add).then_inc(normed, 1)
                for n in range(NU + 2):
                    if n < NU:
                        i, h, keys = units[n]
                        w = len(keys) * P
                        dve.wait_ge(scored, n + 1)
                        o.then(nc.vector.tensor_reduce(top[:, n:n + 1], ps_s[:, n % 2, 0:w], AX.X, ALU.max))
                        if win:
                            o.then(nc.vector.scalar_tensor_tensor(top[:, n:n + 1], top[:, n:n + 1], SCALE, snk[:, h:h + 1], ALU.mult, ALU.max))
                            nc.vector.tensor_scalar(neg[:, n:n + 1], top[:, n:n + 1], -1.0, None, ALU.mult).then_inc(topped, 1)
                        else:
                            nc.vector.tensor_scalar(neg[:, n:n + 1], top[:, n:n + 1], -SCALE, None, ALU.mult).then_inc(topped, 1)
                    if n >= 2:
                        m = n - 2
                        i, h, keys = units[m]
                        if win:
                            dve.wait_ge(exped, 2 * (m + 1))
                            o.then(nc.vector.tensor_tensor(den[:, m:m + 1], den[:, m:m + 1], esnk[:, m:m + 1], ALU.add))
                        else:
                            dve.wait_ge(exped, m + 1)
                        o.then(nc.vector.reciprocal(den[:, m:m + 1], den[:, m:m + 1]))
                        dve.wait_ge(mixed, m + 1)
                        if m >= 8 and m % 4 == 0:
                            dve.wait_ge(back, m // 4 - 1)
                        nc.vector.tensor_scalar(o_tok[:, (m // 4) % 2, h * HEAD:(h + 1) * HEAD], ps_o[:, m % 2, 0:HEAD],
                                                den[:, m:m + 1], None, ALU.mult).then_inc(scaled, 1)

            @block.scalar
            def _(act):
                act.wait_ge(varied, 1)
                nc.scalar.activation(rs[:, :], rs[:, :], ACT.Sqrt).then_inc(rooted, 1)
                for b in range(6):
                    act.wait_ge(turned, b + 1)
                    t0, tw = ((0, SEQ), (SEQ, CTX))[b // 3]
                    dst = (qT[:, 0, t0:t0 + tw], qT[:, 1, t0:t0 + tw], kT[:, t0:t0 + tw])[b % 3]
                    nc.scalar.activation(dst, ps_s[:, b % 2, 0:tw], ACT.Copy).then_inc(kept, 1)

                def turned_back(i):
                    act.wait_ge(back, i + 1)
                    nc.scalar.activation(yT[:, 4 * win:4 * win + 2, i * P:(i + 1) * P],
                                         ps_o[:, 0, 128:128 + 2 * P].rearrange("p (a b) -> p a b", b=P), ACT.Copy).then_inc(back_kept, 1)

                for n in range(NU + 1):
                    if n < NU:
                        i, h, keys = units[n]
                        act.wait_ge(topped, n + 1)
                        if n >= 2:
                            act.wait_ge(spread, n - 1)
                        nc.scalar.activation(prob[:, n % 2, 0:len(keys), :].rearrange("p a b -> p (a b)"), ps_s[:, n % 2, 0:len(keys) * P],
                                             ACT.Exp, bias=neg[:, n:n + 1], scale=SCALE, accum_out=den[:, n:n + 1]).then_inc(exped, 1)
                        if win:
                            nc.scalar.activation(esnk[:, n:n + 1], snk[:, h:h + 1], ACT.Exp, bias=neg[:, n:n + 1]).then_inc(exped, 1)
                    if n >= 1:
                        m = n - 1
                        nk = len(units[m][2])
                        act.wait_ge(spread, m + 1)
                        if m >= 2:
                            act.wait_ge(mixed, m - 1)
                        nc.scalar.activation(probT[:, m % 2, 0:nk, :].rearrange("p a b -> p (a b)"), ps_t[:, 0:nk * P], ACT.Copy).then_inc(spread_kept, 1)
                        if m % N_Q == 0 and m:
                            turned_back(m // N_Q - 1)
                turned_back(NT - 1)

            @block.tensor
            def _(pe):
                ident = cst[:, C_ID:C_ID + P]
                pe.wait_ge(normed, 1)
                for b in range(6):
                    if b >= 2:
                        pe.wait_ge(kept, b - 1)
                    tiles = (range(NTX), range(NTX, NT))[b // 3]
                    for n, i in enumerate(tiles):
                        src = tmp[:, i, (b % 3) * P:(b % 3 + 1) * P]
                        last = nc.tensor.transpose(ps_s[:, b % 2, n * P:(n + 1) * P], src, ident)
                    last.then_inc(turned, 1)
                pe.wait_ge(kept, 6)

                def scores(n):
                    i, h, keys = units[n]
                    kv, pair = h // 2, h % 2
                    if n >= 2:
                        pe.wait_ge(exped, (1 + win) * (n - 1))
                    for c, j, m in runs(keys):
                        masked = [t for t in range(j, j + m) if win and i < NTX and t < NTX and abs(t - i) == 1]
                        last = nc.tensor.matmul(ps_s[:, n % 2, c:c + m * P], qT[64 * kv:64 * kv + 64, pair, i * P:(i + 1) * P],
                                                kT[64 * kv:64 * kv + 64, j * P:(j + m) * P], start=True, stop=True)
                        for t in masked:
                            cm = C_PREV if t < i else C_NEXT
                            cc = c + (t - j) * P
                            last = nc.tensor.matmul(ps_s[:, n % 2, cc:cc + P], ident, cst[:, cm:cm + P], start=False,
                                                    stop=t == masked[-1], skip_group_check=True)
                    last.then_inc(scored, 1)

                def turn_back(i):
                    pe.wait_ge(scaled, 4 * (i + 1))
                    if i:
                        pe.wait_ge(back_kept, i)
                    for a in range(2):
                        last = nc.tensor.transpose(ps_o[:, 0, 128 + a * P:128 + (a + 1) * P], o_tok[:, i % 2, a * P:(a + 1) * P], ident)
                    last.then_inc(back, 1)

                for n in range(NU + 2):
                    if n < NU:
                        scores(n)
                    if 1 <= n <= NU:
                        m = n - 1
                        nk = len(units[m][2])
                        pe.wait_ge(exped, (1 + win) * m + 1)
                        if m:
                            pe.wait_ge(spread_kept, m)
                        for a in range(nk):
                            last = nc.tensor.transpose(ps_t[:, a * P:(a + 1) * P], prob[:, m % 2, a, :], ident)
                        last.then_inc(spread, 1)
                    if n >= 2:
                        m = n - 2
                        i, h, keys = units[m]
                        pe.wait_ge(spread_kept, m + 1)
                        if m >= 2:
                            pe.wait_ge(scaled, m - 1)
                        if m % 2 == 0 and m >= 4:
                            if m % 4 == 0:
                                turn_back(m // 4 - 1)
                                pe.wait_ge(back_kept, m // 4)
                        for a, j in enumerate(keys):
                            last = nc.tensor.matmul(ps_o[:, m % 2, 0:HEAD], probT[:, m % 2, a, :], vals(j, h // 2),
                                                    start=(a == 0), stop=(a == len(keys) - 1))
                        last.then_inc(mixed, 1)
                turn_back(NT - 1)


def convolution(nc, A, g, layer):
    pf, cst, yT = g["pf"], g["cst"], g["yT"]
    W = PAD + SEQ + PAD + CTX + PAD
    L = SEQ + PAD + CTX
    SEG = ((0, SEQ), (SEQ + PAD, CTX))
    with ExitStack() as es:
        sb = lambda n, s: es.enter_context(nc.sbuf_tensor(f"conv_{n}", s, F32))
        hp = sb("hp", [P, 2, W])
        acc = sb("acc", [P, 2, L])
        tok = sb("tok", [P, NT, GROUP])
        sq = sb("sq", [P, NT, GROUP])
        st = sb("st", [P, 3, NT])
        dw = sb("dw", [P, 2, CONV_W])
        col = sb("col", [P, 4, 2])
        pw = sb("pw", [P, 2, GROUP])
        act_in = sb("lin", [P, 2, TOK])
        sil = sb("sil", [P, 2, TOK])
        ps = es.enter_context(nc.psum_tensor("conv_ps", [P, 4, 2 * BANK], F32))
        names = "loaded gated padded own own_a convolved turned tok_kept varied rooted normed back sig_done lin_done silued done kept"
        with stage(nc, "conv", names) as (block, loaded, gated, padded, own, own_a, convolved, turned, tok_kept, varied, rooted,
                                          normed, back, sig_done, lin_done, silued, done, kept):
            NL = 10

            @block.sync
            def _(sp):
                one = lambda n: A[n][bass.ds(layer, 1), :].rearrange("a (c p) -> p (a c)", p=P)
                for c in range(2):
                    sp.dma_start(dw[:, c, :], A["conv_dw_w"][bass.ds(layer, 1), :, c * P:(c + 1) * P].rearrange("a k p -> p (a k)"),
                                 allow_slow_non_contiguous=True).then_inc(loaded, 16)
                for n, v in enumerate(("conv_dw_b", "conv_ln_g", "conv_ln_b", "conv_pw_b")):
                    sp.dma_start(col[:, n, :], one(v), allow_slow_non_contiguous=True).then_inc(loaded, 16)
                sp.dma_start(pw[:, :, :], A["conv_pw_w"][bass.ds(layer, 1)].rearrange("a (c p) n -> p (a c) n", p=P)).then_inc(loaded, 16)

            @block.scalar
            def _(act):
                nc.scalar.activation(pf[:, 2:4, :], pf[:, 2:4, :], ACT.Sigmoid).then_inc(gated, 1)
                for i in range(NT):
                    act.wait_ge(turned, i + 1)
                    nc.scalar.activation(tok[:, i, :], ps[:, i % 4, 0:GROUP], ACT.Copy).then_inc(tok_kept, 1)
                act.wait_ge(varied, 1)
                nc.scalar.activation(st[:, 1, :], st[:, 1, :], ACT.Sqrt).then_inc(rooted, 1)
                for c in range(2):
                    act.wait_ge(back, c + 1)
                    nc.scalar.activation(act_in[:, c, :], ps[:, c, 0:TOK], ACT.Identity, scale=col[:, 1, c:c + 1], bias=col[:, 2, c:c + 1]).then_inc(lin_done, 1)
                    nc.scalar.activation(sil[:, c, :], ps[:, c, 0:TOK], ACT.Sigmoid, scale=col[:, 1, c:c + 1], bias=col[:, 2, c:c + 1]).then_inc(sig_done, 1)
                for c in range(2):
                    act.wait_ge(done, c + 1)
                    nc.scalar.activation(yT[:, 2 + c, :], ps[:, 2 + c, 0:TOK], ACT.Identity, bias=col[:, 3, c:c + 1]).then_inc(kept, 1)

            @block.vector
            def _(dve):
                o = Own(dve, own)
                o.then(nc.vector.memset(hp[:, :, :], 0.0))
                dve.wait_ge(gated, 1)
                for (a, w), t0 in zip(SEG, (0, SEQ)):
                    o(nc.vector.tensor_tensor(hp[:, :, PAD + a:PAD + a + w], pf[:, 0:2, t0:t0 + w], pf[:, 2:4, t0:t0 + w], ALU.mult))
                o.settle()
                dve.wait_ge(loaded, 16 * 7)
                for c in range(2):
                    o(nc.vector.tensor_scalar(acc[:, c, :], hp[:, c, 0:L], dw[:, c, 0:1], col[:, 0, c:c + 1], ALU.mult, ALU.add))
                for k in range(1, CONV_W):
                    for c in range(2):
                        dve.wait_ge(own, o.n - 1)
                        o(nc.vector.scalar_tensor_tensor(acc[:, c, :], hp[:, c, k:k + L], dw[:, c, k:k + 1], acc[:, c, :], ALU.mult, ALU.add))
                dve.wait_ge(own, o.n)
                dve.sem_inc(convolved, 1)
                dve.wait_ge(tok_kept, NT)
                o.then(nc.vector.tensor_reduce(st[:, 0, :], tok[:, :, :], AX.X, ALU.add))
                o.then(nc.vector.tensor_scalar(st[:, 0, :], st[:, 0, :], 1.0 / GROUP, None, ALU.mult))
                o.then(nc.vector.tensor_tensor(tok[:, :, :], tok[:, :, :], st[:, 0, :].rearrange("p (t o) -> p t o", o=1)
                                               .broadcast_to([P, NT, GROUP]), ALU.subtract))
                o.then(nc.vector.tensor_tensor(sq[:, :, :], tok[:, :, :], tok[:, :, :], ALU.mult))
                o.then(nc.vector.tensor_reduce(st[:, 1, :], sq[:, :, :], AX.X, ALU.add))
                nc.vector.tensor_scalar(st[:, 1, :], st[:, 1, :], 1.0 / GROUP, EPS, ALU.mult, ALU.add).then_inc(varied, 1)
                dve.wait_ge(rooted, 1)
                o.then(nc.vector.reciprocal(st[:, 2, :], st[:, 1, :]))
                nc.vector.tensor_tensor(tok[:, :, :], tok[:, :, :], st[:, 2, :].rearrange("p (t o) -> p t o", o=1)
                                        .broadcast_to([P, NT, GROUP]), ALU.mult).then_inc(normed, 1)
                for c in range(2):
                    dve.wait_ge(sig_done, c + 1)
                    dve.wait_ge(lin_done, c + 1)
                    nc.vector.tensor_tensor(sil[:, c, :], sil[:, c, :], act_in[:, c, :], ALU.mult).then_inc(silued, 1)

            @block.tensor
            def _(pe):
                ident = cst[:, C_ID:C_ID + P]
                pe.wait_ge(convolved, 1)
                for i in range(NT):
                    if i >= 4:
                        pe.wait_ge(tok_kept, i - 3)
                    at = i * P + (PAD if i >= NTX else 0)
                    for c in range(2):
                        last = nc.tensor.transpose(ps[:, i % 4, c * P:(c + 1) * P], acc[:, c, at:at + P], ident)
                    last.then_inc(turned, 1)
                pe.wait_ge(normed, 1)
                for c in range(2):
                    for i in range(NT):
                        last = nc.tensor.transpose(ps[:, c, i * P:(i + 1) * P], tok[:, i, c * P:(c + 1) * P], ident)
                    last.then_inc(back, 1)
                pe.wait_ge(silued, 2)
                for c in range(2):
                    for t0, tw in ((0, SEQ), (SEQ, CTX)):
                        for k in range(2):
                            last = nc.tensor.matmul(ps[:, 2 + c, t0:t0 + tw], pw[:, k, c * P:(c + 1) * P], sil[:, k, t0:t0 + tw],
                                                    start=(k == 0), stop=(k == 1))
                    last.then_inc(done, 1)


def recurrence(nc, A, g, layer):
    pt, pf, cst, yT, lb = g["pt"], g["pf"], g["cst"], g["yT"], g["lb"]
    G = 2
    ZC, VC, GC = 6, 1024, 1280
    q = pf[:, 4:6, :]
    scr = pf[:, 0:4, :].rearrange("p a t -> p (a t)").rearrange("p (i h n) -> p i h n", i=NT, h=2)
    ORDER = ([4, 5, 0, 1, 2, 3], [5, 4, 3, 2, 1, 0])
    NM = LEVELS + 1
    with ExitStack() as es:
        sb = lambda n, s: es.enter_context(nc.sbuf_tensor(f"rec_{n}", s, F32))
        e1, e2, e3, kk = (sb(n, [P, G, TOK]) for n in ("e1", "e2", "e3", "k"))
        cum = sb("cum", [P, G, NT, P + 1])
        qe = sb("qe", [P, 2, G, TOK])
        ke = sb("ke", [P, 2, G, TOK])
        lbl = sb("lbl", [P, 3, 4])
        dec = sb("dec", [P, G, NT])
        state = sb("state", [P, G, HEAD])
        ktok = sb("ktok", [P, NT, GROUP])
        osum = sb("osum", [P, NT, GROUP])
        rs = sb("rs", [P, NT * 4])
        onorm = sb("onorm", [P, HEAD])
        ps_s = es.enter_context(nc.psum_tensor("rec_ps_s", [P, 2, 2, BANK], F32))
        ps_o = es.enter_context(nc.psum_tensor("rec_ps_o", [P, 2, BANK], F32))
        ps_u = es.enter_context(nc.psum_tensor("rec_ps_u", [P, BANK], F32))
        names = ("loaded own own_a z_in first_ln diff lse_ln k_arg k_exp level_diff level_exp factors scored picked "
                 "carry_diff carry_exp carried turned turned_kept read updated state_done summed varied rooted sig gate_out back back_kept")
        with stage(nc, "rec", names) as (block, loaded, own, own_a, z_in, first_ln, diff, lse_ln, k_arg, k_exp, level_diff, level_exp,
                                         factors, scored, picked, carry_diff, carry_exp, carried, turned, turned_kept, read, updated,
                                         state_done, summed, varied, rooted, sig, gate_out, back, back_kept):
            def by_tile(ap):
                return ap.rearrange("p g (i t) -> p (g i) t", t=P)

            cum_t = cum[:, :, :, :].rearrange("p g i t -> p (g i) t")

            @block.sync
            def _(sp):
                sp.dma_start(onorm[:, :], A["hgrn_onorm_g"][bass.ds(layer, 1), :].broadcast_to([P, HEAD])).then_inc(loaded, 16)

            @block.scalar
            def _(act):
                o = Own(act, own_a)
                for d in range(2):
                    z = pf[:, ZC + 2 * d:ZC + 2 * d + 2, :]
                    if d:
                        act.wait_ge(carried, 1)
                    o.then(nc.scalar.activation(e1[:, :, :], z, ACT.Abs))
                    o.then(nc.scalar.activation(e1[:, :, :], e1[:, :, :], ACT.Exp, scale=-1.0))
                    nc.scalar.activation(e2[:, :, :], e1[:, :, :], ACT.Ln, bias=1.0).then_inc(first_ln, 1)
                    act.wait_ge(diff, d + 1)
                    o.then(nc.scalar.activation(qe[:, 0, :, :], qe[:, 0, :, :], ACT.Abs))
                    o.then(nc.scalar.activation(qe[:, 0, :, :], qe[:, 0, :, :], ACT.Exp, scale=-1.0))
                    nc.scalar.activation(qe[:, 0, :, :], qe[:, 0, :, :], ACT.Ln, bias=1.0).then_inc(lse_ln, 1)
                    act.wait_ge(k_arg, d + 1)
                    nc.scalar.activation(kk[:, :, :], kk[:, :, :], ACT.Exp).then_inc(k_exp, 1)
                    for lev in range(LEVELS):
                        act.wait_ge(level_diff, LEVELS * d + lev + 1)
                        o.then(nc.scalar.activation(e3[:, :, :], e1[:, :, :], ACT.Abs))
                        if lev:
                            act.wait_ge(factors, NM * d + lev + 1)
                        nc.scalar.activation(e2[:, :, :], e3[:, :, :], ACT.Exp, scale=-1.0).then_inc(level_exp, 1)
                    act.wait_ge(factors, NM * (d + 1))
                    nc.scalar.activation(by_tile(e2[:, :, :]), cum_t[:, :, 1 - d:1 - d + P], ACT.Exp).then_inc(carry_exp, 1)
                    nc.scalar.activation(dec[:, :, :], cum[:, :, :, P], ACT.Exp).then_inc(carry_exp, 1)
                    act.wait_ge(carry_diff, d + 1)
                    nc.scalar.activation(e1[:, :, :], e1[:, :, :], ACT.Exp).then_inc(carry_exp, 1)
                    for i in range(NT):
                        act.wait_ge(turned, NT * d + i + 1)
                        nc.scalar.activation(ktok[:, i, :], ps_s[:, i % 2, 0, 0:GROUP], ACT.Copy).then_inc(turned_kept, 1)
                act.wait_ge(varied, 1)
                nc.scalar.activation(rs[:, :], rs[:, :], ACT.Sqrt).then_inc(rooted, 1)
                nc.scalar.activation(qe[:, 0, :, :].rearrange("p g (i c) -> p (g i) c", c=GROUP), pt[:, :, GC:GC + GROUP], ACT.Sigmoid).then_inc(sig, 1)
                for i in range(NT):
                    act.wait_ge(back, i + 1)
                    nc.scalar.activation(yT[:, 6:8, i * P:(i + 1) * P], ps_s[:, i % 2, 0, 0:2 * P].rearrange("p (a b) -> p a b", b=P), ACT.Copy).then_inc(back_kept, 1)

            @block.vector
            def _(dve):
                o = Own(dve, own)
                tt = nc.vector.tensor_tensor
                o(nc.vector.memset(cum[:, :, :, 0], 0.0))
                o.then(nc.vector.tensor_copy(lbl[:, :, :], lb[:, bass.ds(layer, 1), :, :].rearrange("p a b c -> p (a b) c")))
                for d in range(2):
                    z = pf[:, ZC + 2 * d:ZC + 2 * d + 2, :]
                    o.then(nc.vector.tensor_scalar(e3[:, :, :], z, 0.0, None, ALU.min))
                    o.then(tt(kk[:, :, :], e3[:, :, :], z, ALU.subtract))
                    dve.wait_ge(first_ln, d + 1)
                    for gg in range(G):
                        o(nc.vector.tensor_scalar(e1[:, gg, :], kk[:, gg, :], lbl[:, 1, 2 * d + gg:2 * d + gg + 1], None, ALU.add))
                    o.settle()
                    tt(qe[:, 0, :, :], e3[:, :, :], e1[:, :, :], ALU.subtract).then_inc(diff, 1)
                    o.then(tt(e3[:, :, :], e3[:, :, :], e1[:, :, :], ALU.max))
                    tt(kk[:, :, :], kk[:, :, :], e2[:, :, :], ALU.subtract).then_inc(k_arg, 1)
                    o.then(tt(e3[:, :, :], e3[:, :, :], e2[:, :, :], ALU.subtract))
                    dve.wait_ge(lse_ln, d + 1)
                    o.then(tt(e3[:, :, :], e3[:, :, :], qe[:, 0, :, :], ALU.add))
                    ones = cst[:, C_COL:C_COL + 1].broadcast_to([P, P])
                    for gg in range(G):
                        for i in range(NT):
                            o(nc.vector.tensor_tensor_scan(cum[:, gg, i, 1:P + 1], ones, e3[:, gg, i * P:(i + 1) * P], 0.0, ALU.mult, ALU.add))
                    dve.wait_ge(k_exp, d + 1)
                    for gg in range(G):
                        o(nc.vector.tensor_scalar(kk[:, gg, :], kk[:, gg, :], lbl[:, 2, 2 * d + gg:2 * d + gg + 1], None, ALU.mult))
                    o.settle()
                    dve.sem_inc(factors, 1)
                    for lev in range(LEVELS + 1):
                        if lev < LEVELS:
                            n = 1 << lev
                            at = cum_t[:, :, 1 - d:1 - d + P].rearrange("p a (b t) -> p a b t", t=2 * n)
                            mid = cum_t[:, :, 0:P].rearrange("p a (b t) -> p a b t", t=2 * n)[:, :, :, n:n + 1]
                            if lev:
                                dve.wait_ge(level_exp, LEVELS * d + lev)
                            tt(by_tile(e1[:, :, :]).rearrange("p a (b t) -> p a b t", t=2 * n), at,
                               mid.broadcast_to([P, G * NT, P // (2 * n), 2 * n]), ALU.subtract).then_inc(level_diff, 1)
                        for i in range(NT):
                            m = (NM * d + lev) * NT + i
                            dve.wait_ge(scored, m + 1)
                            src = ps_s[:, m % 2, :, 0:2 * P]
                            dst = scr[:, i, :, :]
                            four = lambda ap: ap.rearrange("p h (g t) -> p h g t", t=P)
                            if lev == 0:
                                mask = cst[:, C_ID:C_ID + P].rearrange("p (a b t) -> p a b t", a=1, b=1)
                                tt(four(dst), four(src), mask.broadcast_to([P, 2, 2, P]), ALU.mult).then_inc(picked, 1)
                            else:
                                cm = (C_LEV, C_LEVR)[d] + (lev - 1) * P
                                mask = cst[:, cm:cm + P].bitcast(U32).rearrange("p (a b t) -> p a b t", a=1, b=1)
                                dve.wait_ge(picked, m - NT + 1)
                                nc.vector.copy_predicated(four(dst), mask.broadcast_to([P, 2, 2, P]), four(src)).then_inc(picked, 1)
                        if lev < LEVELS:
                            dve.wait_ge(level_exp, LEVELS * d + lev + 1)
                            o(tt(qe[:, lev % 2, :, :], q, e2[:, :, :], ALU.mult))
                            o.then(tt(ke[:, lev % 2, :, :], kk[:, :, :], e2[:, :, :], ALU.mult))
                            dve.sem_inc(factors, 1)
                    tt(by_tile(e1[:, :, :]), cum_t[:, :, P:P + 1].broadcast_to([P, G * NT, P]), cum_t[:, :, 1 - d:1 - d + P],
                       ALU.subtract).then_inc(carry_diff, 1)
                    dve.wait_ge(carry_exp, 3 * (d + 1))
                    to_start, to_end = e2[:, :, :], e1[:, :, :]
                    o(tt(qe[:, 0, :, :], q, (to_start, to_end)[d], ALU.mult))
                    o.then(tt(ke[:, 0, :, :], kk[:, :, :], (to_end, to_start)[d], ALU.mult))
                    dve.sem_inc(carried, 1)
                    for n, i in enumerate(ORDER[d]):
                        dve.wait_ge(updated, NT * d + n + 1)
                        dve.wait_ge(read, NT * d + n + 1)
                        for gg in range(G):
                            if n == 0:
                                o(nc.vector.tensor_copy(state[:, gg, :], ps_u[:, gg * HEAD:(gg + 1) * HEAD]))
                            else:
                                o(nc.vector.scalar_tensor_tensor(state[:, gg, :], state[:, gg, :], dec[:, gg, i:i + 1],
                                                                 ps_u[:, gg * HEAD:(gg + 1) * HEAD], ALU.mult, ALU.add))
                        dst = osum[:, i, :].rearrange("p (g h e) -> p h g e", g=2, h=2)
                        src = ps_o[:, :, 0:2 * HEAD].rearrange("p h (g e) -> p h g e", e=HEAD)
                        if d == 0:
                            o(nc.vector.tensor_copy(dst, src))
                        else:
                            o(tt(dst, dst, src, ALU.add))
                        o.settle()
                        dve.sem_inc(state_done, 1)
                heads = lambda ap: ap.rearrange("p i (h e) -> p (i h) e", e=HEAD)
                wide = lambda k: ke[:, k, :, :].rearrange("p g (i c) -> p (g i) c", c=GROUP)
                o.then(tt(wide(0), osum[:, :, :], osum[:, :, :], ALU.mult))
                o.then(nc.vector.tensor_reduce(rs[:, :], heads(wide(0)), AX.X, ALU.add))
                nc.vector.tensor_scalar(rs[:, :], rs[:, :], 1.0 / HEAD, EPS, ALU.mult, ALU.add).then_inc(varied, 1)
                dve.wait_ge(rooted, 1)
                o.then(nc.vector.reciprocal(rs[:, :], rs[:, :]))
                o.then(tt(heads(osum[:, :, :]), heads(osum[:, :, :]), rs[:, :].rearrange("p (h o) -> p h o", o=1).broadcast_to([P, 4 * NT, HEAD]), ALU.mult))
                dve.wait_ge(loaded, 16)
                o.then(tt(heads(osum[:, :, :]), heads(osum[:, :, :]), onorm[:, :].rearrange("p (o e) -> p o e", o=1).broadcast_to([P, 4 * NT, HEAD]), ALU.mult))
                dve.wait_ge(sig, 1)
                o.then(tt(wide(1), qe[:, 0, :, :].rearrange("p g (i c) -> p (g i) c", c=GROUP), pt[:, :, GC:GC + GROUP], ALU.mult))
                tt(osum[:, :, :], osum[:, :, :], wide(1), ALU.mult).then_inc(gate_out, 1)

            @block.tensor
            def _(pe):
                ident = cst[:, C_ID:C_ID + P]
                for d in range(2):
                    for lev in range(NM):
                        pe.wait_ge(factors, NM * d + lev + 1)
                        for i in range(NT):
                            m = (NM * d + lev) * NT + i
                            if m >= 2:
                                pe.wait_ge(picked, m - 1)
                            for gg in range(G):
                                for hf in range(2):
                                    part = slice(64 * hf, 64 * hf + 64)
                                    if lev == 0:
                                        l, r = kk[part, gg, i * P:(i + 1) * P], pf[part, 4 + gg, i * P:(i + 1) * P]
                                    else:
                                        l = ke[part, (lev - 1) % 2, gg, i * P:(i + 1) * P]
                                        r = qe[part, (lev - 1) % 2, gg, i * P:(i + 1) * P]
                                    last = nc.tensor.matmul(ps_s[:, m % 2, hf, gg * P:(gg + 1) * P], l, r, start=True, stop=True)
                            last.then_inc(scored, 1)
                    pe.wait_ge(carried, d + 1)
                    pe.wait_ge(picked, NM * NT * (d + 1))
                    for i in range(NT):
                        if i >= 2:
                            pe.wait_ge(turned_kept, NT * d + i - 1)
                        for gg in range(G):
                            last = nc.tensor.transpose(ps_s[:, i % 2, 0, gg * P:(gg + 1) * P], ke[:, 0, gg, i * P:(i + 1) * P], ident)
                        last.then_inc(turned, 1)
                    pe.wait_ge(turned_kept, NT * (d + 1))
                    for n, i in enumerate(ORDER[d]):
                        if n or d:
                            pe.wait_ge(state_done, NT * d + n)
                        for hf in range(2):
                            part = slice(64 * hf, 64 * hf + 64)
                            for gg in range(G):
                                v = pt[:, i, VC + (2 * gg + hf) * HEAD:VC + (2 * gg + hf + 1) * HEAD]
                                last = nc.tensor.matmul(ps_o[:, hf, gg * HEAD:(gg + 1) * HEAD], scr[:, i, hf, gg * P:(gg + 1) * P], v,
                                                        start=True, stop=(n == 0))
                                if n:
                                    last = nc.tensor.matmul(ps_o[:, hf, gg * HEAD:(gg + 1) * HEAD], qe[part, 0, gg, i * P:(i + 1) * P],
                                                            state[part, gg, :], start=False, stop=True)
                        last.then_inc(read, 1)
                        for gg in range(G):
                            for hf in range(2):
                                v = pt[:, i, VC + (2 * gg + hf) * HEAD:VC + (2 * gg + hf + 1) * HEAD]
                                last = nc.tensor.matmul(ps_u[64 * hf:64 * hf + 64, gg * HEAD:(gg + 1) * HEAD],
                                                        ktok[:, i, gg * P + 64 * hf:gg * P + 64 * hf + 64], v, start=True, stop=True)
                        last.then_inc(updated, 1)
                pe.wait_ge(gate_out, 1)
                for i in range(NT):
                    if i >= 2:
                        pe.wait_ge(back_kept, i - 1)
                    for a in range(2):
                        last = nc.tensor.transpose(ps_s[:, i % 2, 0, a * P:(a + 1) * P], osum[:, i, a * P:(a + 1) * P], ident)
                    last.then_inc(back, 1)


def gated_add(dve, o, g, gate, ps, i, h, tmp):
    x = g["x"]
    s = 0 if i < NTX else 1
    o.then(dve.tensor_tensor(tmp, ps, gate[:, s, h * BANK:(h + 1) * BANK], ALU.mult))
    return dve.tensor_tensor(x[:, i, h * BANK:(h + 1) * BANK], x[:, i, h * BANK:(h + 1) * BANK], tmp, ALU.add)


def out_projection(nc, A, g, layer):
    yT = g["yT"]
    jobs = [(h, i) for h in range(2) for i in range(NT)]
    with ExitStack() as es:
        w = es.enter_context(nc.sbuf_tensor("w_out_t", [P, 2, KT, BANK], F32))
        gate = es.enter_context(nc.sbuf_tensor("out_gate", [P, 2, D], F32))
        tmp = es.enter_context(nc.sbuf_tensor("out_tmp", [P, BANK], F32))
        pr = es.enter_context(nc.psum_tensor("out_ps_row", [P, 2, 2 * BANK], F32))
        ps = es.enter_context(nc.psum_tensor("out_ps", [P, 4, BANK], F32))
        with stage(nc, "outp", "w0 w1 spread gates own done added") as (block, w0, w1, spread, gates, own, done, added):
            w_in = (w0, w1)

            @block.sync
            def _(sp):
                for h in range(2):
                    sp.dma_start(w[:, h, :, :], A["w_out"][bass.ds(layer, 1), :, h * BANK:(h + 1) * BANK]
                                 .rearrange("a (k p) n -> p (a k) n", p=P)).then_inc(w_in[h], 16)

            @block.tensor
            def _(pe):
                for s in range(2):
                    broadcast_row(nc, g, pr[:, s, :], 2, s).then_inc(spread, 1)
                for n, (h, i) in enumerate(jobs):
                    if i == 0:
                        pe.wait_ge(w_in[h], 16)
                    if n >= 4:
                        pe.wait_ge(added, n - 3)
                    for k in range(KT):
                        last = nc.tensor.matmul(ps[:, n % 4, :], yT[:, k, i * P:(i + 1) * P], w[:, h, k, :], start=(k == 0), stop=(k == KT - 1))
                    last.then_inc(done, 1)

            @block.scalar
            def _(act):
                for s in range(2):
                    act.wait_ge(spread, s + 1)
                    nc.scalar.activation(gate[:, s, :], pr[:, s, :], ACT.Copy).then_inc(gates, 1)

            @block.vector
            def _(dve):
                o = Own(dve, own)
                dve.wait_ge(gates, 2)
                for n, (h, i) in enumerate(jobs):
                    dve.wait_ge(done, n + 1)
                    if n:
                        dve.wait_ge(added, n)
                    gated_add(nc.vector, o, g, gate, ps[:, n % 4, :], i, h, tmp[:, :]).then_inc(added, 1)


def shared_expert(nc, A, g, layer, hT, gate):
    cst = g["cst"]
    with ExitStack() as es:
        sb = lambda n, s: es.enter_context(nc.sbuf_tensor(f"sh_{n}", s, F32))
        wgu = sb("wgu", [P, KT, 2 * HID])
        wd = sb("wd", [P, 2, D])
        sig = sb("sig", [P, 2, HID])
        hid = sb("hid", [P, 2, HID])
        hidT = sb("hidT", [P, 2, HID])
        tmp = sb("tmp", [P, BANK])
        ps_gu = es.enter_context(nc.psum_tensor("sh_ps_gu", [P, 2, BANK], F32))
        ps_h = es.enter_context(nc.psum_tensor("sh_ps_h", [P, 2, BANK], F32))
        ps_y = es.enter_context(nc.psum_tensor("sh_ps_y", [P, 2, 2 * BANK], F32))
        names = "w_in spread gates own gu_done sig_done hid_done turned hidT_done y_done y_used"
        with stage(nc, "shared", names) as (block, w_in, spread, gates, own, gu_done, sig_done, hid_done, turned, hidT_done, y_done, y_used):
            @block.sync
            def _(sp):
                for n, c in (("sh_w_gate", 0), ("sh_w_up", HID)):
                    sp.dma_start(wgu[:, :, c:c + HID], A[n][bass.ds(layer, 1)].rearrange("a (k p) n -> p (a k) n", p=P)).then_inc(w_in, 16)
                sp.dma_start(wd[:, :, :], A["sh_w_down"][bass.ds(layer, 1)].rearrange("a (k p) n -> p (a k) n", p=P)).then_inc(w_in, 16)

            @block.tensor
            def _(pe):
                ident = cst[:, C_ID:C_ID + P]
                for s in range(2):
                    broadcast_row(nc, g, ps_y[:, s, :], 5, s).then_inc(spread, 1)
                pe.wait_ge(w_in, 48)
                pe.wait_ge(gates, 2)
                for i in range(NT + 1):
                    if i < NT:
                        if i >= 2:
                            pe.wait_ge(hid_done, i - 1)
                        for k in range(KT):
                            last = nc.tensor.matmul(ps_gu[:, i % 2, :], hT[:, k, i * P:(i + 1) * P], wgu[:, k, :], start=(k == 0), stop=(k == KT - 1))
                        last.then_inc(gu_done, 1)
                    if i:
                        m = i - 1
                        pe.wait_ge(hid_done, m + 1)
                        for a in range(2):
                            last = nc.tensor.transpose(ps_h[:, m % 2, a * P:(a + 1) * P], hid[:, m % 2, a * P:(a + 1) * P], ident)
                        last.then_inc(turned, 1)
                        pe.wait_ge(hidT_done, m + 1)
                        if m >= 2:
                            pe.wait_ge(y_used, 2 * (m - 1))
                        for h in range(2):
                            for a in range(2):
                                last = nc.tensor.matmul(ps_y[:, m % 2, h * BANK:(h + 1) * BANK], hidT[:, m % 2, a * P:(a + 1) * P],
                                                        wd[:, a, h * BANK:(h + 1) * BANK], start=(a == 0), stop=(a == 1))
                        last.then_inc(y_done, 1)

            @block.scalar
            def _(act):
                for s in range(2):
                    act.wait_ge(spread, s + 1)
                    nc.scalar.activation(gate[:, s, :], ps_y[:, s, :], ACT.Copy).then_inc(gates, 1)
                for i in range(NT):
                    act.wait_ge(gu_done, i + 1)
                    if i >= 2:
                        act.wait_ge(hid_done, i - 1)
                    nc.scalar.activation(sig[:, i % 2, :], ps_gu[:, i % 2, 0:HID], ACT.Sigmoid).then_inc(sig_done, 1)
                    act.wait_ge(turned, i + 1)
                    if i >= 2:
                        act.wait_ge(y_done, i - 1)
                    nc.scalar.activation(hidT[:, i % 2, :], ps_h[:, i % 2, 0:HID], ACT.Copy).then_inc(hidT_done, 1)

            @block.vector
            def _(dve):
                o = Own(dve, own)
                for i in range(NT + 1):
                    if i < NT:
                        dve.wait_ge(sig_done, i + 1)
                        if i >= 2:
                            dve.wait_ge(turned, i - 1)
                        o.then(nc.vector.tensor_tensor(sig[:, i % 2, :], sig[:, i % 2, :], ps_gu[:, i % 2, 0:HID], ALU.mult))
                        nc.vector.tensor_tensor(hid[:, i % 2, :], sig[:, i % 2, :], ps_gu[:, i % 2, HID:2 * HID], ALU.mult).then_inc(hid_done, 1)
                    if i:
                        m = i - 1
                        dve.wait_ge(y_done, m + 1)
                        dve.wait_ge(gates, 2)
                        for h in range(2):
                            if m or h:
                                dve.wait_ge(y_used, 2 * m + h)
                            gated_add(nc.vector, o, g, gate, ps_y[:, m % 2, h * BANK:(h + 1) * BANK], m, h, tmp[:, :]).then_inc(y_used, 1)


MAX_EXTRA = 64
N_SLOT_TAB = N_EXP + MAX_EXTRA


def routing(nc, A, g, layer, hT, r):
    cst = g["cst"]
    E = N_EXP
    with ExitStack() as es:
        sb = lambda n, s: es.enter_context(nc.sbuf_tensor(f"rt_{n}", s, F32))
        wr = sb("w", [P, KT, E])
        bias = sb("bias", [P, E])
        sc = sb("score", [P, NT, E])
        sel = sb("sel", [P, NT, E])
        best = sb("best", [P, NT, N_GRP, 8])
        gs = sb("gsum", [P, NT, N_GRP])
        gt = sb("gt", [P, NT, N_GRP, N_GRP])
        eq = sb("eq", [P, NT, N_GRP, N_GRP])
        keep = sb("keep", [P, NT, N_GRP])
        pen = sb("pen", [P, NT, N_GRP])
        top = sb("top", [P, NT, 8])
        rep = sb("rep", [P, NT, E])
        msk = sb("mask", [P, NT, E])
        den = sb("den", [P, NT])
        place = sb("place", [P, NT, E])
        ones = sb("ones", [P, P])
        extra = sb("extra", [P, E])
        cumx = sb("cumx", [P, E])
        over = sb("over", [P, E])
        le = sb("le", [P, E])
        colx = sb("colx", [P, 3])
        dg = sb("dg", [P, 2, MAX_EXTRA])
        npair = sb("npair", [1, 4])
        ps_l = es.enter_context(nc.psum_tensor("rt_ps_l", [P, BANK], F32))
        ps_r = es.enter_context(nc.psum_tensor("rt_ps_r", [P, BANK], F32))
        ps_c = es.enter_context(nc.psum_tensor("rt_ps_c", [P, BANK], F32))
        names = "w_in logits scored own chosen ranked extras listed"
        with stage(nc, "route", names) as (block, w_in, logits, scored, own, chosen, ranked, extras, listed):
            @block.sync
            def _(sp):
                sp.dma_start(wr[:, :, :], A["router_w"][bass.ds(layer, 1)].rearrange("a (k p) n -> p (a k) n", p=P)).then_inc(w_in, 16)
                sp.dma_start(bias[:, :], A["router_bias"][bass.ds(layer, 1), :].broadcast_to([P, E])).then_inc(w_in, 16)

            @block.scalar
            def _(act):
                act.wait_ge(logits, 1)
                nc.scalar.activation(sc[:, :, :].rearrange("p a b -> p (a b)"), ps_l[:, 0:NT * E], ACT.Sigmoid).then_inc(scored, 1)

            @block.tensor
            def _(pe):
                pe.wait_ge(w_in, 32)
                for i in range(NT):
                    for k in range(KT):
                        last = nc.tensor.matmul(ps_l[:, i * E:(i + 1) * E], hT[:, k, i * P:(i + 1) * P], wr[:, k, :], start=(k == 0), stop=(k == KT - 1))
                last.then_inc(logits, 1)
                pe.wait_ge(chosen, 1)
                for i in range(NT):
                    nc.tensor.matmul(ps_r[:, i * E:(i + 1) * E], cst[:, C_TRI:C_TRI + P], msk[:, i, :], start=True, stop=(i == 0))
                    for j in range(i):
                        nc.tensor.matmul(ps_r[:, i * E:(i + 1) * E], ones[:, :], msk[:, j, :], start=False, stop=(j == i - 1))
                for j in range(NT):
                    last = nc.tensor.matmul(ps_c[:, 0:E], ones[:, :], msk[:, j, :], start=(j == 0), stop=(j == NT - 1))
                last.then_inc(ranked, 1)
                pe.wait_ge(extras, 1)
                nc.tensor.matmul(ps_c[:, E:E + 2 * MAX_EXTRA], ones[:, :], dg[:, :, :].rearrange("p a b -> p (a b)"), start=True, stop=True).then_inc(listed, 1)

            @block.vector
            def _(dve):
                v = nc.vector
                o = Own(dve, own)
                o(v.memset(ones[:, :], 1.0))
                dve.wait_ge(scored, 1)
                dve.wait_ge(w_in, 32)
                o.then(v.tensor_tensor(sel[:, :, :], sc[:, :, :], bias[:, :].rearrange("p (o e) -> p o e", o=1).broadcast_to([P, NT, E]), ALU.add))
                for i in range(NT):
                    for q in range(N_GRP):
                        o(v.max(out=best[:, i, q, :], in_=sel[:, i, q * PER_GRP:(q + 1) * PER_GRP]))
                o.settle()
                o.then(v.tensor_tensor(gs[:, :, :], best[:, :, :, 0], best[:, :, :, 1], ALU.add))
                for i in range(NT):
                    other = gs[:, i, :].rearrange("p (o k) -> p o k", o=1).broadcast_to([P, N_GRP, N_GRP])
                    self_ = gs[:, i, :].rearrange("p (j o) -> p j o", o=1).broadcast_to([P, N_GRP, N_GRP])
                    o(v.tensor_tensor(gt[:, i, :, :], other, self_, ALU.is_gt))
                    o(v.tensor_tensor(eq[:, i, :, :], other, self_, ALU.is_equal))
                o.settle()
                low = cst[:, C_LOW:C_LOW + 64].rearrange("p (o n) -> p o n", o=1).broadcast_to([P, NT, 64])
                flat = lambda ap: ap.rearrange("p i a b -> p i (a b)")
                o.then(v.tensor_tensor(flat(eq[:, :, :, :]), flat(eq[:, :, :, :]), low, ALU.mult))
                o.then(v.tensor_tensor(gt[:, :, :, :], gt[:, :, :, :], eq[:, :, :, :], ALU.add))
                o.then(v.tensor_reduce(keep[:, :, :], gt[:, :, :, :], AX.X, ALU.add))
                o.then(v.tensor_scalar(keep[:, :, :], keep[:, :, :], 3.5, None, ALU.is_lt))
                o.then(v.tensor_scalar(pen[:, :, :], keep[:, :, :], -1.0, -NEG, ALU.add, ALU.mult))
                grp = lambda ap: ap.rearrange("p i (q e) -> p (i q) e", e=PER_GRP)
                wide = lambda ap: ap.rearrange("p i (q o) -> p (i q) o", o=1).broadcast_to([P, NT * N_GRP, PER_GRP])
                o.then(v.tensor_tensor(grp(sel[:, :, :]), grp(sel[:, :, :]), wide(keep[:, :, :]), ALU.mult))
                o.then(v.tensor_tensor(grp(sel[:, :, :]), grp(sel[:, :, :]), wide(pen[:, :, :]), ALU.add))
                for i in range(NT):
                    o(v.max(out=top[:, i, :], in_=sel[:, i, :]))
                o.settle()
                for i in range(NT):
                    o(v.match_replace(out=rep[:, i, :], in_to_replace=top[:, i, :], in_values=sel[:, i, :], imm_value=2 * NEG))
                o.settle()
                o.then(v.tensor_scalar(msk[:, :, :], rep[:, :, :], 1.5 * NEG, None, ALU.is_lt))
                o.then(v.tensor_tensor(sel[:, :, :], sc[:, :, :], msk[:, :, :], ALU.mult))
                o.then(v.tensor_reduce(den[:, :], sel[:, :, :], AX.X, ALU.add))
                o.then(v.reciprocal(den[:, :], den[:, :]))
                o.then(v.tensor_tensor(sel[:, :, :], sel[:, :, :], den[:, :].rearrange("p (t o) -> p t o", o=1).broadcast_to([P, NT, E]), ALU.mult))
                vals = r["vals"][:, :, :].rearrange("p t (e c) -> p t e c", c=4)
                o(v.tensor_scalar(vals[:, :, :, 2], sel[:, :, :], ROUTED_SCALE, None, ALU.mult))
                for i in range(NT):
                    o(v.tensor_tensor_scan(place[:, i, :], cst[:, C_COL:C_COL + 1].broadcast_to([P, E]), msk[:, i, :], 0.0, ALU.mult, ALU.add))
                o.settle()
                o.then(v.tensor_tensor(place[:, :, :], place[:, :, :], msk[:, :, :], ALU.subtract))
                o.then(v.tensor_scalar(msk[:, NTX:NT, :], msk[:, NTX:NT, :], cst[:, bass.ds(layer + (C_COL + 10), 1)], None, ALU.mult))
                dve.sem_inc(chosen, 1)
                token = cst[:, C_COL + 4:C_COL + 4 + NT].rearrange("p (t o) -> p t o", o=1).broadcast_to([P, NT, E])
                o(v.tensor_copy(vals[:, :, :, 0], token))
                o.then(v.tensor_scalar(sel[:, :, :], token, float(TOP_K), None, ALU.mult))
                o(v.tensor_tensor(vals[:, :, :, 1], sel[:, :, :], place[:, :, :], ALU.add))
                o(v.memset(vals[:, :, :, 3], 1.0))
                dve.wait_ge(ranked, 1)
                rank = r["rank"]
                o.then(v.scalar_tensor_tensor(rank[:, :, :].rearrange("p a b -> p (a b)"), ps_r[:, 0:NT * E], 1.0,
                                              msk[:, :, :].rearrange("p a b -> p (a b)"), ALU.add, ALU.mult))
                o(v.tensor_scalar(rank[:, :, :], rank[:, :, :], -1.0, None, ALU.add))
                o.then(v.tensor_scalar(extra[:, :], ps_c[:, 0:E], float(P), None, ALU.is_gt))
                for m in range(2, NT):
                    o.then(v.tensor_scalar(over[:, :], ps_c[:, 0:E], float(m * P), None, ALU.is_gt))
                    o.then(v.tensor_tensor(extra[:, :], extra[:, :], over[:, :], ALU.add))
                o.then(v.tensor_tensor_scan(cumx[:, :], cst[:, C_COL:C_COL + 1].broadcast_to([P, E]), extra[:, :], 0.0, ALU.mult, ALU.add))
                row = cst[:, C_COL + 1:C_COL + 2]
                o.then(v.tensor_scalar(le[:, :], cumx[:, :], row, None, ALU.is_le))
                o.then(v.tensor_reduce(colx[:, 0:1], le[:, :], AX.X, ALU.add))
                o.then(v.tensor_tensor(le[:, :], le[:, :], extra[:, :], ALU.mult))
                o.then(v.tensor_reduce(colx[:, 1:2], le[:, :], AX.X, ALU.add))
                o.then(v.tensor_tensor(colx[:, 1:2], row, colx[:, 1:2], ALU.subtract))
                o.then(v.tensor_scalar(colx[:, 1:2], colx[:, 1:2], 1.0, float(P), ALU.add, ALU.mult))
                o.then(v.tensor_scalar(colx[:, 2:3], colx[:, 0:1], E - 0.5, 1e6, ALU.is_gt, ALU.mult))
                o.then(v.tensor_tensor(colx[:, 1:2], colx[:, 1:2], colx[:, 2:3], ALU.add))
                o.then(v.tensor_scalar(colx[:, 0:1], colx[:, 0:1], float(E - 1), None, ALU.min))
                for a in range(2):
                    o(v.tensor_scalar(dg[:, a, :], cst[:, C_ID:C_ID + MAX_EXTRA], colx[:, a:a + 1], None, ALU.mult))
                o.settle()
                dve.sem_inc(extras, 1)
                first, expert = r["first"], r["expert"]
                o(v.memset(first[:, 0:E], 0.0))
                o(v.tensor_copy(expert[:, 0:E], cst[0:1, C_IOTA:C_IOTA + E]))
                dve.wait_ge(listed, 1)
                o(v.tensor_copy(expert[:, E:E + MAX_EXTRA], ps_c[0:1, E:E + MAX_EXTRA]))
                o(v.tensor_copy(first[:, E:E + MAX_EXTRA], ps_c[:, E + MAX_EXTRA:E + 2 * MAX_EXTRA]))
                o.then(v.tensor_copy(r["n_i"][:, 0:1], cumx[0:1, E - 1:E]))
                o.then(v.tensor_scalar(r["n_i"][:, 1:2], r["n_i"][:, 0:1], 1, None, ALU.bitwise_and))
                o.then(v.tensor_copy(npair[:, 0:2], r["n_i"][:, 0:2]))
                o.then(v.tensor_tensor(npair[:, 2:3], npair[:, 0:1], npair[:, 1:2], ALU.add))
                o.then(v.tensor_scalar(npair[:, 2:3], npair[:, 2:3], float(E), None, ALU.add))
                o.then(v.tensor_copy(r["n_i"][:, 2:3], npair[:, 2:3]))


def routed_experts(nc, A, g, layer, r, h_dram, y_dram):
    cst = g["cst"]
    rank, vals, first, expert, n_i = r["rank"], r["vals"], r["first"], r["expert"], r["n_i"]
    with ExitStack() as es:
        sb = lambda n, s, dt=F32: es.enter_context(nc.sbuf_tensor(f"ex_{n}", s, dt))
        wgu = sb("wgu", [P, 2, KT, 2 * HID])
        wd = sb("wd", [P, 2, 2, D])
        hot = sb("hot", [P, NT, P])
        slot = sb("slot", [P, 2, 4])
        miss = sb("miss", [P, 2])
        at_in = sb("at_in", [P, 2, 1], I32)
        at_out = sb("at_out", [P, 2, 1], I32)
        wt = sb("wt", [P, 2, 1])
        rows = sb("rows", [P, 2, D])
        rowsT = sb("rowsT", [P, 2, D])
        sig = sb("sig", [P, HID])
        hid = sb("hid", [P, HID])
        hidT = sb("hidT", [P, HID])
        res = sb("res", [P, 2, D])
        pt = lambda n, s: es.enter_context(nc.psum_tensor(f"ex_ps_{n}", s, F32))
        ps_i = pt("i", [P, BANK])
        ps_x = pt("x", [P, 2 * BANK])
        ps_gu = pt("gu", [P, BANK])
        ps_h = pt("h", [P, BANK])
        ps_y = pt("y", [P, 2 * BANK])
        names = ("gu0 gu1 dn0 dn1 hot_done slots copied missed idx_ready out_ready taken turned rowsT_done gu_done sig_done half_hid "
                 "hid_done hid_turned hidT_done y_done res_done out_free")
        with stage(nc, "experts", names, g["rows_sems"]) as (
                block, gu0, gu1, dn0, dn1, hot_done, slots, copied, missed, idx_ready, out_ready, taken, turned, rowsT_done, gu_done,
                sig_done, half_hid, hid_done, hid_turned, hidT_done, y_done, res_done, out_free):
            gu_in, dn_in = (gu0, gu1), (dn0, dn1)
            gathered, scattered = g["rows_sems"][0:2], g["rows_sems"][2:4]

            def count(eng):
                return eng.value_load(n_i[0:1, 2:3], min_val=N_EXP, max_val=N_EXP + MAX_EXTRA - 4)

            def expert_of(eng, b):
                return eng.value_load(expert[0:1, bass.ds(b, 1)], min_val=0, max_val=N_EXP - 1)

            def blocks(eng, body):
                body(0, 0)
                body(1, 1)
                with eng.Fori(2, count(eng), 2) as b0:
                    body(b0, 0)
                    body(b0 + 1, 1)

            def wait(eng, sem, value):
                if not (isinstance(value, int) and value == 0):
                    eng.wait_ge(sem, value)

            def seen(b, a, units=16):
                return (b - a) * (units // 2) + units

            @block.sync
            def _(sp):
                def body(b, a):
                    e = expert_of(sp, b)
                    if not isinstance(b, int):
                        sp.wait_ge(gu_done, b - 1)
                    for n, c in (("exp_w_gate", 0), ("exp_w_up", HID)):
                        sp.dma_start(wgu[:, a, :, c:c + HID], A[n][bass.ds(layer, 1), bass.ds(e, 1)]
                                     .rearrange("a e (k p) n -> p (a e k) n", p=P)).then_inc(gu_in[a], 16)
                    if not isinstance(b, int):
                        sp.wait_ge(y_done, b - 1)
                    sp.dma_start(wd[:, a, :, :], A["exp_w_down"][bass.ds(layer, 1), bass.ds(e, 1)]
                                 .rearrange("a e (k p) n -> p (a e k) n", p=P)).then_inc(dn_in[a], 16)

                blocks(sp, body)

            @block.gpsimd
            def _(pool):
                def gather(b, a):
                    pool.wait_ge(idx_ready, b + 1)
                    pool.sem_inc(taken, 1)
                    pool.indirect_dma_start(out=rows[:, a, :], out_offset=None, in_=h_dram[:, :],
                                            in_offset=bass.IndirectOffsetOnAxis(ap=at_in[:, a, :], axis=0)).then_inc(gathered[a], 16)

                def body(b, a):
                    pool.wait_ge(turned, b + 1)
                    gather(b + 2, a)
                    if not (isinstance(b, int) and b == 0):
                        pool.wait_ge(scattered[1 - a], seen(b - 1, 1 - a))
                        pool.sem_inc(out_free, 1)
                    pool.wait_ge(res_done, b + 1)
                    pool.sem_inc(taken, 1)
                    pool.indirect_dma_start(out=y_dram[:, :], out_offset=bass.IndirectOffsetOnAxis(ap=at_out[:, a, :], axis=0),
                                            in_=res[:, a, :], in_offset=None).then_inc(scattered[a], 16)

                gather(0, 0)
                gather(1, 1)
                blocks(pool, body)
                n = count(pool)
                pool.wait_ge(scattered[1], n * 8)
                for a in range(2):
                    pool.wait_ge(gathered[a], n * 8 + 16)
                pool.sem_inc(taken, 1)
                pool.dma_reset(range(gathered[0].num, scattered[1].num + 1))

            @block.vector
            def _(dve):
                v = nc.vector

                def find(b):
                    e = expert_of(dve, b)
                    wait(dve, slots, b)
                    for i in range(NT):
                        last = v.tensor_scalar(hot[:, i, :], cst[:, C_IOTA:C_IOTA + P], first[:, bass.ds(b, 1)],
                                               rank[:, i, bass.ds(e, 1)], ALU.add, ALU.is_equal)
                    last.then_inc(hot_done, 1)

                def place_in(b, a):
                    dve.wait_ge(slots, b + 1)
                    v.tensor_copy(slot[:, a, :], ps_i[:, 0:4]).then_inc(copied, 1)
                    dve.wait_ge(copied, b + 1)
                    if not isinstance(b, int):
                        dve.wait_ge(gathered[a], seen(b - 2, a))
                    v.tensor_copy(at_in[:, a, :], slot[:, a, 0:1]).then_inc(idx_ready, 1)

                def place_out(b, a):
                    if not (isinstance(b, int) and b < 2):
                        dve.wait_ge(out_free, b - 1)
                    v.tensor_copy(wt[:, a, :], slot[:, a, 2:3])
                    v.tensor_scalar(miss[:, a:a + 1], slot[:, a, 3:4], -1.0, 1.0, ALU.mult, ALU.add).then_inc(missed, 1)
                    dve.wait_ge(missed, b + 1)
                    v.scalar_tensor_tensor(at_out[:, a, :], miss[:, a:a + 1], cst[:, C_COL + 2:C_COL + 3], slot[:, a, 1:2],
                                           ALU.mult, ALU.add).then_inc(out_ready, 1)

                def body(b, a):
                    find(b + 2)
                    dve.wait_ge(sig_done, b + 1)
                    v.tensor_tensor(sig[:, :], sig[:, :], ps_gu[:, 0:HID], ALU.mult).then_inc(half_hid, 1)
                    dve.wait_ge(half_hid, b + 1)
                    v.tensor_tensor(hid[:, :], sig[:, :], ps_gu[:, HID:2 * HID], ALU.mult).then_inc(hid_done, 1)
                    place_in(b + 2, a)
                    place_out(b + 1, 1 - a)

                for b in range(2):
                    find(b)
                    place_in(b, b)
                place_out(0, 0)
                blocks(dve, body)

            @block.scalar
            def _(act):
                def turn(b, a):
                    act.wait_ge(turned, b + 1)
                    nc.scalar.activation(rowsT[:, a, :], ps_x[:, :], ACT.Copy).then_inc(rowsT_done, 1)

                def body(b, a):
                    act.wait_ge(gu_done, b + 1)
                    nc.scalar.activation(sig[:, :], ps_gu[:, 0:HID], ACT.Sigmoid).then_inc(sig_done, 1)
                    turn(b + 1, 1 - a)
                    act.wait_ge(hid_turned, b + 1)
                    nc.scalar.activation(hidT[:, :], ps_h[:, 0:HID], ACT.Copy).then_inc(hidT_done, 1)
                    act.wait_ge(y_done, b + 1)
                    act.wait_ge(out_ready, b + 1)
                    nc.scalar.activation(res[:, a, :], ps_y[:, :], ACT.Copy, scale=wt[:, a, :]).then_inc(res_done, 1)

                turn(0, 0)
                blocks(act, body)

            @block.tensor
            def _(pe):
                ident = cst[:, C_ID:C_ID + P]

                def slots_of(b):
                    e = expert_of(pe, b)
                    pe.wait_ge(hot_done, b + 1)
                    wait(pe, copied, b)
                    for i in range(NT):
                        last = nc.tensor.matmul(ps_i[:, 0:4], hot[:, i, :], vals[:, i, bass.ds(e * 4, 4)], start=(i == 0), stop=(i == NT - 1))
                    last.then_inc(slots, 1)

                def turn(b, a):
                    pe.wait_ge(gathered[a], seen(b, a))
                    wait(pe, rowsT_done, b)
                    for k in range(KT):
                        last = nc.tensor.transpose(ps_x[:, k * P:(k + 1) * P], rows[:, a, k * P:(k + 1) * P], ident)
                    last.then_inc(turned, 1)

                def body(b, a):
                    pe.wait_ge(gu_in[a], seen(b, a, 32))
                    pe.wait_ge(rowsT_done, b + 1)
                    wait(pe, hid_done, b)
                    for k in range(KT):
                        last = nc.tensor.matmul(ps_gu[:, :], rowsT[:, a, k * P:(k + 1) * P], wgu[:, a, k, :], start=(k == 0), stop=(k == KT - 1))
                    last.then_inc(gu_done, 1)
                    turn(b + 1, 1 - a)
                    slots_of(b + 2)
                    pe.wait_ge(hid_done, b + 1)
                    for m in range(2):
                        last = nc.tensor.transpose(ps_h[:, m * P:(m + 1) * P], hid[:, m * P:(m + 1) * P], ident)
                    last.then_inc(hid_turned, 1)
                    pe.wait_ge(hidT_done, b + 1)
                    pe.wait_ge(dn_in[a], seen(b, a))
                    wait(pe, res_done, b)
                    for h in range(2):
                        for m in range(2):
                            last = nc.tensor.matmul(ps_y[:, h * BANK:(h + 1) * BANK], hidT[:, m * P:(m + 1) * P],
                                                    wd[:, a, m, h * BANK:(h + 1) * BANK], start=(m == 0), stop=(m == 1))
                    last.then_inc(y_done, 1)

                slots_of(0)
                slots_of(1)
                turn(0, 0)
                blocks(pe, body)


def combine(nc, A, g, layer, y_dram, gate):
    x = g["x"]
    with ExitStack() as es:
        y = es.enter_context(nc.sbuf_tensor("cb_y", [P, 2, TOP_K, D], F32))
        tot = es.enter_context(nc.sbuf_tensor("cb_sum", [P, D], F32))
        with stage(nc, "combine", "in0 in1 summed own used") as (block, in0, in1, summed, own, used):
            arrived = (in0, in1)

            @block.sync
            def _(sp):
                for i in range(NT):
                    if i >= 2:
                        sp.wait_ge(summed, i - 1)
                    sp.dma_start(y[:, i % 2, :, :], y_dram[i * P * TOP_K:(i + 1) * P * TOP_K, :].rearrange("(t k) d -> t k d", k=TOP_K)
                                 ).then_inc(arrived[i % 2], 16)

            @block.vector
            def _(dve):
                o = Own(dve, own)
                for i in range(NT):
                    s = 0 if i < NTX else 1
                    dve.wait_ge(arrived[i % 2], 16 * (i // 2 + 1))
                    if i:
                        dve.wait_ge(used, i)
                    nc.vector.tensor_reduce(tot[:, :], y[:, i % 2, :, :].rearrange("p k d -> p d k"), AX.X, ALU.add).then_inc(summed, 1)
                    dve.wait_ge(summed, i + 1)
                    o.then(nc.vector.tensor_tensor(tot[:, :], tot[:, :], gate[:, s, :], ALU.mult))
                    nc.vector.tensor_tensor(x[:, i, :], x[:, i, :], tot[:, :], ALU.add).then_inc(used, 1)


def moe(nc, A, g, layer, h_dram, y_dram):
    with ExitStack() as es:
        sb = lambda n, s, dt=F32: es.enter_context(nc.sbuf_tensor(f"moe_{n}", s, dt))
        gate = sb("gate", [P, 2, D])
        r = {"rank": sb("rank", [P, NT, N_EXP]), "vals": sb("vals", [P, NT, N_EXP * 4]), "first": sb("first", [P, N_SLOT_TAB]),
             "expert": sb("expert", [1, N_SLOT_TAB], I32), "n_i": sb("n_i", [1, 4], I32)}
        with nc.sbuf_tensor("h2T", [P, KT, TOK], F32) as hT:
            norm_rows(nc, A, g, layer, 3, "norm2_g", hT, h_dram)
            routing(nc, A, g, layer, hT, r)
            shared_expert(nc, A, g, layer, hT, gate)
        routed_experts(nc, A, g, layer, r, h_dram, y_dram)
        combine(nc, A, g, layer, y_dram, gate)


_INS = ("x c ctx c_ctx w_mod b_mod norm1_g norm2_g w_in w_out gqa_q_gain gqa_k_gain win_q_gain win_k_gain win_sink "
        "conv_dw_w conv_dw_b conv_ln_g conv_ln_b conv_pw_w conv_pw_b hgrn_lb_logits hgrn_onorm_g router_w router_bias "
        "exp_w_gate exp_w_up exp_w_down sh_w_gate sh_w_up sh_w_down").split()


def kernel(**inputs):
    import concourse.bacc as bacc
    from concourse.bass_utils import run_bass_kernel_spmd

    nc = bacc.Bacc("TRN2", target_bir_lowering=False, num_devices=1)
    arrays = {f"in_{n}": np.ascontiguousarray(inputs[n]) for n in _INS}
    arrays["in_consts"] = shape_constants()
    A = {n[3:]: nc.dram_tensor(n, a.shape, mybir.dt.from_np(a.dtype), kind="ExternalInput").ap() for n, a in arrays.items()}
    out = nc.dram_tensor("out", (1, SEQ, D), F32, kind="ExternalOutput").ap()
    build(nc, A, out)
    got = run_bass_kernel_spmd(nc, [arrays], core_ids=[0])
    return got.results[0]["out"]
```

```python
import concourse.bass as bass
from concourse import mybir
from contextlib import ExitStack, contextmanager
import numpy as np

F32 = mybir.dt.float32
I32 = mybir.dt.int32
U32 = mybir.dt.uint32
ALU = mybir.AluOpType
ACT = mybir.ActivationFunctionType
AX = mybir.AxisListType

P = 128
D = 1024
KT = D // P
SEQ = 512
CTX = 256
TOK = SEQ + CTX
NT = TOK // P
NTX = SEQ // P
NTC = CTX // P
DEPTH = 2
GRID_W = 64
HEAD = 64
N_Q = 4
N_KV = 2
GROUP = 256
D_IN = 2816
SCALE = HEAD ** -0.5
CONV_W = 31
PAD = CONV_W // 2
CONV_SPAN = PAD + SEQ + PAD + CTX + PAD
CONV_OUT = SEQ + PAD + CTX
N_EXP = 64
TOP_K = 8
N_GRP = 8
PER_GRP = N_EXP // N_GRP
HID = 256
ROUTED_SCALE = 2.5
EPS = 1e-6
LEVELS = 7
NEG = -1e30
BANK = 512

C_ID = 0
C_SEL = C_ID + P
C_PREV = C_SEL + 2 * P
C_NEXT = C_PREV + P
TILES_A_MASK = 3
_blocks = [TILES_A_MASK * P >> lev for lev in range(LEVELS)]
C_LEV = [[C_NEXT + P + d * sum(_blocks) + sum(_blocks[:lev]) for lev in range(LEVELS)] for d in range(2)]
C_TRI = C_NEXT + P + 2 * sum(_blocks)
C_IOTA = C_TRI + P
C_COL = C_IOTA + P
C_LOW = C_COL + 16
C_COS = C_LOW + 64
C_SIN = C_COS + NTX * HEAD
C_ALL = C_SIN + NTX * HEAD


def shape_constants():
    c = np.zeros((P, C_ALL), np.float32)
    r = np.arange(P)
    c[:, C_ID:C_ID + P] = np.eye(P)
    for j in range(4):
        for s in range(2):
            c[32 * j + s, C_SEL + s * P:C_SEL + (s + 1) * P] = 1.0
    c[:, C_PREV:C_PREV + P] = np.where(r[None, :] >= r[:, None], 0.0, NEG)
    c[:, C_NEXT:C_NEXT + P] = np.where(r[None, :] <= r[:, None], 0.0, NEG)
    for lev in range(LEVELS):
        n = 1 << lev
        for d in range(2):
            block = (np.arange(_blocks[lev]) % (P // (2 * n)))[None, :]
            c[:, C_LEV[d][lev]:C_LEV[d][lev] + _blocks[lev]] = (r[:, None] // (2 * n) == block) & (r[:, None] % (2 * n) // n == d)
    c[:, C_TRI:C_TRI + P] = r[:, None] < r[None, :]
    c[:, C_IOTA:C_IOTA + P] = r[None, :]
    c[:, C_COL] = 1.0
    c[:, C_COL + 1] = r
    c[:, C_COL + 2] = TOK * TOP_K + r
    c[:, C_COL + 10:C_COL + 10 + DEPTH - 1] = 1.0
    k8 = np.arange(N_GRP)
    c[:, C_LOW:C_LOW + 64] = (k8[None, :] < k8[:, None]).reshape(1, 64)
    for i in range(NT):
        c[:, C_COL + 4 + i] = i * P + r
    freqs = HEAD // 4
    inv = np.power(10000.0, -np.arange(freqs, dtype=np.float32) / freqs).astype(np.float32)
    for i in range(NTX):
        t = i * P + r
        for ax, pos in enumerate((t // GRID_W, t % GRID_W)):
            ang = pos.astype(np.float32)[:, None] * inv[None, :]
            at = i * HEAD + ax * 2 * freqs
            c[:, C_COS + at:C_COS + at + freqs] = np.cos(ang)
            c[:, C_COS + at + freqs:C_COS + at + 2 * freqs] = np.cos(ang)
            c[:, C_SIN + at:C_SIN + at + freqs] = -np.sin(ang)
            c[:, C_SIN + at + freqs:C_SIN + at + 2 * freqs] = np.sin(ang)
    return c


@contextmanager
def stage(nc, name, sem_names, kept=()):
    sems = [nc.alloc_semaphore(name=f"{name}_{s}") for s in sem_names.split()]
    with nc.Block(name) as block:
        yield (block, *sems)
    for s in sems:
        nc.all_engine_barrier(sems_to_clear=s)
        nc.release_semaphore(s)
    for s in kept:
        nc.all_engine_barrier(sems_to_clear=s)


class Own:

    def __init__(self, eng, sem):
        self.eng, self.sem, self.n = eng, sem, 0

    def __call__(self, ins):
        ins.then_inc(self.sem, 1)
        self.n += 1
        return ins

    def settle(self):
        self.eng.wait_ge(self.sem, self.n)

    def then(self, ins):
        self(ins)
        self.settle()


def build(nc, A, out):
    with ExitStack() as es:
        def sb(name, shape, dt=F32, stack=es):
            return stack.enter_context(nc.sbuf_tensor(name, shape, dt))

        g = {}
        g["x"] = sb("x_res", [P, NT, D])
        g["cst"] = sb("cst", [P, C_ALL])
        g["cT"] = sb("cT", [P, KT, 2])
        g["lb"] = sb("lb", [P, DEPTH, 3, 4])
        g["mods"] = sb("mods", [P, 3, BANK])
        h_dram = nc.dram_tensor("h_rows", (TOK, D), F32).ap()
        y_dram = nc.dram_tensor("expert_rows", (TOK * TOP_K + P, D), F32).ap()
        g["rows_sems"] = [nc.alloc_semaphore(name=n) for n in ("gathered0", "gathered1", "scattered0", "scattered1")]
        prologue(nc, A, g)
        with nc.Fori(0, DEPTH) as layer:
            modulation(nc, A, g, layer)
            with ExitStack() as mix:
                g["pt"] = sb("p_tok", [P, NT, 1536], stack=mix)
                g["pf"] = sb("p_feat", [P, 10, TOK], stack=mix)
                g["cum"] = sb("log_gate_sums", [P, 2, 2, NT, P + 1], stack=mix)
                with nc.sbuf_tensor("hT", [P, KT, TOK], F32) as hT:
                    norm_rows(nc, A, g, layer, 0, "norm1_g", hT, None)
                    projections(nc, A, g, layer, hT)
                g["yT"] = sb("yT", [P, KT, TOK], stack=mix)
                attention(nc, A, g, layer, 0)
                attention(nc, A, g, layer, 1)
                convolution(nc, A, g, layer)
                recurrence(nc, A, g, layer)
                out_projection(nc, A, g, layer)
            moe(nc, A, g, layer, h_dram, y_dram)
        with stage(nc, "store", "stored") as (block, stored):
            @block.sync
            def _(sp):
                sp.dma_start(out[0].rearrange("(t p) d -> p t d", p=P), g["x"][:, 0:NTX, :]).then_inc(stored, 16)
                sp.wait_ge(stored, 16)


def prologue(nc, A, g):
    x, cst, cT, lb = g["x"], g["cst"], g["cT"], g["lb"]
    with ExitStack() as es:
        craw = es.enter_context(nc.sbuf_tensor("craw", [P, KT, 2], F32))
        csig = es.enter_context(nc.sbuf_tensor("csig", [P, KT, 2], F32))
        lg = es.enter_context(nc.sbuf_tensor("lg", [P, DEPTH, 4], F32))
        mx = es.enter_context(nc.sbuf_tensor("lg_max", [P, 4], F32))
        den = es.enter_context(nc.sbuf_tensor("lg_den", [P, 4], F32))
        with stage(nc, "prologue", "loaded streams acted own ready") as (block, loaded, streams, acted, own, ready):
            @block.sync
            def _(sp):
                sp.dma_start(craw[:, :, 0], A["c"][0].rearrange("(k p) -> p k", p=P),
                             allow_slow_non_contiguous=True).then_inc(loaded, 16)
                sp.dma_start(craw[:, :, 1], A["c_ctx"].rearrange("(k p) -> p k", p=P),
                             allow_slow_non_contiguous=True).then_inc(loaded, 16)
                for l in range(DEPTH):
                    for d in range(2):
                        sp.dma_start(lg[:, l, 2 * d:2 * d + 2],
                                     A["hgrn_lb_logits"][d, l].rearrange("(g p) -> p g", p=P),
                                     allow_slow_non_contiguous=True).then_inc(loaded, 16)
                sp.dma_start(cst[:, :], A["consts"]).then_inc(streams, 16)
                sp.dma_start(x[:, 0:NTX, :], A["x"][0].rearrange("(t p) d -> p t d", p=P)).then_inc(streams, 16)
                sp.dma_start(x[:, NTX:NT, :], A["ctx"][0].rearrange("(t p) d -> p t d", p=P)).then_inc(streams, 16)
                sp.wait_ge(streams, 48)

            @block.scalar
            def _(act):
                act.wait_ge(loaded, 96)
                nc.scalar.activation(csig[:, :, :], craw[:, :, :], ACT.Sigmoid).then_inc(acted, 1)
                act.wait_ge(ready, 1)
                nc.scalar.activation(lg[:, :, :], lg[:, :, :], ACT.Exp).then_inc(acted, 1)
                act.wait_ge(ready, 2)
                nc.scalar.activation(lb[:, :, 1, :], lb[:, :, 1, :], ACT.Ln).then_inc(acted, 1)

            @block.vector
            def _(dve):
                o = Own(dve, own)
                dve.wait_ge(loaded, 96)
                o.then(nc.vector.tensor_tensor(mx[:, :], lg[:, 0, :], lg[:, 1, :], ALU.max))
                o(nc.vector.tensor_tensor(lg[:, 0, :], lg[:, 0, :], mx[:, :], ALU.subtract))
                nc.vector.tensor_tensor(lg[:, 1, :], lg[:, 1, :], mx[:, :], ALU.subtract).then_inc(ready, 1)
                dve.wait_ge(acted, 2)
                o(nc.vector.tensor_tensor(cT[:, :, :], craw[:, :, :], csig[:, :, :], ALU.mult))
                o.then(nc.vector.tensor_tensor(den[:, :], lg[:, 0, :], lg[:, 1, :], ALU.add))
                o.then(nc.vector.reciprocal(den[:, :], den[:, :]))
                o(nc.vector.tensor_tensor(lg[:, 0, :], lg[:, 0, :], den[:, :], ALU.mult))
                o.then(nc.vector.tensor_tensor(lg[:, 1, :], lg[:, 1, :], den[:, :], ALU.mult))
                o(nc.vector.memset(lb[:, 0, 0, :], 0.0))
                o.then(nc.vector.tensor_tensor(lb[:, 1, 0, :], lg[:, 0, :], lg[:, 1, :], ALU.add))
                o.then(nc.vector.tensor_tensor(lb[:, 1, 0, :], lb[:, 1, 0, :], lg[:, 0, :], ALU.subtract))
                o(nc.vector.tensor_scalar(lb[:, :, 2, :], lb[:, :, 0, :], -1.0, 1.0, ALU.mult, ALU.add))
                nc.vector.tensor_scalar(lb[:, :, 1, :], lb[:, :, 0, :], 1e-18, None, ALU.max).then_inc(ready, 1)
                o.then(nc.vector.tensor_scalar(lg[:, :, :], lb[:, :, 0, :], 0.0, NEG, ALU.is_equal, ALU.mult))
                dve.wait_ge(acted, 3)
                nc.vector.tensor_tensor(lb[:, :, 1, :], lb[:, :, 1, :], lg[:, :, :], ALU.add).then_inc(ready, 1)


def modulation(nc, A, g, layer):
    cT, cst, mods = g["cT"], g["cst"], g["mods"]
    NBUF, CH = 3, 12
    with ExitStack() as es:
        w = es.enter_context(nc.sbuf_tensor("w_mod_t", [P, NBUF, 6 * D], F32))
        b = es.enter_context(nc.sbuf_tensor("b_mod_t", [1, 6 * D], F32))
        one = es.enter_context(nc.sbuf_tensor("one_row", [1, 2], F32))
        ps = es.enter_context(nc.psum_tensor("mod_ps", [P, 3, BANK], F32))
        with stage(nc, "mod", "w0 w1 w2 bias w_used ones summed kept") as (block, w0, w1, w2, bias, w_used, ones, summed, kept):
            w_in = (w0, w1, w2)

            @block.sync
            def _(sp):
                sp.dma_start(b[:, :], A["b_mod"][bass.ds(layer, 1), :]).then_inc(bias, 16)
                for k in range(KT):
                    if k >= NBUF:
                        sp.wait_ge(w_used, k - NBUF + 1)
                    sp.dma_start(w[:, k % NBUF, :],
                                 A["w_mod"][bass.ds(layer, 1), k * P:(k + 1) * P, :].rearrange("a p n -> (a p) n")
                                 ).then_inc(w_in[k % NBUF], 16)

            @block.vector
            def _(dve):
                nc.vector.memset(one[:, :], 1.0).then_inc(ones, 1)
                dve.wait_ge(summed, 1)
                for j in range(4):
                    nc.vector.tensor_copy(mods[32 * j:32 * j + 2, :, :], ps[32 * j:32 * j + 2, :, :]).then_inc(kept, 1)

            @block.tensor
            def _(pe):
                for k in range(KT):
                    pe.wait_ge(w_in[k % NBUF], 16 * (k // NBUF + 1))
                    for c in range(CH):
                        last = nc.tensor.matmul(ps[32 * (c % 4):32 * (c % 4) + 2, c // 4, :], cT[:, k, :],
                                                w[:, k % NBUF, c * BANK:(c + 1) * BANK], start=(k == 0), stop=False)
                    last.then_inc(w_used, 1)
                pe.wait_ge(bias, 16)
                pe.wait_ge(ones, 1)
                for c in range(CH):
                    last = nc.tensor.matmul(ps[32 * (c % 4):32 * (c % 4) + 2, c // 4, :], one[0:1, :],
                                            b[0:1, c * BANK:(c + 1) * BANK], start=False, stop=True)
                last.then_inc(summed, 1)


def broadcast_row(nc, g, ps, kind, stream):
    cst, mods = g["cst"], g["mods"]
    for h in range(2):
        c = 2 * kind + h
        j = 32 * (c % 4)
        last = nc.tensor.matmul(ps[:, h * BANK:(h + 1) * BANK], cst[j:j + 2, C_SEL + stream * P:C_SEL + (stream + 1) * P],
                                mods[j:j + 2, c // 4, :], start=True, stop=True)
    return last


def norm_rows(nc, A, g, layer, kind, gain, hT, h_dram):
    x, cst = g["x"], g["cst"]
    with ExitStack() as es:
        gr = es.enter_context(nc.sbuf_tensor(f"gain_row{kind}", [P, D], F32))
        mul = es.enter_context(nc.sbuf_tensor(f"mul_row{kind}", [P, 2, D], F32))
        add = es.enter_context(nc.sbuf_tensor(f"add_row{kind}", [P, 2, D], F32))
        h = es.enter_context(nc.sbuf_tensor(f"h_tok{kind}", [P, 2, D], F32))
        sq = es.enter_context(nc.sbuf_tensor(f"h_sq{kind}", [P, D], F32))
        ss = es.enter_context(nc.sbuf_tensor(f"h_ss{kind}", [P, NT], F32))
        rs = es.enter_context(nc.sbuf_tensor(f"h_rstd{kind}", [P, NT], F32))
        pr = es.enter_context(nc.psum_tensor(f"row_ps{kind}", [P, 2, 2 * BANK], F32))
        pt = es.enter_context(nc.psum_tensor(f"hT_ps{kind}", [P, 2, 2 * BANK], F32))
        names = "gain_in spread rows own squared varied rooted h_ready turned kept stored0 stored1"
        with stage(nc, f"norm{kind}", names) as (block, gain_in, spread, rows, own, squared, varied, rooted, h_ready,
                                                 turned, kept, stored0, stored1):
            stored = (stored0, stored1)

            @block.sync
            def _(sp):
                sp.dma_start(gr[:, :], A[gain][bass.ds(layer, 1), :].broadcast_to([P, D])).then_inc(gain_in, 16)
                if h_dram is not None:
                    for i in range(NT):
                        sp.wait_ge(h_ready, i + 1)
                        sp.dma_start(h_dram[i * P:(i + 1) * P, :], h[:, i % 2, :]).then_inc(stored[i % 2], 16)
                    for a in range(2):
                        sp.wait_ge(stored[a], 16 * NT // 2)

            @block.tensor
            def _(pe):
                for n, (kd, s) in enumerate(((kind + 1, 0), (kind + 1, 1), (kind, 0), (kind, 1))):
                    if n >= 2:
                        pe.wait_ge(rows, n - 1)
                    broadcast_row(nc, g, pr[:, n % 2, :], kd, s).then_inc(spread, 1)
                for i in range(NT):
                    pe.wait_ge(h_ready, i + 1)
                    if i >= 2:
                        pe.wait_ge(kept, i - 1)
                    for k in range(KT):
                        last = nc.tensor.transpose(pt[:, i % 2, k * P:(k + 1) * P], h[:, i % 2, k * P:(k + 1) * P],
                                                   cst[:, C_ID:C_ID + P])
                    last.then_inc(turned, 1)

            @block.scalar
            def _(act):
                for i in range(NT):
                    if i:
                        act.wait_ge(squared, i)
                    nc.scalar.activation(sq[:, :], x[:, i, :], ACT.Square, accum_out=ss[:, i:i + 1]).then_inc(squared, 1)
                act.wait_ge(varied, 1)
                nc.scalar.activation(rs[:, :], rs[:, :], ACT.Sqrt).then_inc(rooted, 1)
                for i in range(NT):
                    act.wait_ge(turned, i + 1)
                    nc.scalar.activation(hT[:, :, i * P:(i + 1) * P],
                                         pt[:, i % 2, :].rearrange("p (k t) -> p k t", t=P), ACT.Copy).then_inc(kept, 1)

            @block.vector
            def _(dve):
                o = Own(dve, own)
                dve.wait_ge(gain_in, 16)
                for s in range(2):
                    dve.wait_ge(spread, s + 1)
                    nc.vector.scalar_tensor_tensor(mul[:, s, :], pr[:, s, :], 1.0, gr[:, :], ALU.add, ALU.mult).then_inc(rows, 1)
                for s in range(2):
                    dve.wait_ge(spread, s + 3)
                    nc.vector.tensor_copy(add[:, s, :], pr[:, s, :]).then_inc(rows, 1)
                dve.wait_ge(squared, NT)
                nc.vector.tensor_scalar(rs[:, :], ss[:, :], 1.0 / D, EPS, ALU.mult, ALU.add).then_inc(varied, 1)
                dve.wait_ge(rooted, 1)
                dve.wait_ge(rows, 4)
                o.then(nc.vector.reciprocal(rs[:, :], rs[:, :]))
                for i in range(NT):
                    s = 0 if i < NTX else 1
                    if i >= 2:
                        dve.wait_ge(turned, i - 1)
                        if h_dram is not None:
                            dve.wait_ge(stored[i % 2], 16 * (i // 2))
                    o.then(nc.vector.scalar_tensor_tensor(h[:, i % 2, :], x[:, i, :], rs[:, i:i + 1], mul[:, s, :], ALU.mult, ALU.mult))
                    nc.vector.tensor_tensor(h[:, i % 2, :], h[:, i % 2, :], add[:, s, :], ALU.add).then_inc(h_ready, 1)


def projections(nc, A, g, layer, hT):
    pt, pf = g["pt"], g["pf"]
    CW = 256
    CHUNKS = ([(1024 + CW * j, "f", 2 * j) for j in range(2)] + [(2048 + CW * j, "f", 6 + 2 * j) for j in range(2)]
              + [(1536, "f", 4)] + [(CW * j, "t", CW * j) for j in range(4)] + [(1792, "t", 1024), (2560, "t", 1280)])
    jobs = []
    for c, (c0, kind, at) in enumerate(CHUNKS):
        if kind == "t":
            jobs += [(c, kind, 0, CW, pt[:, i, at:at + CW], i * P) for i in range(NT)]
        else:
            jobs += [(c, kind, P * j, tw, pf[:, at + j, t0:t0 + tw], t0) for j in range(2) for t0, tw in ((0, SEQ), (SEQ, CTX))]
    CONV_IN, GATES_IN = 8, 16
    GATE_STEPS = [31, 33, 35, 38, 40, 42]
    with ExitStack() as es:
        sb = lambda n, s: es.enter_context(nc.sbuf_tensor(f"proj_{n}", s, F32))
        w = sb("w", [P, 2, KT, CW])
        scratch = [sb(n, [P, 2, TOK]) for n in ("e1", "e2", "e3", "e4")]
        lbl = sb("lbl", [P, 3, 4])
        hp = sb("hp", [P, 2, CONV_SPAN])
        dw = sb("dw", [P, 2, CONV_W])
        dwb = sb("dwb", [P, 2])
        ps = es.enter_context(nc.psum_tensor("p_ps", [P, 8, BANK], F32))
        names = "w0 w1 w_used done kept taps_in gated own own_a exp_arg first_ln diff lse_ln k_arg k_exp"
        with stage(nc, "proj", names) as (block, w0, w1, w_used, done, kept, taps_in, gated, own, own_a, exp_arg, first_ln, diff,
                                          lse_ln, k_arg, k_exp):
            w_in = (w0, w1)

            @block.sync
            def _(sp):
                for c, (c0, _, _) in enumerate(CHUNKS):
                    if c >= 2:
                        sp.wait_ge(w_used, c - 1)
                    sp.dma_start(w[:, c % 2, :, :], A["w_in"][bass.ds(layer, 1), :, c0:c0 + CW].rearrange("a (k p) n -> p (a k) n", p=P)
                                 ).then_inc(w_in[c % 2], 16)
                    if c == 1:
                        for h in range(2):
                            sp.dma_start(dw[:, h, :], A["conv_dw_w"][bass.ds(layer, 1), :, h * P:(h + 1) * P].rearrange("a k p -> p (a k)"),
                                         allow_slow_non_contiguous=True).then_inc(taps_in, 16)
                        sp.dma_start(dwb[:, :], A["conv_dw_b"][bass.ds(layer, 1), :].rearrange("a (c p) -> p (a c)", p=P),
                                     allow_slow_non_contiguous=True).then_inc(taps_in, 16)

            @block.tensor
            def _(pe):
                for n, (c, kind, col, width, dst, t0) in enumerate(jobs):
                    if n == 0 or jobs[n - 1][0] != c:
                        pe.wait_ge(w_in[c % 2], 16 * (c // 2 + 1))
                    if n >= 8:
                        pe.wait_ge(kept, n - 7)
                    for k in range(KT):
                        if kind == "t":
                            last = nc.tensor.matmul(ps[:, n % 8, 0:width], hT[:, k, t0:t0 + P], w[:, c % 2, k, :], start=(k == 0), stop=(k == KT - 1))
                        else:
                            last = nc.tensor.matmul(ps[:, n % 8, 0:width], w[:, c % 2, k, col:col + P], hT[:, k, t0:t0 + width],
                                                    start=(k == 0), stop=(k == KT - 1))
                    last.then_inc(done, 1)
                    if n + 1 == len(jobs) or jobs[n + 1][0] != c:
                        pe.wait_ge(done, n + 1)
                        pe.sem_inc(w_used, 1)

            @block.scalar
            def _(act):
                for n, job in enumerate(jobs):
                    act.wait_ge(done, n + 1)
                    nc.scalar.activation(job[4], ps[:, n % 8, 0:job[3]], ACT.Copy).then_inc(kept, 1)
                    if n + 1 == CONV_IN:
                        act.wait_ge(kept, CONV_IN)
                        nc.scalar.activation(pf[:, 2:4, :], pf[:, 2:4, :], ACT.Sigmoid).then_inc(gated, 1)
                    if n in GATE_STEPS:
                        gates_scalar(nc, act, pf, scratch, GATE_STEPS.index(n), (own_a, exp_arg, first_ln, diff, lse_ln, k_arg, k_exp))

            @block.vector
            def _(dve):
                o = Own(dve, own)
                depthwise(nc, dve, o, pf, hp, dw, dwb, (gated, taps_in))
                dve.wait_ge(kept, GATES_IN)
                gates_vector(nc, dve, o, layer, g["lb"], lbl, pf, g["cst"], g["cum"], scratch, (exp_arg, first_ln, diff, lse_ln, k_arg, k_exp))


def attention(nc, A, g, layer, win):
    pt, cst, yT = g["pt"], g["cst"], g["yT"]
    name = ("glob", "win")[win]
    qg, kg = (("gqa_q_gain", "gqa_k_gain"), ("win_q_gain", "win_k_gain"))[win]
    c0 = 512 * win
    QK = (N_Q + N_KV) * HEAD
    NH = N_Q + N_KV
    qk = pt[:, :, c0:c0 + QK]

    def vals(j, kv):
        return pt[:, j, c0 + QK + kv * HEAD:c0 + QK + (kv + 1) * HEAD]

    units = []
    for i in range(NT):
        if i >= NTX:
            keys = list(range(NTX, NT))
        elif win:
            keys = list(range(max(0, i - 1), min(NTX, i + 2))) + list(range(NTX, NT))
        else:
            keys = list(range(NT))
        for h in (0, 2, 1, 3):
            units.append((i, h, keys))
    NU = len(units)

    def runs(keys):
        out = []
        for n, j in enumerate(keys):
            if out and out[-1][1] + out[-1][2] == j and (n * P) % BANK:
                out[-1][2] += 1
            else:
                out.append([n * P, j, 1])
        return out

    with ExitStack() as es:
        sb = lambda n, s: es.enter_context(nc.sbuf_tensor(f"{name}_{n}", s, F32))
        tmp = sb("tmp", [P, NT, QK])
        swp = sb("swp", [P, NTX, QK])
        gain = sb("gain", [P, NH, HEAD])
        rs = sb("rs", [P, NT * NH])
        qT = sb("qT", [P, 2, TOK])
        kT = sb("kT", [P, TOK])
        prob = sb("prob", [P, 2, NT, P])
        probT = sb("probT", [P, 2, NT, P])
        o_tok = sb("o", [P, 2, GROUP])
        top = sb("top", [P, NU])
        neg = sb("neg", [P, NU])
        den = sb("den", [P, NU])
        snk = sb("snk", [P, N_Q])
        esnk = sb("esnk", [P, NU])
        ps_s = es.enter_context(nc.psum_tensor(f"{name}_ps_s", [P, 2, 2 * BANK], F32))
        ps_t = es.enter_context(nc.psum_tensor(f"{name}_ps_t", [P, 2 * BANK], F32))
        ps_o = es.enter_context(nc.psum_tensor(f"{name}_ps_o", [P, 2, BANK], F32))
        names = ("gains varied rooted normed turned kept own own_a scored topped exped spread spread_kept "
                 "mixed scaled back back_kept")
        with stage(nc, name, names) as (block, gains, varied, rooted, normed, turned, kept, own, own_a, scored, topped,
                                        exped, spread, spread_kept, mixed, scaled, back, back_kept):
            @block.sync
            def _(sp):
                for h in range(NH):
                    sp.dma_start(gain[:, h, :], A[qg if h < N_Q else kg][bass.ds(layer, 1), :].broadcast_to([P, HEAD])
                                 ).then_inc(gains, 16)
                if win:
                    sp.dma_start(snk[:, :], A["win_sink"][bass.ds(layer, 1), :].broadcast_to([P, N_Q])).then_inc(gains, 16)

            @block.vector
            def _(dve):
                o = Own(dve, own)
                heads = lambda ap: ap.rearrange("p t (h d) -> p t h d", d=HEAD)
                o.then(nc.vector.tensor_tensor(tmp[:, :, :], qk, qk, ALU.mult))
                o.then(nc.vector.tensor_reduce(rs[:, :], tmp[:, :, :].rearrange("p t (h d) -> p (t h) d", d=HEAD), AX.X, ALU.add))
                nc.vector.tensor_scalar(rs[:, :], rs[:, :], 1.0 / HEAD, EPS, ALU.mult, ALU.add).then_inc(varied, 1)
                dve.wait_ge(rooted, 1)
                o.then(nc.vector.reciprocal(rs[:, :], rs[:, :]))
                by_head = rs[:, :].rearrange("p (t h o) -> p t h o", h=NH, o=1)
                for b in range(3):
                    pick = slice(b, N_Q, 2) if b < 2 else slice(N_Q, NH)
                    o(nc.vector.tensor_tensor(heads(tmp[:, :, :])[:, :, 2 * b:2 * b + 2, :], heads(qk)[:, :, pick, :],
                                              by_head[:, :, pick, :].broadcast_to([P, NT, 2, HEAD]), ALU.mult))
                o.settle()
                dve.wait_ge(gains, 16 * (NH + win))
                o.then(nc.vector.tensor_tensor(heads(tmp[:, :, :]), heads(tmp[:, :, :]),
                                               gain[:, :, :].rearrange("p (o h) d -> p o h d", o=1).broadcast_to([P, NT, NH, HEAD]), ALU.mult))
                half = HEAD // 4
                for i in range(NTX):
                    part = lambda ap, a: ap.rearrange("p (h x a f) -> p h x a f", x=2, a=2, f=half)[:, :, :, a, :]
                    sin = cst[:, C_SIN + i * HEAD:C_SIN + (i + 1) * HEAD].rearrange("p (o x a f) -> p o x a f", o=1, x=2, a=2)
                    for a in range(2):
                        o(nc.vector.tensor_tensor(part(swp[:, i, :], a), part(tmp[:, i, :], 1 - a),
                                                  sin[:, :, :, a, :].broadcast_to([P, NH, 2, half]), ALU.mult))
                o.settle()
                cos = cst[:, C_COS:C_COS + NTX * HEAD].rearrange("p (t o d) -> p t o d", t=NTX, o=1).broadcast_to([P, NTX, NH, HEAD])
                o.then(nc.vector.tensor_tensor(heads(tmp[:, 0:NTX, :]), heads(tmp[:, 0:NTX, :]), cos, ALU.mult))
                nc.vector.tensor_tensor(tmp[:, 0:NTX, :], tmp[:, 0:NTX, :], swp[:, :, :], ALU.add).then_inc(normed, 1)
                for n in range(NU + 2):
                    if n < NU:
                        i, h, keys = units[n]
                        w = len(keys) * P
                        dve.wait_ge(scored, n + 1)
                        o.then(nc.vector.tensor_reduce(top[:, n:n + 1], ps_s[:, n % 2, 0:w], AX.X, ALU.max))
                        if win:
                            o.then(nc.vector.scalar_tensor_tensor(top[:, n:n + 1], top[:, n:n + 1], SCALE, snk[:, h:h + 1], ALU.mult, ALU.max))
                            nc.vector.tensor_scalar(neg[:, n:n + 1], top[:, n:n + 1], -1.0, None, ALU.mult).then_inc(topped, 1)
                        else:
                            nc.vector.tensor_scalar(neg[:, n:n + 1], top[:, n:n + 1], -SCALE, None, ALU.mult).then_inc(topped, 1)
                    if n >= 2:
                        m = n - 2
                        i, h, keys = units[m]
                        if win:
                            dve.wait_ge(exped, 2 * (m + 1))
                            o.then(nc.vector.tensor_tensor(den[:, m:m + 1], den[:, m:m + 1], esnk[:, m:m + 1], ALU.add))
                        else:
                            dve.wait_ge(exped, m + 1)
                        o.then(nc.vector.reciprocal(den[:, m:m + 1], den[:, m:m + 1]))
                        dve.wait_ge(mixed, m + 1)
                        if m >= 8 and m % 4 == 0:
                            dve.wait_ge(back, m // 4 - 1)
                        nc.vector.tensor_scalar(o_tok[:, (m // 4) % 2, h * HEAD:(h + 1) * HEAD], ps_o[:, m % 2, 0:HEAD],
                                                den[:, m:m + 1], None, ALU.mult).then_inc(scaled, 1)

            @block.scalar
            def _(act):
                act.wait_ge(varied, 1)
                nc.scalar.activation(rs[:, :], rs[:, :], ACT.Sqrt).then_inc(rooted, 1)
                for b in range(6):
                    act.wait_ge(turned, b + 1)
                    t0, tw = ((0, SEQ), (SEQ, CTX))[b // 3]
                    dst = (qT[:, 0, t0:t0 + tw], qT[:, 1, t0:t0 + tw], kT[:, t0:t0 + tw])[b % 3]
                    nc.scalar.activation(dst, ps_s[:, b % 2, 0:tw], ACT.Copy).then_inc(kept, 1)

                def turned_back(i):
                    act.wait_ge(back, i + 1)
                    nc.scalar.activation(yT[:, 4 * win:4 * win + 2, i * P:(i + 1) * P],
                                         ps_o[:, 0, 128:128 + 2 * P].rearrange("p (a b) -> p a b", b=P), ACT.Copy).then_inc(back_kept, 1)

                for n in range(NU + 1):
                    if n < NU:
                        i, h, keys = units[n]
                        act.wait_ge(topped, n + 1)
                        if n >= 2:
                            act.wait_ge(spread, n - 1)
                        nc.scalar.activation(prob[:, n % 2, 0:len(keys), :].rearrange("p a b -> p (a b)"), ps_s[:, n % 2, 0:len(keys) * P],
                                             ACT.Exp, bias=neg[:, n:n + 1], scale=SCALE, accum_out=den[:, n:n + 1]).then_inc(exped, 1)
                        if win:
                            nc.scalar.activation(esnk[:, n:n + 1], snk[:, h:h + 1], ACT.Exp, bias=neg[:, n:n + 1]).then_inc(exped, 1)
                    if n >= 1:
                        m = n - 1
                        nk = len(units[m][2])
                        act.wait_ge(spread, m + 1)
                        if m >= 2:
                            act.wait_ge(mixed, m - 1)
                        nc.scalar.activation(probT[:, m % 2, 0:nk, :].rearrange("p a b -> p (a b)"), ps_t[:, 0:nk * P], ACT.Copy).then_inc(spread_kept, 1)
                        if m % N_Q == 0 and m:
                            turned_back(m // N_Q - 1)
                turned_back(NT - 1)

            @block.tensor
            def _(pe):
                ident = cst[:, C_ID:C_ID + P]
                pe.wait_ge(normed, 1)
                for b in range(6):
                    if b >= 2:
                        pe.wait_ge(kept, b - 1)
                    tiles = (range(NTX), range(NTX, NT))[b // 3]
                    for n, i in enumerate(tiles):
                        src = tmp[:, i, (b % 3) * P:(b % 3 + 1) * P]
                        last = nc.tensor.transpose(ps_s[:, b % 2, n * P:(n + 1) * P], src, ident)
                    last.then_inc(turned, 1)
                pe.wait_ge(kept, 6)

                def scores(n):
                    i, h, keys = units[n]
                    kv, pair = h // 2, h % 2
                    if n >= 2:
                        pe.wait_ge(exped, (1 + win) * (n - 1))
                    for c, j, m in runs(keys):
                        masked = [t for t in range(j, j + m) if win and i < NTX and t < NTX and abs(t - i) == 1]
                        last = nc.tensor.matmul(ps_s[:, n % 2, c:c + m * P], qT[64 * kv:64 * kv + 64, pair, i * P:(i + 1) * P],
                                                kT[64 * kv:64 * kv + 64, j * P:(j + m) * P], start=True, stop=True)
                        for t in masked:
                            cm = C_PREV if t < i else C_NEXT
                            cc = c + (t - j) * P
                            last = nc.tensor.matmul(ps_s[:, n % 2, cc:cc + P], ident, cst[:, cm:cm + P], start=False,
                                                    stop=t == masked[-1], skip_group_check=True)
                    last.then_inc(scored, 1)

                def turn_back(i):
                    pe.wait_ge(scaled, 4 * (i + 1))
                    if i:
                        pe.wait_ge(back_kept, i)
                    for a in range(2):
                        last = nc.tensor.transpose(ps_o[:, 0, 128 + a * P:128 + (a + 1) * P], o_tok[:, i % 2, a * P:(a + 1) * P], ident)
                    last.then_inc(back, 1)

                for n in range(NU + 2):
                    if n < NU:
                        scores(n)
                    if 1 <= n <= NU:
                        m = n - 1
                        nk = len(units[m][2])
                        pe.wait_ge(exped, (1 + win) * m + 1)
                        if m:
                            pe.wait_ge(spread_kept, m)
                        for a in range(nk):
                            last = nc.tensor.transpose(ps_t[:, a * P:(a + 1) * P], prob[:, m % 2, a, :], ident)
                        last.then_inc(spread, 1)
                    if n >= 2:
                        m = n - 2
                        i, h, keys = units[m]
                        pe.wait_ge(spread_kept, m + 1)
                        if m >= 2:
                            pe.wait_ge(scaled, m - 1)
                        if m % 2 == 0 and m >= 4:
                            if m % 4 == 0:
                                turn_back(m // 4 - 1)
                                pe.wait_ge(back_kept, m // 4)
                        for a, j in enumerate(keys):
                            last = nc.tensor.matmul(ps_o[:, m % 2, 0:HEAD], probT[:, m % 2, a, :], vals(j, h // 2),
                                                    start=(a == 0), stop=(a == len(keys) - 1))
                        last.then_inc(mixed, 1)
                turn_back(NT - 1)


def convolved_rows(pf):
    return pf[:, 0:4, :].rearrange("p a t -> p (a t)")[:, 0:2 * CONV_OUT].rearrange("p (a t) -> p a t", a=2)


def depthwise(nc, dve, o, pf, hp, dw, dwb, sems):
    gated, taps_in = sems
    acc, L = convolved_rows(pf), CONV_OUT
    o.then(nc.vector.memset(hp[:, :, :], 0.0))
    dve.wait_ge(gated, 1)
    for (a, w), t0 in zip(((0, SEQ), (SEQ + PAD, CTX)), (0, SEQ)):
        o(nc.vector.tensor_tensor(hp[:, :, PAD + a:PAD + a + w], pf[:, 0:2, t0:t0 + w], pf[:, 2:4, t0:t0 + w], ALU.mult))
    o.settle()
    dve.wait_ge(taps_in, 16 * 3)
    for c in range(2):
        o(nc.vector.tensor_scalar(acc[:, c, :], hp[:, c, 0:L], dw[:, c, 0:1], dwb[:, c:c + 1], ALU.mult, ALU.add))
    for k in range(1, CONV_W):
        for c in range(2):
            dve.wait_ge(o.sem, o.n - 1)
            o(nc.vector.scalar_tensor_tensor(acc[:, c, :], hp[:, c, k:k + L], dw[:, c, k:k + 1], acc[:, c, :], ALU.mult, ALU.add))
    o.settle()


def convolution(nc, A, g, layer):
    pf, cst, yT = g["pf"], g["cst"], g["yT"]
    acc = convolved_rows(pf)
    with ExitStack() as es:
        sb = lambda n, s: es.enter_context(nc.sbuf_tensor(f"conv_{n}", s, F32))
        tok = sb("tok", [P, NT, GROUP])
        sq = sb("sq", [P, NT, GROUP])
        st = sb("st", [P, 3, NT])
        col = sb("col", [P, 3, 2])
        pw = sb("pw", [P, 2, GROUP])
        act_in = sb("lin", [P, 2, TOK])
        sil = sb("sil", [P, 2, TOK])
        ps = es.enter_context(nc.psum_tensor("conv_ps", [P, 4, 2 * BANK], F32))
        names = "loaded own turned tok_kept varied rooted normed back sig_done lin_done silued done kept"
        with stage(nc, "conv", names) as (block, loaded, own, turned, tok_kept, varied, rooted,
                                          normed, back, sig_done, lin_done, silued, done, kept):
            @block.sync
            def _(sp):
                one = lambda n: A[n][bass.ds(layer, 1), :].rearrange("a (c p) -> p (a c)", p=P)
                for n, v in enumerate(("conv_ln_g", "conv_ln_b", "conv_pw_b")):
                    sp.dma_start(col[:, n, :], one(v), allow_slow_non_contiguous=True).then_inc(loaded, 16)
                sp.dma_start(pw[:, :, :], A["conv_pw_w"][bass.ds(layer, 1)].rearrange("a (c p) n -> p (a c) n", p=P)).then_inc(loaded, 16)

            @block.scalar
            def _(act):
                for i in range(NT):
                    act.wait_ge(turned, i + 1)
                    nc.scalar.activation(tok[:, i, :], ps[:, i % 4, 0:GROUP], ACT.Copy).then_inc(tok_kept, 1)
                act.wait_ge(varied, 1)
                nc.scalar.activation(st[:, 1, :], st[:, 1, :], ACT.Sqrt).then_inc(rooted, 1)
                for c in range(2):
                    act.wait_ge(back, c + 1)
                    act.wait_ge(loaded, 16 * 4)
                    nc.scalar.activation(act_in[:, c, :], ps[:, c, 0:TOK], ACT.Identity, scale=col[:, 0, c:c + 1], bias=col[:, 1, c:c + 1]).then_inc(lin_done, 1)
                    nc.scalar.activation(sil[:, c, :], ps[:, c, 0:TOK], ACT.Sigmoid, scale=col[:, 0, c:c + 1], bias=col[:, 1, c:c + 1]).then_inc(sig_done, 1)
                for c in range(2):
                    act.wait_ge(done, c + 1)
                    nc.scalar.activation(yT[:, 2 + c, :], ps[:, 2 + c, 0:TOK], ACT.Identity, bias=col[:, 2, c:c + 1]).then_inc(kept, 1)

            @block.vector
            def _(dve):
                o = Own(dve, own)
                dve.wait_ge(tok_kept, NT)
                o.then(nc.vector.tensor_reduce(st[:, 0, :], tok[:, :, :], AX.X, ALU.add))
                o.then(nc.vector.tensor_scalar(st[:, 0, :], st[:, 0, :], 1.0 / GROUP, None, ALU.mult))
                o.then(nc.vector.tensor_tensor(tok[:, :, :], tok[:, :, :], st[:, 0, :].rearrange("p (t o) -> p t o", o=1)
                                               .broadcast_to([P, NT, GROUP]), ALU.subtract))
                o.then(nc.vector.tensor_tensor(sq[:, :, :], tok[:, :, :], tok[:, :, :], ALU.mult))
                o.then(nc.vector.tensor_reduce(st[:, 1, :], sq[:, :, :], AX.X, ALU.add))
                nc.vector.tensor_scalar(st[:, 1, :], st[:, 1, :], 1.0 / GROUP, EPS, ALU.mult, ALU.add).then_inc(varied, 1)
                dve.wait_ge(rooted, 1)
                o.then(nc.vector.reciprocal(st[:, 2, :], st[:, 1, :]))
                nc.vector.tensor_tensor(tok[:, :, :], tok[:, :, :], st[:, 2, :].rearrange("p (t o) -> p t o", o=1)
                                        .broadcast_to([P, NT, GROUP]), ALU.mult).then_inc(normed, 1)
                for c in range(2):
                    dve.wait_ge(sig_done, c + 1)
                    dve.wait_ge(lin_done, c + 1)
                    nc.vector.tensor_tensor(sil[:, c, :], sil[:, c, :], act_in[:, c, :], ALU.mult).then_inc(silued, 1)

            @block.tensor
            def _(pe):
                ident = cst[:, C_ID:C_ID + P]
                for i in range(NT):
                    if i >= 4:
                        pe.wait_ge(tok_kept, i - 3)
                    at = i * P + (PAD if i >= NTX else 0)
                    for c in range(2):
                        last = nc.tensor.transpose(ps[:, i % 4, c * P:(c + 1) * P], acc[:, c, at:at + P], ident)
                    last.then_inc(turned, 1)
                pe.wait_ge(normed, 1)
                for c in range(2):
                    for i in range(NT):
                        last = nc.tensor.transpose(ps[:, c, i * P:(i + 1) * P], tok[:, i, c * P:(c + 1) * P], ident)
                    last.then_inc(back, 1)
                pe.wait_ge(silued, 2)
                pe.wait_ge(loaded, 16 * 4)
                for c in range(2):
                    for t0, tw in ((0, SEQ), (SEQ, CTX)):
                        for k in range(2):
                            last = nc.tensor.matmul(ps[:, 2 + c, t0:t0 + tw], pw[:, k, c * P:(c + 1) * P], sil[:, k, t0:t0 + tw],
                                                    start=(k == 0), stop=(k == 1))
                    last.then_inc(done, 1)


def recurrence(nc, A, g, layer):
    pt, pf, cst, yT, cum = g["pt"], g["pf"], g["cst"], g["yT"], g["cum"]
    G = 2
    KC, VC, GC = 6, 1024, 1280
    q = pf[:, 4:6, :]
    kk = [pf[:, KC + 2 * d:KC + 2 * d + 2, :] for d in range(2)]
    scr = pf[:, 0:4, :].rearrange("p a t -> p (a t)").rearrange("p (g i h t) -> p g i h t", g=G, i=NT, h=2)
    ORDER = ([4, 5, 0, 1, 2, 3], [5, 4, 3, 2, 1, 0])
    NG = NT // TILES_A_MASK
    HALF = P // 2

    def group(d, lev, j):
        return (d * LEVELS + lev) * NG + j

    with ExitStack() as es:
        sb = lambda n, s: es.enter_context(nc.sbuf_tensor(f"rec_{n}", s, F32))
        e1, e2, e3 = (sb(n, [P, G, TOK]) for n in ("e1", "e2", "e3"))
        qe = sb("qe", [P, 2, G * NT, 2, HALF])
        ke = sb("ke", [P, 2, G, TOK])
        dec = sb("dec", [P, 2, G, NT])
        state = sb("state", [P, 2, NT, G, P])
        same = sb("same", [P, NT * 4])
        rs = sb("rs", [P, NT * 4])
        onorm = sb("onorm", [P, HEAD])
        pair = sb("pair", [P, 2])
        qc = [ke[:, d, :, :] for d in range(2)]
        ktok = [qe[:, d, :, :, :].rearrange("p a h t -> p (a h t)").rearrange("p (i c) -> p i c", c=GROUP) for d in range(2)]
        osum = kk[0].rearrange("p g t -> p (g t)").rearrange("p (i c) -> p i c", c=GROUP)
        ps_s = es.enter_context(nc.psum_tensor("rec_ps_s", [P, 2, 2, BANK], F32))
        ps_o = es.enter_context(nc.psum_tensor("rec_ps_o", [P, 2, BANK], F32))
        ps_u = es.enter_context(nc.psum_tensor("rec_ps_u", [P, 2, BANK], F32))
        names = ("loaded own own_p cleared paired level_diff level_exp q_low q_high k_factors scored picked same_done "
                 "carry_diff carry_exp q_carried k_carried turned turned_kept updated state_used states_done out_done out_kept "
                 "varied rooted sig gate_out back back_kept")
        with stage(nc, "rec", names) as (block, loaded, own, own_p, cleared, paired, level_diff, level_exp, q_low, q_high, k_factors,
                                         scored, picked, same_done, carry_diff, carry_exp, q_carried, k_carried, turned, turned_kept,
                                         updated, state_used, states_done, out_done, out_kept, varied, rooted, sig, gate_out, back,
                                         back_kept):
            def by_tile(ap):
                return ap.rearrange("p g (i t) -> p (g i) t", t=P)

            cum_t = [cum[:, d, :, :, :].rearrange("p g i t -> p (g i) t") for d in range(2)]

            def half(ap, n, a):
                return ap.rearrange("p a (b x t) -> p a b x t", x=2, t=n)[:, :, :, a, :]

            def packed(ap, n):
                return ap.rearrange("p (a b t) -> p a b t", a=G * NT, t=n)

            def level_queries(eng, d, lev, hf):
                n = 1 << lev
                part = slice(HEAD * hf, HEAD * hf + HEAD)
                return eng.tensor_tensor(qe[part, lev % 2, :, hf, :].rearrange("p a (b t) -> p a b t", t=n), half(by_tile(q[part]), n, 1 - d),
                                         packed((e2, e3)[lev % 2][part, 1 - d, :], n), ALU.mult)

            @block.sync
            def _(sp):
                sp.dma_start(onorm[:, :], A["hgrn_onorm_g"][bass.ds(layer, 1), :].broadcast_to([P, HEAD])).then_inc(loaded, 16)

            @block.scalar
            def _(act):
                for d in range(2):
                    for lev in range(LEVELS):
                        step = d * LEVELS + lev
                        act.wait_ge(level_diff, step + 1)
                        if step >= 2:
                            used = max(s for s in range(step) if (s % LEVELS) % 2 == lev % 2) + 1
                            for sem in (q_low, q_high, k_factors):
                                act.wait_ge(sem, used)
                        nc.scalar.activation((e2, e3)[lev % 2][:, :, :], e1[:, :, :], ACT.Exp).then_inc(level_exp, 1)
                for sem in (q_low, q_high, k_factors):
                    act.wait_ge(sem, 2 * LEVELS)
                for d in range(2):
                    if d:
                        act.wait_ge(q_carried, 1)
                    nc.scalar.activation(by_tile(e2[:, :, :]), cum_t[d][:, :, 1 - d:1 - d + P], ACT.Exp).then_inc(carry_exp, 1)
                    nc.scalar.activation(dec[:, d, :, :], cum[:, d, :, :, P], ACT.Exp).then_inc(carry_exp, 1)
                    to_end = (e1, e3)[d]
                    act.wait_ge(carry_diff, d + 1)
                    nc.scalar.activation(to_end[:, :, :], to_end[:, :, :], ACT.Exp).then_inc(carry_exp, 1)
                for d in range(2):
                    for i in range(NT):
                        act.wait_ge(turned, NT * d + i + 1)
                        nc.scalar.activation(ktok[d][:, i, :], ps_s[:, i % 2, 0, 0:GROUP], ACT.Copy).then_inc(turned_kept, 1)
                act.wait_ge(q_carried, 2)
                nc.scalar.activation(e3[:, :, :].rearrange("p g (i c) -> p (g i) c", c=GROUP), pt[:, :, GC:GC + GROUP], ACT.Sigmoid).then_inc(sig, 1)
                act.wait_ge(varied, 1)
                nc.scalar.activation(rs[:, :], rs[:, :], ACT.Sqrt).then_inc(rooted, 1)
                for i in range(NT):
                    act.wait_ge(back, i + 1)
                    nc.scalar.activation(yT[:, 6:8, i * P:(i + 1) * P], ps_s[:, i % 2, 0, 0:2 * P].rearrange("p (a b) -> p a b", b=P), ACT.Copy).then_inc(back_kept, 1)

            @block.gpsimd
            def _(pool):
                nc.gpsimd.memset(ke[:, :, :, :], 0.0).then_inc(cleared, 1)
                nc.gpsimd.memset(qe[:, :, :, :, :], 0.0).then_inc(cleared, 1)
                nc.gpsimd.memset(scr, 0.0).then_inc(cleared, 1)
                nc.gpsimd.memset(state[:, :, :, :, :], 0.0).then_inc(cleared, 1)
                pool.wait_ge(cleared, 4)
                nc.gpsimd.memset(pair[:, :], 0.0).then_inc(own_p, 1)
                pool.wait_ge(own_p, 1)
                for hf in range(2):
                    if hf:
                        pool.wait_ge(cleared, 5)
                    nc.gpsimd.memset(pair[HEAD * hf:HEAD * hf + HEAD, hf:hf + 1], 1.0).then_inc(cleared, 1)
                pool.wait_ge(cleared, 6)
                for d in range(2):
                    for lev in range(LEVELS):
                        n = 1 << lev
                        step = d * LEVELS + lev
                        if step >= 2:
                            used = max(s for s in range(step) if (s % LEVELS) % 2 == lev % 2)
                            pool.wait_ge(scored, NG * (used + 1))
                        pool.wait_ge(level_exp, step + 1)
                        if step:
                            pool.wait_ge(k_factors, step)
                        level_queries(nc.gpsimd, d, lev, 1).then_inc(q_high, 1)
                        pool.wait_ge(q_high, step + 1)
                        nc.gpsimd.tensor_tensor(half(by_tile(ke[:, lev % 2, :, :]), n, d), half(by_tile(kk[d]), n, d),
                                                packed((e2, e3)[lev % 2][:, d, :], n), ALU.mult).then_inc(k_factors, 1)

            @block.vector
            def _(dve):
                o = Own(dve, own)
                tt = nc.vector.tensor_tensor

                def distances(d, lev):
                    n = 1 << lev
                    at = cum_t[d][:, :, 1 - d:1 - d + P]
                    mid = cum_t[d][:, :, 0:P].rearrange("p a (b t) -> p a b t", t=2 * n)[:, :, :, n:n + 1].broadcast_to([P, G * NT, P // (2 * n), n])
                    if d or lev:
                        dve.wait_ge(level_exp, LEVELS * d + lev)
                    o(tt(packed(e1[:, 0, :], n), mid, half(at, n, 0), ALU.subtract))
                    o(tt(packed(e1[:, 1, :], n), half(at, n, 1), mid, ALU.subtract))
                    o.settle()
                    dve.sem_inc(level_diff, 1)

                def targets(d, lev):
                    dve.wait_ge(level_exp, LEVELS * d + lev + 1)
                    level_queries(nc.vector, d, lev, 0).then_inc(q_low, 1)

                steps = [(d, lev) for d in range(2) for lev in range(LEVELS)]
                o.then(tt(e3[:, :, :], kk[0], kk[1], ALU.add))
                tt(e3[:, :, :], e3[:, :, :], q, ALU.mult).then_inc(paired, 1)
                distances(0, 0)
                dve.wait_ge(cleared, 6)
                dve.wait_ge(same_done, 1)
                o.then(nc.vector.tensor_copy(same[:, :], ps_u[:, 0, 0:4 * NT]))
                targets(0, 0)
                distances(0, 1)
                for s, (d, lev) in enumerate(steps):
                    n = 1 << lev
                    if s + 1 < len(steps):
                        if lev + 1 == LEVELS:
                            dve.wait_ge(scored, NG * (s + 1))
                        targets(*steps[s + 1])
                    if s + 2 < len(steps):
                        distances(*steps[s + 2])
                    for j in range(NG):
                        m = NG * s + j
                        dve.wait_ge(scored, m + 1)
                        if s:
                            dve.wait_ge(picked, m - NG + 1)
                        w = TILES_A_MASK
                        nb = w * P // n
                        src = ps_s[:, m % 2, :, 0:w * P].rearrange("p g (b t) -> p g b t", t=n)
                        dst = scr[:, :, j * w:(j + 1) * w, :, :].rearrange("p g i h (b x t) -> p g (i h b) x t", x=2, t=n)[:, :, :, 1 - d, :]
                        cm = C_LEV[d][lev]
                        mask = cst[:, cm:cm + nb].bitcast(U32).rearrange("p (a b t) -> p a b t", a=1, t=1)
                        nc.vector.copy_predicated(dst, mask.broadcast_to([P, 2, nb, n]), src).then_inc(picked, 1)
                for d in range(2):
                    to_start, to_end = e2[:, :, :], (e1, e3)[d][:, :, :]
                    tt(by_tile(to_end), cum_t[d][:, :, P:P + 1].broadcast_to([P, G * NT, P]), cum_t[d][:, :, 1 - d:1 - d + P],
                       ALU.subtract).then_inc(carry_diff, 1)
                for d in range(2):
                    dve.wait_ge(carry_exp, 3 * (d + 1))
                    to_start, to_end = e2[:, :, :], (e1, e3)[d][:, :, :]
                    tt(qc[d], q, (to_start, to_end)[d], ALU.mult).then_inc(q_carried, 1)
                    key = (to_end, to_start)[d]
                    tt(key, kk[d], key, ALU.mult).then_inc(k_carried, 1)
                for d in range(2):
                    for n in range(NT - 1):
                        i, nxt = ORDER[d][n], ORDER[d][n + 1]
                        dve.wait_ge(updated, (NT - 1) * d + n + 1)
                        for hf in range(2):
                            part = slice(HEAD * hf, HEAD * hf + HEAD)
                            for gg in range(G):
                                src = ps_u[part, n % 2, gg * P + HEAD * hf:gg * P + HEAD * hf + HEAD]
                                new = state[part, d, nxt, gg, HEAD * hf:HEAD * hf + HEAD]
                                if n == 0:
                                    o(nc.vector.tensor_copy(new, src))
                                else:
                                    o(nc.vector.scalar_tensor_tensor(new, state[part, d, i, gg, HEAD * hf:HEAD * hf + HEAD],
                                                                     dec[part, d, gg, i:i + 1], src, ALU.mult, ALU.add))
                        o.settle()
                        dve.sem_inc(states_done, 1)
                heads = lambda ap: ap.rearrange("p i (h e) -> p (i h) e", e=HEAD)
                wide = lambda e: e[:, :, :].rearrange("p g (i c) -> p (g i) c", c=GROUP)
                split = lambda ap: ap.rearrange("p i (h e) -> p i h e", e=HEAD)
                o.then(tt(split(osum), split(pt[:, :, VC:VC + GROUP]), same[:, :].rearrange("p (i h o) -> p i h o", i=NT, o=1).broadcast_to([P, NT, 4, HEAD]), ALU.mult))
                for i in range(NT):
                    dve.wait_ge(out_done, i + 1)
                    o(tt(osum[:, i, :], osum[:, i, :], ps_o[:, i % 2, 0:GROUP], ALU.add))
                    o.settle()
                    dve.sem_inc(out_kept, 1)
                o.then(tt(wide(e1), osum, osum, ALU.mult))
                o.then(nc.vector.tensor_reduce(rs[:, :], heads(wide(e1)), AX.X, ALU.add))
                nc.vector.tensor_scalar(rs[:, :], rs[:, :], 1.0 / HEAD, EPS, ALU.mult, ALU.add).then_inc(varied, 1)
                dve.wait_ge(sig, 1)
                o.then(tt(wide(e3), wide(e3), pt[:, :, GC:GC + GROUP], ALU.mult))
                dve.wait_ge(loaded, 16)
                o.then(tt(heads(wide(e3)), heads(wide(e3)), onorm[:, :].rearrange("p (o e) -> p o e", o=1).broadcast_to([P, 4 * NT, HEAD]), ALU.mult))
                dve.wait_ge(rooted, 1)
                o.then(nc.vector.reciprocal(rs[:, :], rs[:, :]))
                o.then(tt(heads(osum), heads(osum), rs[:, :].rearrange("p (h o) -> p h o", o=1).broadcast_to([P, 4 * NT, HEAD]), ALU.mult))
                tt(osum, osum, wide(e3), ALU.mult).then_inc(gate_out, 1)

            @block.tensor
            def _(pe):
                ident = cst[:, C_ID:C_ID + P]
                pe.wait_ge(paired, 1)
                pe.wait_ge(cleared, 6)
                for i in range(NT):
                    for gg in range(G):
                        last = nc.tensor.matmul(ps_u[:, 0, 4 * i + 2 * gg:4 * i + 2 * gg + 2], e3[:, gg, i * P:(i + 1) * P], pair[:, :], start=True, stop=True)
                last.then_inc(same_done, 1)
                for d in range(2):
                    for lev in range(LEVELS):
                        step = d * LEVELS + lev
                        for sem in (q_low, q_high, k_factors):
                            pe.wait_ge(sem, step + 1)
                        for j in range(NG):
                            m = group(d, lev, j)
                            if m >= 2:
                                pe.wait_ge(picked, m - 1)
                            for n in range(TILES_A_MASK):
                                i = j * TILES_A_MASK + n
                                for gg in range(G):
                                    last = nc.tensor.matmul(ps_s[:, m % 2, gg, n * P:(n + 1) * P], ke[:, lev % 2, gg, i * P:(i + 1) * P],
                                                            qe[:, lev % 2, gg * NT + i, :, :].rearrange("p h t -> p (h t)"), start=True, stop=True)
                            last.then_inc(scored, 1)
                pe.wait_ge(picked, NG * 2 * LEVELS)
                for d in range(2):
                    pe.wait_ge(k_carried, d + 1)
                    for i in range(NT):
                        if d or i >= 2:
                            pe.wait_ge(turned_kept, NT * d + i - 1)
                        for gg in range(G):
                            last = nc.tensor.transpose(ps_s[:, i % 2, 0, gg * P:(gg + 1) * P], (e1, e2)[d][:, gg, i * P:(i + 1) * P], ident)
                        last.then_inc(turned, 1)
                for d in range(2):
                    for n, i in enumerate(ORDER[d][:-1]):
                        m = (NT - 1) * d + n
                        pe.wait_ge(turned_kept, NT * (d + 1))
                        if m >= 2:
                            pe.wait_ge(states_done, m - 1 if n != 0 else m)
                        for gg in range(G):
                            last = nc.tensor.matmul(ps_u[:, n % 2, gg * P:(gg + 1) * P], ktok[d][:, i, gg * P:(gg + 1) * P],
                                                    pt[:, i, VC + gg * P:VC + (gg + 1) * P], start=True, stop=True)
                        last.then_inc(updated, 1)
                pe.wait_ge(states_done, 2 * (NT - 1))
                pe.wait_ge(q_carried, 2)
                for i in range(NT):
                    if i >= 2:
                        pe.wait_ge(out_kept, i - 1)
                    for gg in range(G):
                        for d in range(2):
                            if d:
                                for hf in range(2):
                                    c = gg * P + hf * HEAD
                                    nc.tensor.matmul(ps_o[:, i % 2, c:c + HEAD], scr[:, gg, i, hf, :], pt[:, i, VC + c:VC + c + HEAD],
                                                     start=False, stop=False)
                            last = nc.tensor.matmul(ps_o[:, i % 2, gg * P:(gg + 1) * P], qc[d][:, gg, i * P:(i + 1) * P], state[:, d, i, gg, :],
                                                    start=(d == 0), stop=(d == 1))
                    last.then_inc(out_done, 1)
                pe.wait_ge(gate_out, 1)
                for i in range(NT):
                    if i >= 2:
                        pe.wait_ge(back_kept, i - 1)
                    for a in range(2):
                        last = nc.tensor.transpose(ps_s[:, i % 2, 0, a * P:(a + 1) * P], osum[:, i, a * P:(a + 1) * P], ident)
                    last.then_inc(back, 1)


def gates_scalar(nc, act, pf, scratch, step, sems):
    e1, e2, _, e4 = scratch
    own_a, exp_arg, first_ln, diff, lse_ln, k_arg, k_exp = sems
    d = step // 3
    if step % 3 == 0:
        act.wait_ge(exp_arg, d + 1)
        nc.scalar.activation(e1[:, :, :], e1[:, :, :], ACT.Exp).then_inc(own_a, 1)
        act.wait_ge(own_a, 2 * d + 1)
        nc.scalar.activation(e2[:, :, :], e1[:, :, :], ACT.Ln, bias=1.0).then_inc(first_ln, 1)
    elif step % 3 == 1:
        act.wait_ge(diff, d + 1)
        nc.scalar.activation(e4[:, :, :], e4[:, :, :], ACT.Exp).then_inc(own_a, 1)
        act.wait_ge(own_a, 2 * d + 2)
        nc.scalar.activation(e4[:, :, :], e4[:, :, :], ACT.Ln, bias=1.0).then_inc(lse_ln, 1)
    else:
        act.wait_ge(k_arg, d + 1)
        z = pf[:, 6 + 2 * d:8 + 2 * d, :]
        nc.scalar.activation(z, z, ACT.Exp).then_inc(k_exp, 1)


def gates_vector(nc, dve, o, layer, lb, lbl, pf, cst, cum, scratch, sems):
    e1, e2, e3, e4 = scratch
    exp_arg, first_ln, diff, lse_ln, k_arg, k_exp = sems
    tt = nc.vector.tensor_tensor
    o(nc.vector.memset(cum[:, :, :, :, 0], 0.0))
    o.then(nc.vector.tensor_copy(lbl[:, :, :], lb[:, bass.ds(layer, 1), :, :].rearrange("p a b c -> p (a b) c")))
    for d in range(2):
        z = pf[:, 6 + 2 * d:8 + 2 * d, :]
        o.then(nc.vector.tensor_scalar(e3[:, :, :], z, 0.0, None, ALU.min))
        o(nc.vector.scalar_tensor_tensor(e1[:, :, :], e3[:, :, :], 2.0, z, ALU.mult, ALU.subtract))
        o.then(tt(z, e3[:, :, :], z, ALU.subtract))
        dve.sem_inc(exp_arg, 1)
        dve.wait_ge(first_ln, d + 1)
        for gg in range(2):
            o(nc.vector.tensor_scalar(e1[:, gg, :], z[:, gg, :], lbl[:, 1, 2 * d + gg:2 * d + gg + 1], None, ALU.add))
        o.settle()
        o.then(tt(e4[:, :, :], e3[:, :, :], e1[:, :, :], ALU.subtract))
        nc.vector.scalar_tensor_tensor(e4[:, :, :], e4[:, :, :], -1.0, e4[:, :, :], ALU.mult, ALU.min).then_inc(diff, 1)
        tt(z, z, e2[:, :, :], ALU.subtract).then_inc(k_arg, 1)
        o.then(tt(e3[:, :, :], e3[:, :, :], e1[:, :, :], ALU.max))
        o.then(tt(e3[:, :, :], e3[:, :, :], e2[:, :, :], ALU.subtract))
        dve.wait_ge(lse_ln, d + 1)
        o.then(tt(e3[:, :, :], e3[:, :, :], e4[:, :, :], ALU.add))
        ones = cst[:, C_COL:C_COL + 1].broadcast_to([P, P])
        for gg in range(2):
            for i in range(NT):
                o(nc.vector.tensor_tensor_scan(cum[:, d, gg, i, 1:P + 1], ones, e3[:, gg, i * P:(i + 1) * P], 0.0, ALU.mult, ALU.add))
        dve.wait_ge(k_exp, d + 1)
        for gg in range(2):
            o(nc.vector.tensor_scalar(z[:, gg, :], z[:, gg, :], lbl[:, 2, 2 * d + gg:2 * d + gg + 1], None, ALU.mult))
        o.settle()


def gated_add(dve, o, g, gate, ps, i, h, tmp):
    x = g["x"]
    s = 0 if i < NTX else 1
    o.then(dve.tensor_tensor(tmp, ps, gate[:, s, h * BANK:(h + 1) * BANK], ALU.mult))
    return dve.tensor_tensor(x[:, i, h * BANK:(h + 1) * BANK], x[:, i, h * BANK:(h + 1) * BANK], tmp, ALU.add)


def out_projection(nc, A, g, layer):
    yT = g["yT"]
    jobs = [(h, i) for h in range(2) for i in range(NT)]
    with ExitStack() as es:
        w = es.enter_context(nc.sbuf_tensor("w_out_t", [P, 2, KT, BANK], F32))
        gate = es.enter_context(nc.sbuf_tensor("out_gate", [P, 2, D], F32))
        tmp = es.enter_context(nc.sbuf_tensor("out_tmp", [P, BANK], F32))
        pr = es.enter_context(nc.psum_tensor("out_ps_row", [P, 2, 2 * BANK], F32))
        ps = es.enter_context(nc.psum_tensor("out_ps", [P, 4, BANK], F32))
        with stage(nc, "outp", "w0 w1 spread gates own done added") as (block, w0, w1, spread, gates, own, done, added):
            w_in = (w0, w1)

            @block.sync
            def _(sp):
                for h in range(2):
                    sp.dma_start(w[:, h, :, :], A["w_out"][bass.ds(layer, 1), :, h * BANK:(h + 1) * BANK]
                                 .rearrange("a (k p) n -> p (a k) n", p=P)).then_inc(w_in[h], 16)

            @block.tensor
            def _(pe):
                for s in range(2):
                    broadcast_row(nc, g, pr[:, s, :], 2, s).then_inc(spread, 1)
                for n, (h, i) in enumerate(jobs):
                    if i == 0:
                        pe.wait_ge(w_in[h], 16)
                    if n >= 4:
                        pe.wait_ge(added, n - 3)
                    for k in range(KT):
                        last = nc.tensor.matmul(ps[:, n % 4, :], yT[:, k, i * P:(i + 1) * P], w[:, h, k, :], start=(k == 0), stop=(k == KT - 1))
                    last.then_inc(done, 1)

            @block.scalar
            def _(act):
                for s in range(2):
                    act.wait_ge(spread, s + 1)
                    nc.scalar.activation(gate[:, s, :], pr[:, s, :], ACT.Copy).then_inc(gates, 1)

            @block.vector
            def _(dve):
                o = Own(dve, own)
                dve.wait_ge(gates, 2)
                for n, (h, i) in enumerate(jobs):
                    dve.wait_ge(done, n + 1)
                    if n:
                        dve.wait_ge(added, n)
                    gated_add(nc.vector, o, g, gate, ps[:, n % 4, :], i, h, tmp[:, :]).then_inc(added, 1)


def shared_expert(nc, A, g, layer, hT, gate):
    cst = g["cst"]
    with ExitStack() as es:
        sb = lambda n, s: es.enter_context(nc.sbuf_tensor(f"sh_{n}", s, F32))
        wgu = sb("wgu", [P, KT, 2 * HID])
        wd = sb("wd", [P, 2, D])
        sig = sb("sig", [P, 2, HID])
        hid = sb("hid", [P, 2, HID])
        hidT = sb("hidT", [P, 2, HID])
        tmp = sb("tmp", [P, BANK])
        ps_gu = es.enter_context(nc.psum_tensor("sh_ps_gu", [P, 2, BANK], F32))
        ps_h = es.enter_context(nc.psum_tensor("sh_ps_h", [P, 2, BANK], F32))
        ps_y = es.enter_context(nc.psum_tensor("sh_ps_y", [P, 2, 2 * BANK], F32))
        names = "w_in spread gates own gu_done sig_done hid_done turned hidT_done y_done y_used"
        with stage(nc, "shared", names) as (block, w_in, spread, gates, own, gu_done, sig_done, hid_done, turned, hidT_done, y_done, y_used):
            @block.sync
            def _(sp):
                for n, c in (("sh_w_gate", 0), ("sh_w_up", HID)):
                    sp.dma_start(wgu[:, :, c:c + HID], A[n][bass.ds(layer, 1)].rearrange("a (k p) n -> p (a k) n", p=P)).then_inc(w_in, 16)
                sp.dma_start(wd[:, :, :], A["sh_w_down"][bass.ds(layer, 1)].rearrange("a (k p) n -> p (a k) n", p=P)).then_inc(w_in, 16)

            @block.tensor
            def _(pe):
                ident = cst[:, C_ID:C_ID + P]
                for s in range(2):
                    broadcast_row(nc, g, ps_y[:, s, :], 5, s).then_inc(spread, 1)
                pe.wait_ge(w_in, 48)
                pe.wait_ge(gates, 2)
                for i in range(NT + 1):
                    if i < NT:
                        if i >= 2:
                            pe.wait_ge(hid_done, i - 1)
                        for k in range(KT):
                            last = nc.tensor.matmul(ps_gu[:, i % 2, :], hT[:, k, i * P:(i + 1) * P], wgu[:, k, :], start=(k == 0), stop=(k == KT - 1))
                        last.then_inc(gu_done, 1)
                    if i:
                        m = i - 1
                        pe.wait_ge(hid_done, m + 1)
                        for a in range(2):
                            last = nc.tensor.transpose(ps_h[:, m % 2, a * P:(a + 1) * P], hid[:, m % 2, a * P:(a + 1) * P], ident)
                        last.then_inc(turned, 1)
                        pe.wait_ge(hidT_done, m + 1)
                        if m >= 2:
                            pe.wait_ge(y_used, 2 * (m - 1))
                        for h in range(2):
                            for a in range(2):
                                last = nc.tensor.matmul(ps_y[:, m % 2, h * BANK:(h + 1) * BANK], hidT[:, m % 2, a * P:(a + 1) * P],
                                                        wd[:, a, h * BANK:(h + 1) * BANK], start=(a == 0), stop=(a == 1))
                        last.then_inc(y_done, 1)

            @block.scalar
            def _(act):
                for s in range(2):
                    act.wait_ge(spread, s + 1)
                    nc.scalar.activation(gate[:, s, :], ps_y[:, s, :], ACT.Copy).then_inc(gates, 1)
                for i in range(NT):
                    act.wait_ge(gu_done, i + 1)
                    if i >= 2:
                        act.wait_ge(hid_done, i - 1)
                    nc.scalar.activation(sig[:, i % 2, :], ps_gu[:, i % 2, 0:HID], ACT.Sigmoid).then_inc(sig_done, 1)
                    act.wait_ge(turned, i + 1)
                    if i >= 2:
                        act.wait_ge(y_done, i - 1)
                    nc.scalar.activation(hidT[:, i % 2, :], ps_h[:, i % 2, 0:HID], ACT.Copy).then_inc(hidT_done, 1)

            @block.vector
            def _(dve):
                o = Own(dve, own)
                for i in range(NT + 1):
                    if i < NT:
                        dve.wait_ge(sig_done, i + 1)
                        if i >= 2:
                            dve.wait_ge(turned, i - 1)
                        o.then(nc.vector.tensor_tensor(sig[:, i % 2, :], sig[:, i % 2, :], ps_gu[:, i % 2, 0:HID], ALU.mult))
                        nc.vector.tensor_tensor(hid[:, i % 2, :], sig[:, i % 2, :], ps_gu[:, i % 2, HID:2 * HID], ALU.mult).then_inc(hid_done, 1)
                    if i:
                        m = i - 1
                        dve.wait_ge(y_done, m + 1)
                        dve.wait_ge(gates, 2)
                        for h in range(2):
                            if m or h:
                                dve.wait_ge(y_used, 2 * m + h)
                            gated_add(nc.vector, o, g, gate, ps_y[:, m % 2, h * BANK:(h + 1) * BANK], m, h, tmp[:, :]).then_inc(y_used, 1)


MAX_EXTRA = 64
N_SLOT_TAB = N_EXP + MAX_EXTRA


def routing(nc, A, g, layer, hT, r):
    cst = g["cst"]
    E = N_EXP
    with ExitStack() as es:
        sb = lambda n, s: es.enter_context(nc.sbuf_tensor(f"rt_{n}", s, F32))
        wr = sb("w", [P, KT, E])
        bias = sb("bias", [P, E])
        sc = sb("score", [P, NT, E])
        sel = sb("sel", [P, NT, E])
        best = sb("best", [P, NT, N_GRP, 8])
        gs = sb("gsum", [P, NT, N_GRP])
        gt = sb("gt", [P, NT, N_GRP, N_GRP])
        eq = sb("eq", [P, NT, N_GRP, N_GRP])
        keep = sb("keep", [P, NT, N_GRP])
        pen = sb("pen", [P, NT, N_GRP])
        top = sb("top", [P, NT, 8])
        rep = sb("rep", [P, NT, E])
        msk = sb("mask", [P, NT, E])
        den = sb("den", [P, NT])
        place = sb("place", [P, NT, E])
        ones = sb("ones", [P, P])
        extra = sb("extra", [P, E])
        cumx = sb("cumx", [P, E])
        over = sb("over", [P, E])
        le = sb("le", [P, E])
        colx = sb("colx", [P, 3])
        dg = sb("dg", [P, 2, MAX_EXTRA])
        npair = sb("npair", [1, 4])
        ps_l = es.enter_context(nc.psum_tensor("rt_ps_l", [P, BANK], F32))
        ps_r = es.enter_context(nc.psum_tensor("rt_ps_r", [P, BANK], F32))
        ps_c = es.enter_context(nc.psum_tensor("rt_ps_c", [P, BANK], F32))
        names = "w_in logits scored own chosen ranked extras listed"
        with stage(nc, "route", names) as (block, w_in, logits, scored, own, chosen, ranked, extras, listed):
            @block.sync
            def _(sp):
                sp.dma_start(wr[:, :, :], A["router_w"][bass.ds(layer, 1)].rearrange("a (k p) n -> p (a k) n", p=P)).then_inc(w_in, 16)
                sp.dma_start(bias[:, :], A["router_bias"][bass.ds(layer, 1), :].broadcast_to([P, E])).then_inc(w_in, 16)

            @block.scalar
            def _(act):
                act.wait_ge(logits, 1)
                nc.scalar.activation(sc[:, :, :].rearrange("p a b -> p (a b)"), ps_l[:, 0:NT * E], ACT.Sigmoid).then_inc(scored, 1)

            @block.tensor
            def _(pe):
                pe.wait_ge(w_in, 32)
                for i in range(NT):
                    for k in range(KT):
                        last = nc.tensor.matmul(ps_l[:, i * E:(i + 1) * E], hT[:, k, i * P:(i + 1) * P], wr[:, k, :], start=(k == 0), stop=(k == KT - 1))
                last.then_inc(logits, 1)
                pe.wait_ge(chosen, 1)
                for i in range(NT):
                    nc.tensor.matmul(ps_r[:, i * E:(i + 1) * E], cst[:, C_TRI:C_TRI + P], msk[:, i, :], start=True, stop=(i == 0))
                    for j in range(i):
                        nc.tensor.matmul(ps_r[:, i * E:(i + 1) * E], ones[:, :], msk[:, j, :], start=False, stop=(j == i - 1))
                for j in range(NT):
                    last = nc.tensor.matmul(ps_c[:, 0:E], ones[:, :], msk[:, j, :], start=(j == 0), stop=(j == NT - 1))
                last.then_inc(ranked, 1)
                pe.wait_ge(extras, 1)
                nc.tensor.matmul(ps_c[:, E:E + 2 * MAX_EXTRA], ones[:, :], dg[:, :, :].rearrange("p a b -> p (a b)"), start=True, stop=True).then_inc(listed, 1)

            @block.vector
            def _(dve):
                v = nc.vector
                o = Own(dve, own)
                o(v.memset(ones[:, :], 1.0))
                dve.wait_ge(scored, 1)
                dve.wait_ge(w_in, 32)
                o.then(v.tensor_tensor(sel[:, :, :], sc[:, :, :], bias[:, :].rearrange("p (o e) -> p o e", o=1).broadcast_to([P, NT, E]), ALU.add))
                for i in range(NT):
                    for q in range(N_GRP):
                        o(v.max(out=best[:, i, q, :], in_=sel[:, i, q * PER_GRP:(q + 1) * PER_GRP]))
                o.settle()
                o.then(v.tensor_tensor(gs[:, :, :], best[:, :, :, 0], best[:, :, :, 1], ALU.add))
                for i in range(NT):
                    other = gs[:, i, :].rearrange("p (o k) -> p o k", o=1).broadcast_to([P, N_GRP, N_GRP])
                    self_ = gs[:, i, :].rearrange("p (j o) -> p j o", o=1).broadcast_to([P, N_GRP, N_GRP])
                    o(v.tensor_tensor(gt[:, i, :, :], other, self_, ALU.is_gt))
                    o(v.tensor_tensor(eq[:, i, :, :], other, self_, ALU.is_equal))
                o.settle()
                low = cst[:, C_LOW:C_LOW + 64].rearrange("p (o n) -> p o n", o=1).broadcast_to([P, NT, 64])
                flat = lambda ap: ap.rearrange("p i a b -> p i (a b)")
                o.then(v.tensor_tensor(flat(eq[:, :, :, :]), flat(eq[:, :, :, :]), low, ALU.mult))
                o.then(v.tensor_tensor(gt[:, :, :, :], gt[:, :, :, :], eq[:, :, :, :], ALU.add))
                o.then(v.tensor_reduce(keep[:, :, :], gt[:, :, :, :], AX.X, ALU.add))
                o.then(v.tensor_scalar(keep[:, :, :], keep[:, :, :], 3.5, None, ALU.is_lt))
                o.then(v.tensor_scalar(pen[:, :, :], keep[:, :, :], -1.0, -NEG, ALU.add, ALU.mult))
                grp = lambda ap: ap.rearrange("p i (q e) -> p (i q) e", e=PER_GRP)
                wide = lambda ap: ap.rearrange("p i (q o) -> p (i q) o", o=1).broadcast_to([P, NT * N_GRP, PER_GRP])
                o.then(v.tensor_tensor(grp(sel[:, :, :]), grp(sel[:, :, :]), wide(keep[:, :, :]), ALU.mult))
                o.then(v.tensor_tensor(grp(sel[:, :, :]), grp(sel[:, :, :]), wide(pen[:, :, :]), ALU.add))
                for i in range(NT):
                    o(v.max(out=top[:, i, :], in_=sel[:, i, :]))
                o.settle()
                for i in range(NT):
                    o(v.match_replace(out=rep[:, i, :], in_to_replace=top[:, i, :], in_values=sel[:, i, :], imm_value=2 * NEG))
                o.settle()
                o.then(v.tensor_scalar(msk[:, :, :], rep[:, :, :], 1.5 * NEG, None, ALU.is_lt))
                o.then(v.tensor_tensor(sel[:, :, :], sc[:, :, :], msk[:, :, :], ALU.mult))
                o.then(v.tensor_reduce(den[:, :], sel[:, :, :], AX.X, ALU.add))
                o.then(v.reciprocal(den[:, :], den[:, :]))
                o.then(v.tensor_tensor(sel[:, :, :], sel[:, :, :], den[:, :].rearrange("p (t o) -> p t o", o=1).broadcast_to([P, NT, E]), ALU.mult))
                vals = r["vals"][:, :, :].rearrange("p t (e c) -> p t e c", c=4)
                o(v.tensor_scalar(vals[:, :, :, 2], sel[:, :, :], ROUTED_SCALE, None, ALU.mult))
                for i in range(NT):
                    o(v.tensor_tensor_scan(place[:, i, :], cst[:, C_COL:C_COL + 1].broadcast_to([P, E]), msk[:, i, :], 0.0, ALU.mult, ALU.add))
                o.settle()
                o.then(v.tensor_tensor(place[:, :, :], place[:, :, :], msk[:, :, :], ALU.subtract))
                o.then(v.tensor_scalar(msk[:, NTX:NT, :], msk[:, NTX:NT, :], cst[:, bass.ds(layer + (C_COL + 10), 1)], None, ALU.mult))
                dve.sem_inc(chosen, 1)
                token = cst[:, C_COL + 4:C_COL + 4 + NT].rearrange("p (t o) -> p t o", o=1).broadcast_to([P, NT, E])
                o(v.tensor_copy(vals[:, :, :, 0], token))
                o.then(v.tensor_scalar(sel[:, :, :], token, float(TOP_K), None, ALU.mult))
                o(v.tensor_tensor(vals[:, :, :, 1], sel[:, :, :], place[:, :, :], ALU.add))
                o(v.memset(vals[:, :, :, 3], 1.0))
                dve.wait_ge(ranked, 1)
                rank = r["rank"]
                o.then(v.scalar_tensor_tensor(rank[:, :, :].rearrange("p a b -> p (a b)"), ps_r[:, 0:NT * E], 1.0,
                                              msk[:, :, :].rearrange("p a b -> p (a b)"), ALU.add, ALU.mult))
                o(v.tensor_scalar(rank[:, :, :], rank[:, :, :], -1.0, None, ALU.add))
                o.then(v.tensor_scalar(extra[:, :], ps_c[:, 0:E], float(P), None, ALU.is_gt))
                for m in range(2, NT):
                    o.then(v.tensor_scalar(over[:, :], ps_c[:, 0:E], float(m * P), None, ALU.is_gt))
                    o.then(v.tensor_tensor(extra[:, :], extra[:, :], over[:, :], ALU.add))
                o.then(v.tensor_tensor_scan(cumx[:, :], cst[:, C_COL:C_COL + 1].broadcast_to([P, E]), extra[:, :], 0.0, ALU.mult, ALU.add))
                row = cst[:, C_COL + 1:C_COL + 2]
                o.then(v.tensor_scalar(le[:, :], cumx[:, :], row, None, ALU.is_le))
                o.then(v.tensor_reduce(colx[:, 0:1], le[:, :], AX.X, ALU.add))
                o.then(v.tensor_tensor(le[:, :], le[:, :], extra[:, :], ALU.mult))
                o.then(v.tensor_reduce(colx[:, 1:2], le[:, :], AX.X, ALU.add))
                o.then(v.tensor_tensor(colx[:, 1:2], row, colx[:, 1:2], ALU.subtract))
                o.then(v.tensor_scalar(colx[:, 1:2], colx[:, 1:2], 1.0, float(P), ALU.add, ALU.mult))
                o.then(v.tensor_scalar(colx[:, 2:3], colx[:, 0:1], E - 0.5, 1e6, ALU.is_gt, ALU.mult))
                o.then(v.tensor_tensor(colx[:, 1:2], colx[:, 1:2], colx[:, 2:3], ALU.add))
                o.then(v.tensor_scalar(colx[:, 0:1], colx[:, 0:1], float(E - 1), None, ALU.min))
                for a in range(2):
                    o(v.tensor_scalar(dg[:, a, :], cst[:, C_ID:C_ID + MAX_EXTRA], colx[:, a:a + 1], None, ALU.mult))
                o.settle()
                dve.sem_inc(extras, 1)
                first, expert = r["first"], r["expert"]
                o(v.memset(first[:, 0:E], 0.0))
                o(v.tensor_copy(expert[:, 0:E], cst[0:1, C_IOTA:C_IOTA + E]))
                dve.wait_ge(listed, 1)
                o(v.tensor_copy(expert[:, E:E + MAX_EXTRA], ps_c[0:1, E:E + MAX_EXTRA]))
                o(v.tensor_copy(first[:, E:E + MAX_EXTRA], ps_c[:, E + MAX_EXTRA:E + 2 * MAX_EXTRA]))
                o.then(v.tensor_copy(r["n_i"][:, 0:1], cumx[0:1, E - 1:E]))
                o.then(v.tensor_scalar(r["n_i"][:, 1:2], r["n_i"][:, 0:1], 1, None, ALU.bitwise_and))
                o.then(v.tensor_copy(npair[:, 0:2], r["n_i"][:, 0:2]))
                o.then(v.tensor_tensor(npair[:, 2:3], npair[:, 0:1], npair[:, 1:2], ALU.add))
                o.then(v.tensor_scalar(npair[:, 2:3], npair[:, 2:3], float(E), None, ALU.add))
                o.then(v.tensor_copy(r["n_i"][:, 2:3], npair[:, 2:3]))


def routed_experts(nc, A, g, layer, r, h_dram, y_dram):
    cst = g["cst"]
    rank, vals, first, expert, n_i = r["rank"], r["vals"], r["first"], r["expert"], r["n_i"]
    with ExitStack() as es:
        sb = lambda n, s, dt=F32: es.enter_context(nc.sbuf_tensor(f"ex_{n}", s, dt))
        wgu = sb("wgu", [P, 2, KT, 2 * HID])
        wd = sb("wd", [P, 2, 2, D])
        hot = sb("hot", [P, NT, P])
        slot = sb("slot", [P, 2, 4])
        miss = sb("miss", [P, 2])
        at_in = sb("at_in", [P, 2, 1], I32)
        at_out = sb("at_out", [P, 2, 1], I32)
        wt = sb("wt", [P, 2, 1])
        rows = sb("rows", [P, 2, D])
        rowsT = sb("rowsT", [P, 2, D])
        sig = sb("sig", [P, HID])
        hid = sb("hid", [P, HID])
        hidT = sb("hidT", [P, HID])
        res = sb("res", [P, 2, D])
        pt = lambda n, s: es.enter_context(nc.psum_tensor(f"ex_ps_{n}", s, F32))
        ps_i = pt("i", [P, BANK])
        ps_x = pt("x", [P, 2 * BANK])
        ps_gu = pt("gu", [P, BANK])
        ps_h = pt("h", [P, BANK])
        ps_y = pt("y", [P, 2 * BANK])
        names = ("gu0 gu1 dn0 dn1 hot_done slots copied missed idx_ready out_ready taken turned rowsT_done gu_done sig_done half_hid "
                 "hid_done hid_turned hidT_done y_done res_done out_free")
        with stage(nc, "experts", names, g["rows_sems"]) as (
                block, gu0, gu1, dn0, dn1, hot_done, slots, copied, missed, idx_ready, out_ready, taken, turned, rowsT_done, gu_done,
                sig_done, half_hid, hid_done, hid_turned, hidT_done, y_done, res_done, out_free):
            gu_in, dn_in = (gu0, gu1), (dn0, dn1)
            gathered, scattered = g["rows_sems"][0:2], g["rows_sems"][2:4]

            def count(eng):
                return eng.value_load(n_i[0:1, 2:3], min_val=N_EXP, max_val=N_EXP + MAX_EXTRA - 4)

            def expert_of(eng, b):
                return eng.value_load(expert[0:1, bass.ds(b, 1)], min_val=0, max_val=N_EXP - 1)

            def blocks(eng, body):
                body(0, 0)
                body(1, 1)
                with eng.Fori(2, count(eng), 2) as b0:
                    body(b0, 0)
                    body(b0 + 1, 1)

            def wait(eng, sem, value):
                if not (isinstance(value, int) and value == 0):
                    eng.wait_ge(sem, value)

            def seen(b, a, units=16):
                return (b - a) * (units // 2) + units

            @block.sync
            def _(sp):
                def body(b, a):
                    e = expert_of(sp, b)
                    if not isinstance(b, int):
                        sp.wait_ge(gu_done, b - 1)
                    for n, c in (("exp_w_gate", 0), ("exp_w_up", HID)):
                        sp.dma_start(wgu[:, a, :, c:c + HID], A[n][bass.ds(layer, 1), bass.ds(e, 1)]
                                     .rearrange("a e (k p) n -> p (a e k) n", p=P)).then_inc(gu_in[a], 16)
                    if not isinstance(b, int):
                        sp.wait_ge(y_done, b - 1)
                    sp.dma_start(wd[:, a, :, :], A["exp_w_down"][bass.ds(layer, 1), bass.ds(e, 1)]
                                 .rearrange("a e (k p) n -> p (a e k) n", p=P)).then_inc(dn_in[a], 16)

                blocks(sp, body)

            @block.gpsimd
            def _(pool):
                def gather(b, a):
                    pool.wait_ge(idx_ready, b + 1)
                    pool.sem_inc(taken, 1)
                    pool.indirect_dma_start(out=rows[:, a, :], out_offset=None, in_=h_dram[:, :],
                                            in_offset=bass.IndirectOffsetOnAxis(ap=at_in[:, a, :], axis=0)).then_inc(gathered[a], 16)

                def body(b, a):
                    pool.wait_ge(turned, b + 1)
                    gather(b + 2, a)
                    if not (isinstance(b, int) and b == 0):
                        pool.wait_ge(scattered[1 - a], seen(b - 1, 1 - a))
                        pool.sem_inc(out_free, 1)
                    pool.wait_ge(res_done, b + 1)
                    pool.sem_inc(taken, 1)
                    pool.indirect_dma_start(out=y_dram[:, :], out_offset=bass.IndirectOffsetOnAxis(ap=at_out[:, a, :], axis=0),
                                            in_=res[:, a, :], in_offset=None).then_inc(scattered[a], 16)

                gather(0, 0)
                gather(1, 1)
                blocks(pool, body)
                n = count(pool)
                pool.wait_ge(scattered[1], n * 8)
                for a in range(2):
                    pool.wait_ge(gathered[a], n * 8 + 16)
                pool.sem_inc(taken, 1)
                pool.dma_reset(range(gathered[0].num, scattered[1].num + 1))

            @block.vector
            def _(dve):
                v = nc.vector

                def find(b):
                    e = expert_of(dve, b)
                    wait(dve, slots, b)
                    for i in range(NT):
                        last = v.tensor_scalar(hot[:, i, :], cst[:, C_IOTA:C_IOTA + P], first[:, bass.ds(b, 1)],
                                               rank[:, i, bass.ds(e, 1)], ALU.add, ALU.is_equal)
                    last.then_inc(hot_done, 1)

                def place_in(b, a):
                    dve.wait_ge(slots, b + 1)
                    v.tensor_copy(slot[:, a, :], ps_i[:, 0:4]).then_inc(copied, 1)
                    dve.wait_ge(copied, b + 1)
                    if not isinstance(b, int):
                        dve.wait_ge(gathered[a], seen(b - 2, a))
                    v.tensor_copy(at_in[:, a, :], slot[:, a, 0:1]).then_inc(idx_ready, 1)

                def place_out(b, a):
                    if not (isinstance(b, int) and b < 2):
                        dve.wait_ge(out_free, b - 1)
                    v.tensor_copy(wt[:, a, :], slot[:, a, 2:3])
                    v.tensor_scalar(miss[:, a:a + 1], slot[:, a, 3:4], -1.0, 1.0, ALU.mult, ALU.add).then_inc(missed, 1)
                    dve.wait_ge(missed, b + 1)
                    v.scalar_tensor_tensor(at_out[:, a, :], miss[:, a:a + 1], cst[:, C_COL + 2:C_COL + 3], slot[:, a, 1:2],
                                           ALU.mult, ALU.add).then_inc(out_ready, 1)

                def body(b, a):
                    find(b + 2)
                    dve.wait_ge(sig_done, b + 1)
                    v.tensor_tensor(sig[:, :], sig[:, :], ps_gu[:, 0:HID], ALU.mult).then_inc(half_hid, 1)
                    dve.wait_ge(half_hid, b + 1)
                    v.tensor_tensor(hid[:, :], sig[:, :], ps_gu[:, HID:2 * HID], ALU.mult).then_inc(hid_done, 1)
                    place_in(b + 2, a)
                    place_out(b + 1, 1 - a)

                for b in range(2):
                    find(b)
                    place_in(b, b)
                place_out(0, 0)
                blocks(dve, body)

            @block.scalar
            def _(act):
                def turn(b, a):
                    act.wait_ge(turned, b + 1)
                    nc.scalar.activation(rowsT[:, a, :], ps_x[:, :], ACT.Copy).then_inc(rowsT_done, 1)

                def body(b, a):
                    act.wait_ge(gu_done, b + 1)
                    nc.scalar.activation(sig[:, :], ps_gu[:, 0:HID], ACT.Sigmoid).then_inc(sig_done, 1)
                    turn(b + 1, 1 - a)
                    act.wait_ge(hid_turned, b + 1)
                    nc.scalar.activation(hidT[:, :], ps_h[:, 0:HID], ACT.Copy).then_inc(hidT_done, 1)
                    act.wait_ge(y_done, b + 1)
                    act.wait_ge(out_ready, b + 1)
                    nc.scalar.activation(res[:, a, :], ps_y[:, :], ACT.Copy, scale=wt[:, a, :]).then_inc(res_done, 1)

                turn(0, 0)
                blocks(act, body)

            @block.tensor
            def _(pe):
                ident = cst[:, C_ID:C_ID + P]

                def slots_of(b):
                    e = expert_of(pe, b)
                    pe.wait_ge(hot_done, b + 1)
                    wait(pe, copied, b)
                    for i in range(NT):
                        last = nc.tensor.matmul(ps_i[:, 0:4], hot[:, i, :], vals[:, i, bass.ds(e * 4, 4)], start=(i == 0), stop=(i == NT - 1))
                    last.then_inc(slots, 1)

                def turn(b, a):
                    pe.wait_ge(gathered[a], seen(b, a))
                    wait(pe, rowsT_done, b)
                    for k in range(KT):
                        last = nc.tensor.transpose(ps_x[:, k * P:(k + 1) * P], rows[:, a, k * P:(k + 1) * P], ident)
                    last.then_inc(turned, 1)

                def body(b, a):
                    pe.wait_ge(gu_in[a], seen(b, a, 32))
                    pe.wait_ge(rowsT_done, b + 1)
                    wait(pe, hid_done, b)
                    for k in range(KT):
                        last = nc.tensor.matmul(ps_gu[:, :], rowsT[:, a, k * P:(k + 1) * P], wgu[:, a, k, :], start=(k == 0), stop=(k == KT - 1))
                    last.then_inc(gu_done, 1)
                    turn(b + 1, 1 - a)
                    slots_of(b + 2)
                    pe.wait_ge(hid_done, b + 1)
                    for m in range(2):
                        last = nc.tensor.transpose(ps_h[:, m * P:(m + 1) * P], hid[:, m * P:(m + 1) * P], ident)
                    last.then_inc(hid_turned, 1)
                    pe.wait_ge(hidT_done, b + 1)
                    pe.wait_ge(dn_in[a], seen(b, a))
                    wait(pe, res_done, b)
                    for h in range(2):
                        for m in range(2):
                            last = nc.tensor.matmul(ps_y[:, h * BANK:(h + 1) * BANK], hidT[:, m * P:(m + 1) * P],
                                                    wd[:, a, m, h * BANK:(h + 1) * BANK], start=(m == 0), stop=(m == 1))
                    last.then_inc(y_done, 1)

                slots_of(0)
                slots_of(1)
                turn(0, 0)
                blocks(pe, body)


def combine(nc, A, g, layer, y_dram, gate):
    x = g["x"]
    with ExitStack() as es:
        y = es.enter_context(nc.sbuf_tensor("cb_y", [P, 2, TOP_K, D], F32))
        tot = es.enter_context(nc.sbuf_tensor("cb_sum", [P, D], F32))
        with stage(nc, "combine", "in0 in1 summed own used") as (block, in0, in1, summed, own, used):
            arrived = (in0, in1)

            @block.sync
            def _(sp):
                for i in range(NT):
                    if i >= 2:
                        sp.wait_ge(summed, i - 1)
                    sp.dma_start(y[:, i % 2, :, :], y_dram[i * P * TOP_K:(i + 1) * P * TOP_K, :].rearrange("(t k) d -> t k d", k=TOP_K)
                                 ).then_inc(arrived[i % 2], 16)

            @block.vector
            def _(dve):
                o = Own(dve, own)
                for i in range(NT):
                    s = 0 if i < NTX else 1
                    dve.wait_ge(arrived[i % 2], 16 * (i // 2 + 1))
                    if i:
                        dve.wait_ge(used, i)
                    nc.vector.tensor_reduce(tot[:, :], y[:, i % 2, :, :].rearrange("p k d -> p d k"), AX.X, ALU.add).then_inc(summed, 1)
                    dve.wait_ge(summed, i + 1)
                    o.then(nc.vector.tensor_tensor(tot[:, :], tot[:, :], gate[:, s, :], ALU.mult))
                    nc.vector.tensor_tensor(x[:, i, :], x[:, i, :], tot[:, :], ALU.add).then_inc(used, 1)


def moe(nc, A, g, layer, h_dram, y_dram):
    with ExitStack() as es:
        sb = lambda n, s, dt=F32: es.enter_context(nc.sbuf_tensor(f"moe_{n}", s, dt))
        gate = sb("gate", [P, 2, D])
        r = {"rank": sb("rank", [P, NT, N_EXP]), "vals": sb("vals", [P, NT, N_EXP * 4]), "first": sb("first", [P, N_SLOT_TAB]),
             "expert": sb("expert", [1, N_SLOT_TAB], I32), "n_i": sb("n_i", [1, 4], I32)}
        with nc.sbuf_tensor("h2T", [P, KT, TOK], F32) as hT:
            norm_rows(nc, A, g, layer, 3, "norm2_g", hT, h_dram)
            routing(nc, A, g, layer, hT, r)
            shared_expert(nc, A, g, layer, hT, gate)
        routed_experts(nc, A, g, layer, r, h_dram, y_dram)
        combine(nc, A, g, layer, y_dram, gate)


_INS = ("x c ctx c_ctx w_mod b_mod norm1_g norm2_g w_in w_out gqa_q_gain gqa_k_gain win_q_gain win_k_gain win_sink "
        "conv_dw_w conv_dw_b conv_ln_g conv_ln_b conv_pw_w conv_pw_b hgrn_lb_logits hgrn_onorm_g router_w router_bias "
        "exp_w_gate exp_w_up exp_w_down sh_w_gate sh_w_up sh_w_down").split()


def kernel(**inputs):
    import concourse.bacc as bacc
    from concourse.bass_utils import run_bass_kernel_spmd

    nc = bacc.Bacc("TRN2", target_bir_lowering=False, num_devices=1)
    arrays = {f"in_{n}": np.ascontiguousarray(inputs[n]) for n in _INS}
    arrays["in_consts"] = shape_constants()
    A = {n[3:]: nc.dram_tensor(n, a.shape, mybir.dt.from_np(a.dtype), kind="ExternalInput").ap() for n, a in arrays.items()}
    out = nc.dram_tensor("out", (1, SEQ, D), F32, kind="ExternalOutput").ap()
    build(nc, A, out)
    got = run_bass_kernel_spmd(nc, [arrays], core_ids=[0])
    return got.results[0]["out"]
```

```python
import concourse.bass as bass
from concourse import mybir
from contextlib import ExitStack, contextmanager
import numpy as np

F32 = mybir.dt.float32
I32 = mybir.dt.int32
BF16 = mybir.dt.bfloat16
U32 = mybir.dt.uint32
ALU = mybir.AluOpType
ACT = mybir.ActivationFunctionType
AX = mybir.AxisListType

P = 128
D = 1024
KT = D // P
SEQ = 512
CTX = 256
TOK = SEQ + CTX
NT = TOK // P
NTX = SEQ // P
NTC = CTX // P
DEPTH = 2
GRID_W = 64
HEAD = 64
N_Q = 4
N_KV = 2
GROUP = 256
D_IN = 2816
SCALE = HEAD ** -0.5
QK = (N_Q + N_KV) * HEAD
CONV_W = 31
PAD = CONV_W // 2
CONV_SPAN = PAD + SEQ + PAD + CTX + PAD
CONV_OUT = SEQ + PAD + CTX
N_EXP = 64
TOP_K = 8
N_GRP = 8
PER_GRP = N_EXP // N_GRP
HID = 256
ROUTED_SCALE = 2.5
EPS = 1e-6
LEVELS = 7
NEG = -1e30
BANK = 512

C_ID = 0
C_SEL = C_ID + P
C_PREV = C_SEL + 2 * P
C_NEXT = C_PREV + P
TILES_A_MASK = 3
_blocks = [TILES_A_MASK * P >> lev for lev in range(LEVELS)]
C_LEV = [[C_NEXT + P + d * sum(_blocks) + sum(_blocks[:lev]) for lev in range(LEVELS)] for d in range(2)]
C_TRI = C_NEXT + P + 2 * sum(_blocks)
C_IOTA = C_TRI + P
C_COL = C_IOTA + P
C_LOW = C_COL + 28
C_COS = C_LOW + 64
C_SIN = C_COS + NTX * HEAD
C_ALL = C_SIN + NTX * HEAD


def shape_constants():
    c = np.zeros((P, C_ALL), np.float32)
    r = np.arange(P)
    c[:, C_ID:C_ID + P] = np.eye(P)
    for j in range(4):
        for s in range(2):
            c[32 * j + s, C_SEL + s * P:C_SEL + (s + 1) * P] = 1.0
    c[:, C_PREV:C_PREV + P] = np.where(r[None, :] >= r[:, None], 0.0, -NEG)
    c[:, C_NEXT:C_NEXT + P] = np.where(r[None, :] <= r[:, None], 0.0, -NEG)
    for lev in range(LEVELS):
        n = 1 << lev
        for d in range(2):
            block = (np.arange(_blocks[lev]) % (P // (2 * n)))[None, :]
            c[:, C_LEV[d][lev]:C_LEV[d][lev] + _blocks[lev]] = (r[:, None] // (2 * n) == block) & (r[:, None] % (2 * n) // n == d)
    c[:, C_TRI:C_TRI + P] = r[:, None] < r[None, :]
    c[:, C_IOTA:C_IOTA + P] = r[None, :]
    c[:, C_COL] = 1.0
    c[:, C_COL + 1] = r
    c[:, C_COL + 2] = TOK + r
    c[:, C_COL + 10:C_COL + 10 + DEPTH - 1] = 1.0
    k8 = np.arange(N_GRP)
    c[:, C_LOW:C_LOW + 64] = (k8[None, :] < k8[:, None]).reshape(1, 64)
    for i in range(NT):
        c[:, C_COL + 16 + i] = (i * P + r) // 64 * 64
        c[:, C_COL + 22 + i] = r % 64
    freqs = HEAD // 4
    inv = np.power(10000.0, -np.arange(freqs, dtype=np.float32) / freqs).astype(np.float32)
    for i in range(NTX):
        t = i * P + r
        for ax, pos in enumerate((t // GRID_W, t % GRID_W)):
            ang = pos.astype(np.float32)[:, None] * inv[None, :]
            at = i * HEAD + ax * 2 * freqs
            c[:, C_COS + at:C_COS + at + freqs] = np.cos(ang)
            c[:, C_COS + at + freqs:C_COS + at + 2 * freqs] = np.cos(ang)
            c[:, C_SIN + at:C_SIN + at + freqs] = -np.sin(ang)
            c[:, C_SIN + at + freqs:C_SIN + at + 2 * freqs] = np.sin(ang)
    return c


@contextmanager
def stage(nc, name, sem_names, kept=()):
    sems = [nc.alloc_semaphore(name=f"{name}_{s}") for s in sem_names.split()]
    with nc.Block(name) as block:
        yield (block, *sems)
    numbers = sorted(s.num for s in (*sems, *kept))
    first = [n for n in numbers if n - 1 not in numbers]
    last = [n for n in numbers if n + 1 not in numbers]
    for a, b in zip(first, last):
        nc.all_engine_barrier(sems_to_clear=range(a, b + 1))
    for s in sems:
        nc.release_semaphore(s)


class Own:

    def __init__(self, eng, sem):
        self.eng, self.sem, self.n = eng, sem, 0

    def __call__(self, ins):
        ins.then_inc(self.sem, 1)
        self.n += 1
        return ins

    def settle(self):
        self.eng.wait_ge(self.sem, self.n)

    def then(self, ins):
        self(ins)
        self.settle()


def build(nc, A, out):
    with ExitStack() as es:
        def sb(name, shape, dt=F32, stack=es):
            return stack.enter_context(nc.sbuf_tensor(name, shape, dt))

        g = {}
        g["x"] = sb("x_res", [P, NT, D])
        g["cst"] = sb("cst", [P, C_ALL])
        g["cT"] = sb("cT", [P, KT, 2])
        g["lb"] = sb("lb", [P, DEPTH, 3, 4])
        g["mods"] = sb("mods", [P, 3, BANK])
        h_dram = nc.dram_tensor("h_rows", (TOK, D), F32).ap()
        y_dram = nc.dram_tensor("expert_sums", (TOK + P, D), F32).ap()
        g["rows_sems"] = [nc.alloc_semaphore(name=n) for n in ("gathered0", "gathered1", "scattered0", "scattered1")]
        prologue(nc, A, g)
        with nc.Fori(0, DEPTH) as layer:
            modulation(nc, A, g, layer)
            with ExitStack() as mix:
                g["pt"] = sb("p_tok", [P, NT, 1536], stack=mix)
                g["pf"] = sb("p_feat", [P, 10, TOK], stack=mix)
                g["cum"] = sb("log_gate_sums", [P, 2, 2, NT, P + 1], stack=mix)
                with nc.sbuf_tensor("hT", [P, KT, TOK], F32) as hT:
                    norm_rows(nc, A, g, layer, 0, "norm1_g", hT, None)
                    projections(nc, A, g, layer, hT)
                g["yT"] = sb("yT", [P, KT, TOK], stack=mix)
                attention(nc, A, g, layer)
                convolution(nc, A, g, layer)
                recurrence(nc, A, g, layer)
                out_projection(nc, A, g, layer)
            moe(nc, A, g, layer, h_dram, y_dram)
        with stage(nc, "store", "stored") as (block, stored):
            @block.sync
            def _(sp):
                sp.dma_start(out[0].rearrange("(t p) d -> p t d", p=P), g["x"][:, 0:NTX, :]).then_inc(stored, 16)
                sp.wait_ge(stored, 16)


def prologue(nc, A, g):
    x, cst, cT, lb = g["x"], g["cst"], g["cT"], g["lb"]
    with ExitStack() as es:
        craw = es.enter_context(nc.sbuf_tensor("craw", [P, KT, 2], F32))
        csig = es.enter_context(nc.sbuf_tensor("csig", [P, KT, 2], F32))
        lg = es.enter_context(nc.sbuf_tensor("lg", [P, DEPTH, 4], F32))
        mx = es.enter_context(nc.sbuf_tensor("lg_max", [P, 4], F32))
        den = es.enter_context(nc.sbuf_tensor("lg_den", [P, 4], F32))
        with stage(nc, "prologue", "loaded streams acted own ready") as (block, loaded, streams, acted, own, ready):
            @block.sync
            def _(sp):
                sp.dma_start(craw[:, :, 0], A["c"][0].rearrange("(k p) -> p k", p=P),
                             allow_slow_non_contiguous=True).then_inc(loaded, 16)
                sp.dma_start(craw[:, :, 1], A["c_ctx"].rearrange("(k p) -> p k", p=P),
                             allow_slow_non_contiguous=True).then_inc(loaded, 16)
                for l in range(DEPTH):
                    for d in range(2):
                        sp.dma_start(lg[:, l, 2 * d:2 * d + 2],
                                     A["hgrn_lb_logits"][d, l].rearrange("(g p) -> p g", p=P),
                                     allow_slow_non_contiguous=True).then_inc(loaded, 16)
                sp.dma_start(cst[:, :], A["consts"]).then_inc(streams, 16)
                sp.dma_start(x[:, 0:NTX, :], A["x"][0].rearrange("(t p) d -> p t d", p=P)).then_inc(streams, 16)
                sp.dma_start(x[:, NTX:NT, :], A["ctx"][0].rearrange("(t p) d -> p t d", p=P)).then_inc(streams, 16)
                sp.wait_ge(streams, 48)

            @block.scalar
            def _(act):
                act.wait_ge(loaded, 96)
                nc.scalar.activation(csig[:, :, :], craw[:, :, :], ACT.Sigmoid).then_inc(acted, 1)
                act.wait_ge(ready, 1)
                nc.scalar.activation(lg[:, :, :], lg[:, :, :], ACT.Exp).then_inc(acted, 1)
                act.wait_ge(ready, 2)
                nc.scalar.activation(lb[:, :, 1, :], lb[:, :, 1, :], ACT.Ln).then_inc(acted, 1)

            @block.vector
            def _(dve):
                o = Own(dve, own)
                dve.wait_ge(loaded, 96)
                o.then(nc.vector.tensor_tensor(mx[:, :], lg[:, 0, :], lg[:, 1, :], ALU.max))
                o(nc.vector.tensor_tensor(lg[:, 0, :], lg[:, 0, :], mx[:, :], ALU.subtract))
                nc.vector.tensor_tensor(lg[:, 1, :], lg[:, 1, :], mx[:, :], ALU.subtract).then_inc(ready, 1)
                dve.wait_ge(acted, 2)
                o(nc.vector.tensor_tensor(cT[:, :, :], craw[:, :, :], csig[:, :, :], ALU.mult))
                o.then(nc.vector.tensor_tensor(den[:, :], lg[:, 0, :], lg[:, 1, :], ALU.add))
                o.then(nc.vector.reciprocal(den[:, :], den[:, :]))
                o(nc.vector.tensor_tensor(lg[:, 0, :], lg[:, 0, :], den[:, :], ALU.mult))
                o.then(nc.vector.tensor_tensor(lg[:, 1, :], lg[:, 1, :], den[:, :], ALU.mult))
                o(nc.vector.memset(lb[:, 0, 0, :], 0.0))
                o.then(nc.vector.tensor_tensor(lb[:, 1, 0, :], lg[:, 0, :], lg[:, 1, :], ALU.add))
                o.then(nc.vector.tensor_tensor(lb[:, 1, 0, :], lb[:, 1, 0, :], lg[:, 0, :], ALU.subtract))
                o(nc.vector.tensor_scalar(lb[:, :, 2, :], lb[:, :, 0, :], -1.0, 1.0, ALU.mult, ALU.add))
                nc.vector.tensor_scalar(lb[:, :, 1, :], lb[:, :, 0, :], 1e-18, None, ALU.max).then_inc(ready, 1)
                o.then(nc.vector.tensor_scalar(lg[:, :, :], lb[:, :, 0, :], 0.0, NEG, ALU.is_equal, ALU.mult))
                dve.wait_ge(acted, 3)
                nc.vector.tensor_tensor(lb[:, :, 1, :], lb[:, :, 1, :], lg[:, :, :], ALU.add).then_inc(ready, 1)


def modulation(nc, A, g, layer):
    cT, cst, mods = g["cT"], g["cst"], g["mods"]
    NBUF, CH = 3, 12
    with ExitStack() as es:
        w = es.enter_context(nc.sbuf_tensor("w_mod_t", [P, NBUF, 6 * D], F32))
        b = es.enter_context(nc.sbuf_tensor("b_mod_t", [1, 6 * D], F32))
        one = es.enter_context(nc.sbuf_tensor("one_row", [1, 2], F32))
        ps = es.enter_context(nc.psum_tensor("mod_ps", [P, 3, BANK], F32))
        with stage(nc, "mod", "w0 w1 w2 bias w_used ones summed kept") as (block, w0, w1, w2, bias, w_used, ones, summed, kept):
            w_in = (w0, w1, w2)

            @block.sync
            def _(sp):
                sp.dma_start(b[:, :], A["b_mod"][bass.ds(layer, 1), :]).then_inc(bias, 16)
                for k in range(KT):
                    if k >= NBUF:
                        sp.wait_ge(w_used, k - NBUF + 1)
                    sp.dma_start(w[:, k % NBUF, :],
                                 A["w_mod"][bass.ds(layer, 1), k * P:(k + 1) * P, :].rearrange("a p n -> (a p) n")
                                 ).then_inc(w_in[k % NBUF], 16)

            @block.vector
            def _(dve):
                nc.vector.memset(one[:, :], 1.0).then_inc(ones, 1)
                dve.wait_ge(summed, 1)
                for j in range(4):
                    nc.vector.tensor_copy(mods[32 * j:32 * j + 2, :, :], ps[32 * j:32 * j + 2, :, :]).then_inc(kept, 1)

            @block.tensor
            def _(pe):
                for k in range(KT):
                    pe.wait_ge(w_in[k % NBUF], 16 * (k // NBUF + 1))
                    for c in range(CH):
                        last = nc.tensor.matmul(ps[32 * (c % 4):32 * (c % 4) + 2, c // 4, :], cT[:, k, :],
                                                w[:, k % NBUF, c * BANK:(c + 1) * BANK], start=(k == 0), stop=False)
                    last.then_inc(w_used, 1)
                pe.wait_ge(bias, 16)
                pe.wait_ge(ones, 1)
                for c in range(CH):
                    last = nc.tensor.matmul(ps[32 * (c % 4):32 * (c % 4) + 2, c // 4, :], one[0:1, :],
                                            b[0:1, c * BANK:(c + 1) * BANK], start=False, stop=True)
                last.then_inc(summed, 1)


def broadcast_row(nc, g, ps, kind, stream):
    cst, mods = g["cst"], g["mods"]
    for h in range(2):
        c = 2 * kind + h
        j = 32 * (c % 4)
        last = nc.tensor.matmul(ps[:, h * BANK:(h + 1) * BANK], cst[j:j + 2, C_SEL + stream * P:C_SEL + (stream + 1) * P],
                                mods[j:j + 2, c // 4, :], start=True, stop=True)
    return last


def norm_rows(nc, A, g, layer, kind, gain, hT, h_dram):
    x, cst = g["x"], g["cst"]
    with ExitStack() as es:
        gr = es.enter_context(nc.sbuf_tensor(f"gain_row{kind}", [P, D], F32))
        mul = es.enter_context(nc.sbuf_tensor(f"mul_row{kind}", [P, 2, D], F32))
        add = es.enter_context(nc.sbuf_tensor(f"add_row{kind}", [P, 2, D], F32))
        h = es.enter_context(nc.sbuf_tensor(f"h_tok{kind}", [P, 2, D], F32))
        sq = es.enter_context(nc.sbuf_tensor(f"h_sq{kind}", [P, D], F32))
        ss = es.enter_context(nc.sbuf_tensor(f"h_ss{kind}", [P, NT], F32))
        rs = es.enter_context(nc.sbuf_tensor(f"h_rstd{kind}", [P, NT], F32))
        pr = es.enter_context(nc.psum_tensor(f"row_ps{kind}", [P, 2, 2 * BANK], F32))
        pt = es.enter_context(nc.psum_tensor(f"hT_ps{kind}", [P, 2, 2 * BANK], F32))
        names = "gain_in spread rows own squared varied rooted h_ready turned kept stored0 stored1"
        with stage(nc, f"norm{kind}", names) as (block, gain_in, spread, rows, own, squared, varied, rooted, h_ready,
                                                 turned, kept, stored0, stored1):
            stored = (stored0, stored1)

            @block.sync
            def _(sp):
                sp.dma_start(gr[:, :], A[gain][bass.ds(layer, 1), :].broadcast_to([P, D])).then_inc(gain_in, 16)
                if h_dram is not None:
                    for i in range(NT):
                        sp.wait_ge(h_ready, i + 1)
                        sp.dma_start(h_dram[i * P:(i + 1) * P, :], h[:, i % 2, :]).then_inc(stored[i % 2], 16)
                    for a in range(2):
                        sp.wait_ge(stored[a], 16 * NT // 2)

            @block.tensor
            def _(pe):
                for n, (kd, s) in enumerate(((kind + 1, 0), (kind + 1, 1), (kind, 0), (kind, 1))):
                    if n >= 2:
                        pe.wait_ge(rows, n - 1)
                    broadcast_row(nc, g, pr[:, n % 2, :], kd, s).then_inc(spread, 1)
                for i in range(NT):
                    pe.wait_ge(h_ready, i + 1)
                    if i >= 2:
                        pe.wait_ge(kept, i - 1)
                    for k in range(KT):
                        last = nc.tensor.transpose(pt[:, i % 2, k * P:(k + 1) * P], h[:, i % 2, k * P:(k + 1) * P],
                                                   cst[:, C_ID:C_ID + P])
                    last.then_inc(turned, 1)

            @block.scalar
            def _(act):
                for i in range(NT):
                    if i:
                        act.wait_ge(squared, i)
                    nc.scalar.activation(sq[:, :], x[:, i, :], ACT.Square, accum_out=ss[:, i:i + 1]).then_inc(squared, 1)
                act.wait_ge(varied, 1)
                nc.scalar.activation(rs[:, :], rs[:, :], ACT.Sqrt).then_inc(rooted, 1)
                for i in range(NT):
                    act.wait_ge(turned, i + 1)
                    nc.scalar.activation(hT[:, :, i * P:(i + 1) * P],
                                         pt[:, i % 2, :].rearrange("p (k t) -> p k t", t=P), ACT.Copy).then_inc(kept, 1)

            @block.vector
            def _(dve):
                o = Own(dve, own)
                dve.wait_ge(gain_in, 16)
                for s in range(2):
                    dve.wait_ge(spread, s + 1)
                    nc.vector.scalar_tensor_tensor(mul[:, s, :], pr[:, s, :], 1.0, gr[:, :], ALU.add, ALU.mult).then_inc(rows, 1)
                for s in range(2):
                    dve.wait_ge(spread, s + 3)
                    nc.vector.tensor_copy(add[:, s, :], pr[:, s, :]).then_inc(rows, 1)
                dve.wait_ge(squared, NT)
                nc.vector.tensor_scalar(rs[:, :], ss[:, :], 1.0 / D, EPS, ALU.mult, ALU.add).then_inc(varied, 1)
                dve.wait_ge(rooted, 1)
                dve.wait_ge(rows, 4)
                o.then(nc.vector.reciprocal(rs[:, :], rs[:, :]))
                for i in range(NT):
                    s = 0 if i < NTX else 1
                    if i >= 2:
                        dve.wait_ge(turned, i - 1)
                        if h_dram is not None:
                            dve.wait_ge(stored[i % 2], 16 * (i // 2))
                    o.then(nc.vector.scalar_tensor_tensor(h[:, i % 2, :], x[:, i, :], rs[:, i:i + 1], mul[:, s, :], ALU.mult, ALU.mult))
                    nc.vector.tensor_tensor(h[:, i % 2, :], h[:, i % 2, :], add[:, s, :], ALU.add).then_inc(h_ready, 1)


def projections(nc, A, g, layer, hT):
    pt, pf = g["pt"], g["pf"]
    CW = 256
    CHUNKS = ([(1024 + CW * j, "f", 2 * j) for j in range(2)] + [(2048 + CW * j, "f", 6 + 2 * j) for j in range(2)]
              + [(1536, "f", 4)] + [(CW * j, "t", CW * j) for j in (2, 3, 0, 1)] + [(1792, "t", 1024), (2560, "t", 1280)])
    turned_heads = lambda ap: ap.rearrange("p (b a d) -> p a b d", a=2, b=2)
    jobs = []
    for c, (c0, kind, at) in enumerate(CHUNKS):
        if kind == "t":
            jobs += [(c, kind, 0, CW, pt[:, i, at:at + CW], i * P) for i in range(NT)]
        else:
            jobs += [(c, kind, P * j, tw, pf[:, at + j, t0:t0 + tw], t0) for j in range(2) for t0, tw in ((0, SEQ), (SEQ, CTX))]
    CONV_IN, GATES_IN = 8, 16
    HEADS_IN = (44, 32)
    GATE_STEPS = [29, 31, 33, 36, 38, 40]
    ROOT_STEPS = (48, 42)
    with ExitStack() as es:
        sb = lambda n, s: es.enter_context(nc.sbuf_tensor(f"proj_{n}", s, F32))
        w = sb("w", [P, 2, KT, CW])
        gate_tmp = sb("gate_tmp", [P, 4 * 2 * TOK])
        scratch = [gate_tmp[:, j * 2 * TOK:(j + 1) * 2 * TOK].rearrange("p (g t) -> p g t", g=2) for j in range(4)]
        lbl = sb("lbl", [P, 3, 4])
        hp = sb("hp", [P, 2, CONV_SPAN])
        dw = sb("dw", [P, 2, CONV_W])
        dwb = sb("dwb", [P, 2])
        squares = [gate_tmp[:, 0:NT * QK].rearrange("p (t c) -> p t c", t=NT), sb("sq", [P, NT, QK])]
        gain, rs = ([sb(f"{n}{win}", s) for win in range(2)] for n, s in (
            ("gain", [P, N_Q + N_KV, HEAD]), ("rs", [P, NT * (N_Q + N_KV)])))
        ps = es.enter_context(nc.psum_tensor("p_ps", [P, 8, BANK], F32))
        names = "w0 w1 w_used done kept taps_in gated gains0 gains1 varied0 varied1 rooted0 rooted1 inverted1 own_p own own_a exp_arg first_ln diff lse_ln k_arg k_exp"
        with stage(nc, "proj", names) as (block, w0, w1, w_used, done, kept, taps_in, gated, gains0, gains1, varied0, varied1,
                                          rooted0, rooted1, inverted1, own_p, own, own_a, exp_arg, first_ln, diff, lse_ln, k_arg, k_exp):
            gains_in, varied, rooted = (gains0, gains1), (varied0, varied1), (rooted0, rooted1)
            w_in = (w0, w1)

            @block.sync
            def _(sp):
                for c, (c0, _, _) in enumerate(CHUNKS):
                    if c >= 2:
                        sp.wait_ge(w_used, c - 1)
                    sp.dma_start(w[:, c % 2, :, :], A["w_in"][bass.ds(layer, 1), :, c0:c0 + CW].rearrange("a (k p) n -> p (a k) n", p=P)
                                 ).then_inc(w_in[c % 2], 16)
                    if c == 1:
                        for h in range(2):
                            sp.dma_start(dw[:, h, :], A["conv_dw_w"][bass.ds(layer, 1), :, h * P:(h + 1) * P].rearrange("a k p -> p (a k)"),
                                         allow_slow_non_contiguous=True).then_inc(taps_in, 16)
                        sp.dma_start(dwb[:, :], A["conv_dw_b"][bass.ds(layer, 1), :].rearrange("a (c p) -> p (a c)", p=P),
                                     allow_slow_non_contiguous=True).then_inc(taps_in, 16)
                        for win, names in enumerate((("gqa_q_gain", "gqa_k_gain"), ("win_q_gain", "win_k_gain"))):
                            for h in range(N_Q + N_KV):
                                sp.dma_start(gain[win][:, h, :], A[names[h >= N_Q]][bass.ds(layer, 1), :].broadcast_to([P, HEAD])
                                             ).then_inc(gains_in[win], 16)

            @block.tensor
            def _(pe):
                for n, (c, kind, col, width, dst, t0) in enumerate(jobs):
                    if n == 0 or jobs[n - 1][0] != c:
                        pe.wait_ge(w_in[c % 2], 16 * (c // 2 + 1))
                    if n >= 8:
                        pe.wait_ge(kept, n - 7)
                    for k in range(KT):
                        if kind == "t":
                            last = nc.tensor.matmul(ps[:, n % 8, 0:width], hT[:, k, t0:t0 + P], w[:, c % 2, k, :], start=(k == 0), stop=(k == KT - 1))
                        else:
                            last = nc.tensor.matmul(ps[:, n % 8, 0:width], w[:, c % 2, k, col:col + P], hT[:, k, t0:t0 + width],
                                                    start=(k == 0), stop=(k == KT - 1))
                    last.then_inc(done, 1)
                    if n + 1 == len(jobs) or jobs[n + 1][0] != c:
                        pe.wait_ge(done, n + 1)
                        pe.sem_inc(w_used, 1)

            @block.scalar
            def _(act):
                for n, job in enumerate(jobs):
                    act.wait_ge(done, n + 1)
                    dst, src = job[4], ps[:, n % 8, 0:job[3]]
                    if job[1] == "t" and CHUNKS[job[0]][0] in (0, 2 * CW):
                        dst, src = turned_heads(dst), src.rearrange("p (a b d) -> p a b d", a=2, b=2)
                    nc.scalar.activation(dst, src, ACT.Copy).then_inc(kept, 1)
                    if n + 1 == CONV_IN:
                        act.wait_ge(kept, CONV_IN)
                        nc.scalar.activation(pf[:, 2:4, :], pf[:, 2:4, :], ACT.Sigmoid).then_inc(gated, 1)
                    if n in GATE_STEPS:
                        gates_scalar(act, pf, scratch, GATE_STEPS.index(n), (own_a, exp_arg, first_ln, diff, lse_ln, k_arg, k_exp))
                    if n in ROOT_STEPS:
                        win = ROOT_STEPS.index(n)
                        act.wait_ge(varied[win], 1)
                        nc.scalar.activation(rs[win][:, :], rs[win][:, :], ACT.Sqrt).then_inc(rooted[win], 1)

            @block.gpsimd
            def _(pool):
                pool.wait_ge(kept, HEADS_IN[1])
                heads_ready(nc.gpsimd, pool, Own(pool, own_p), pt, g["cst"], 1, squares[1], gain[1], rs[1], (gains1, varied1, inverted1), False)

            @block.vector
            def _(dve):
                o = Own(dve, own)
                depthwise(nc.vector, dve, o, pf, hp, dw, dwb, (gated, taps_in))
                dve.wait_ge(kept, GATES_IN)
                gates_vector(nc.vector, dve, o, layer, g["lb"], lbl, pf, g["cst"], g["cum"], scratch, (exp_arg, first_ln, diff, lse_ln, k_arg, k_exp))
                dve.wait_ge(rooted1, 1)
                nc.vector.reciprocal(rs[1][:, :], rs[1][:, :]).then_inc(inverted1, 1)
                dve.wait_ge(kept, HEADS_IN[0])
                heads_ready(nc.vector, dve, o, pt, g["cst"], 0, squares[0], gain[0], rs[0], (gains0, varied0, rooted0), True)


def heads_ready(v, eng, o, pt, cst, win, squares, gain, rs, sems, on_vector):
    gains_in, varied, rooted = sems
    NH = N_Q + N_KV
    half = HEAD // 4
    c0 = 512 * win
    qk = pt[:, :, c0:c0 + QK]
    heads = lambda ap: ap.rearrange("p t (h d) -> p t h d", d=HEAD)
    by_head = rs[:, :].rearrange("p (t h o) -> p t h o", h=NH, o=1).broadcast_to([P, NT, NH, HEAD])
    o.then(v.tensor_tensor(squares[:, :, :], qk, qk, ALU.mult))
    if on_vector:
        o.then(v.tensor_reduce(rs[:, :], squares[:, :, :].rearrange("p t (h d) -> p (t h) d", d=HEAD), AX.X, ALU.add))
    else:
        by = squares[:, :, :].rearrange("p t (h d) -> p (t h) d", d=HEAD)
        w = HEAD // 2
        while w > 1:
            o.then(v.tensor_tensor(by[:, :, 0:w], by[:, :, 0:w], by[:, :, w:2 * w], ALU.add))
            w //= 2
        o.then(v.tensor_tensor(rs[:, :].rearrange("p (n o) -> p n o", o=1), by[:, :, 0:1], by[:, :, 1:2], ALU.add))
    v.tensor_scalar(rs[:, :], rs[:, :], 1.0 / HEAD, EPS, ALU.mult, ALU.add).then_inc(varied, 1)
    eng.wait_ge(gains_in, 16 * NH)
    o.then(v.tensor_scalar(gain[:, N_Q:NH, :], gain[:, N_Q:NH, :], -SCALE, None, ALU.mult))
    o.then(v.tensor_tensor(heads(qk), heads(qk), gain[:, :, :].rearrange("p (o h) d -> p o h d", o=1).broadcast_to([P, NT, NH, HEAD]), ALU.mult))
    eng.wait_ge(rooted, 1)
    if on_vector:
        o.then(v.reciprocal(rs[:, :], rs[:, :]))
    o.then(v.tensor_tensor(heads(qk), heads(qk), by_head, ALU.mult))
    for i in range(NTX):
        part = lambda ap, a: ap.rearrange("p (h x a f) -> p h x a f", x=2, a=2, f=half)[:, :, :, a, :]
        sin = cst[:, C_SIN + i * HEAD:C_SIN + (i + 1) * HEAD].rearrange("p (o x a f) -> p o x a f", o=1, x=2, a=2)
        for a in range(2):
            o(v.tensor_tensor(part(squares[:, i, :], a), part(qk[:, i, :], 1 - a), sin[:, :, :, a, :].broadcast_to([P, NH, 2, half]), ALU.mult))
    o.settle()
    cos = cst[:, C_COS:C_COS + NTX * HEAD].rearrange("p (t o d) -> p t o d", t=NTX, o=1).broadcast_to([P, NTX, NH, HEAD])
    o.then(v.tensor_tensor(heads(qk[:, 0:NTX, :]), heads(qk[:, 0:NTX, :]), cos, ALU.mult))
    o.then(v.tensor_tensor(qk[:, 0:NTX, :], qk[:, 0:NTX, :], squares[:, 0:NTX, :], ALU.add))


def attention(nc, A, g, layer):
    pt, cst, yT = g["pt"], g["cst"], g["yT"]

    def vals(win, j, kv):
        return pt[:, j, 512 * win + QK + kv * HEAD:512 * win + QK + (kv + 1) * HEAD]

    units = []
    for win in range(2):
        for i in range(NT):
            if i >= NTX:
                keys = list(range(NTX, NT))
            elif win:
                keys = list(range(max(0, i - 1), min(NTX, i + 2))) + list(range(NTX, NT))
            else:
                keys = list(range(NT))
            for h in range(N_Q):
                units.append((win, i, h, keys))
    NU = len(units)
    exps = lambda n: n + max(0, n - NU // 2)

    def runs(keys):
        out = []
        for n, j in enumerate(keys):
            if out and out[-1][1] + out[-1][2] == j and (n * P) % BANK:
                out[-1][2] += 1
            else:
                out.append([n * P, j, 1])
        return out

    LAG_TURN, LAG_MIX, LAG_OUT = 2, 3, 4
    with ExitStack() as es:
        sb = lambda n, s: es.enter_context(nc.sbuf_tensor(f"at_{n}", s, F32))
        qT = sb("qT", [P, 2, 2, TOK])
        kT = sb("kT", [P, 2, TOK])
        prob = sb("prob", [P, 3, NT, P])
        probT = sb("probT", [P, 2, NT, 2, P])
        low = sb("low", [P, NU])
        den = sb("den", [P, NU])
        snk = sb("snk", [P, N_Q])
        esnk = sb("esnk", [P, NU])
        ps_s = es.enter_context(nc.psum_tensor("at_ps_s", [P, 2, 2 * BANK], F32))
        ps_t = es.enter_context(nc.psum_tensor("at_ps_t", [P, 2 * BANK], F32))
        ps_o = es.enter_context(nc.psum_tensor("at_ps_o", [HEAD, 2, BANK], F32))
        names = "sink_in turned kept own scored bounded exped normal spread spread_kept mixed mixed_kept"
        with stage(nc, "attn", names) as (block, sink_in, turned, kept, own, scored, bounded, exped, normal, spread, spread_kept, mixed,
                                          mixed_kept):
            @block.sync
            def _(sp):
                sp.dma_start(snk[:, :], A["win_sink"][bass.ds(layer, 1), :].broadcast_to([P, N_Q])).then_inc(sink_in, 16)

            @block.vector
            def _(dve):
                v = nc.vector
                o = Own(dve, own)
                dve.wait_ge(sink_in, 16)
                o.then(v.tensor_scalar(snk[:, :], snk[:, :], -1.0, None, ALU.mult))
                for n in range(NU + 1):
                    if n < NU:
                        win, i, h, keys = units[n]
                        dve.wait_ge(scored, n + 1)
                        bound = v.tensor_reduce(low[:, n:n + 1], ps_s[:, n % 2, 0:len(keys) * P], AX.X, ALU.min)
                        if win:
                            o.then(bound)
                            bound = v.tensor_tensor(low[:, n:n + 1], low[:, n:n + 1], snk[:, h:h + 1], ALU.min)
                        bound.then_inc(bounded, 1)
                    if n:
                        m = n - 1
                        win, i, h, keys = units[m]
                        dve.wait_ge(exped, exps(m + 1))
                        if win:
                            o.then(v.tensor_tensor(den[:, m:m + 1], den[:, m:m + 1], esnk[:, m:m + 1], ALU.add))
                        o.then(v.reciprocal(den[:, m:m + 1], den[:, m:m + 1]))
                        p_m = prob[:, m % 3, 0:len(keys), :]
                        v.tensor_scalar(p_m, p_m, den[:, m:m + 1], None, ALU.mult).then_inc(normal, 1)

            @block.scalar
            def _(act):
                for b in range(12):
                    act.wait_ge(turned, b + 1)
                    win, (t0, tw) = b // 6, ((0, SEQ), (SEQ, CTX))[b // 3 % 2]
                    dst = (qT[:, win, 0, t0:t0 + tw], qT[:, win, 1, t0:t0 + tw], kT[:, win, t0:t0 + tw])[b % 3]
                    nc.scalar.activation(dst, ps_s[:, b % 2, 0:tw], ACT.Copy).then_inc(kept, 1)
                act.wait_ge(own, 1)
                for n in range(NU + LAG_OUT):
                    m = n - LAG_TURN
                    if 0 <= m < NU:
                        nk = len(units[m][3])
                        act.wait_ge(spread, m + 1)
                        if m >= 4:
                            act.wait_ge(mixed, m // 2 - 1)
                        nc.scalar.activation(probT[:, m // 2 % 2, 0:nk, m % 2, :], ps_t[:, 0:nk * P].rearrange("p (a b) -> p a b", b=P),
                                             ACT.Copy).then_inc(spread_kept, 1)
                    if n < NU:
                        win, i, h, keys = units[n]
                        act.wait_ge(bounded, n + 1)
                        if n >= 3:
                            act.wait_ge(spread, n - 2)
                        nc.scalar.activation(prob[:, n % 3, 0:len(keys), :].rearrange("p a b -> p (a b)"), ps_s[:, n % 2, 0:len(keys) * P],
                                             ACT.Exp, bias=low[:, n:n + 1], scale=-1.0, accum_out=den[:, n:n + 1]).then_inc(exped, 1)
                        if win:
                            nc.scalar.activation(esnk[:, n:n + 1], snk[:, h:h + 1], ACT.Exp, bias=low[:, n:n + 1], scale=-1.0).then_inc(exped, 1)
                    m = n - LAG_OUT
                    if m >= 0 and m % 2:
                        win, i, h, _ = units[m]
                        act.wait_ge(mixed, m // 2 + 1)
                        for b in range(2):
                            nc.scalar.activation(yT[HEAD * b:HEAD * b + HEAD, 4 * win + h // 2, i * P:(i + 1) * P],
                                                 ps_o[:, m // 2 % 2, b * P:(b + 1) * P], ACT.Copy).then_inc(mixed_kept, 1)

            @block.tensor
            def _(pe):
                ident = cst[:, C_ID:C_ID + P]
                for b in range(12):
                    if b >= 2:
                        pe.wait_ge(kept, b - 1)
                    win, tiles = b // 6, (range(NTX), range(NTX, NT))[b // 3 % 2]
                    c = 512 * win + (b % 3) * P
                    for n, i in enumerate(tiles):
                        last = nc.tensor.transpose(ps_s[:, b % 2, n * P:(n + 1) * P], pt[:, i, c:c + P], ident)
                    last.then_inc(turned, 1)
                pe.wait_ge(kept, 12)

                def scores(n):
                    win, i, h, keys = units[n]
                    kv, pair = h // 2, h % 2
                    part = slice(HEAD * kv, HEAD * kv + HEAD)
                    if n >= 2:
                        pe.wait_ge(exped, exps(n - 1))
                    for c, j, m in runs(keys):
                        masked = [t for t in range(j, j + m) if win and i < NTX and t < NTX and abs(t - i) == 1]
                        last = nc.tensor.matmul(ps_s[:, n % 2, c:c + m * P], qT[part, win, pair, i * P:(i + 1) * P],
                                                kT[part, win, j * P:(j + m) * P], start=True, stop=True)
                        for t in masked:
                            cm = C_PREV if t < i else C_NEXT
                            cc = c + (t - j) * P
                            last = nc.tensor.matmul(ps_s[:, n % 2, cc:cc + P], ident, cst[:, cm:cm + P], start=False,
                                                    stop=t == masked[-1], skip_group_check=True)
                    last.then_inc(scored, 1)

                for n in range(NU + LAG_MIX):
                    if n < NU:
                        scores(n)
                    m = n - LAG_TURN
                    if 0 <= m < NU:
                        pe.wait_ge(normal, m + 1)
                        if m:
                            pe.wait_ge(spread_kept, m)
                        for a in range(len(units[m][3])):
                            last = nc.tensor.transpose(ps_t[:, a * P:(a + 1) * P], prob[:, m % 3, a, :], ident)
                        last.then_inc(spread, 1)
                    m = n - LAG_MIX
                    if m >= 0 and m % 2:
                        win, i, h, keys = units[m]
                        pe.wait_ge(spread_kept, m + 1)
                        if m >= 5:
                            pe.wait_ge(mixed_kept, 2 * (m // 2 - 1))
                        for a, j in enumerate(keys):
                            last = nc.tensor.matmul(ps_o[:, m // 2 % 2, 0:2 * P], vals(win, j, h // 2),
                                                    probT[:, m // 2 % 2, a, :, :].rearrange("p b q -> p (b q)"),
                                                    start=(a == 0), stop=(a == len(keys) - 1))
                        last.then_inc(mixed, 1)


def convolved_rows(pf):
    return pf[:, 0:4, :].rearrange("p a t -> p (a t)")[:, 0:2 * CONV_OUT].rearrange("p (a t) -> p a t", a=2)


def depthwise(v, dve, o, pf, hp, dw, dwb, sems):
    gated, taps_in = sems
    acc, L = convolved_rows(pf), CONV_OUT
    o.then(v.memset(hp[:, :, :], 0.0))
    dve.wait_ge(gated, 1)
    for (a, w), t0 in zip(((0, SEQ), (SEQ + PAD, CTX)), (0, SEQ)):
        o(v.tensor_tensor(hp[:, :, PAD + a:PAD + a + w], pf[:, 0:2, t0:t0 + w], pf[:, 2:4, t0:t0 + w], ALU.mult))
    o.settle()
    dve.wait_ge(taps_in, 16 * 3)
    for c in range(2):
        o(v.tensor_scalar(acc[:, c, :], hp[:, c, 0:L], dw[:, c, 0:1], dwb[:, c:c + 1], ALU.mult, ALU.add))
    for k in range(1, CONV_W):
        for c in range(2):
            dve.wait_ge(o.sem, o.n - 1)
            o(v.scalar_tensor_tensor(acc[:, c, :], hp[:, c, k:k + L], dw[:, c, k:k + 1], acc[:, c, :], ALU.mult, ALU.add))
    o.settle()


def convolution(nc, A, g, layer):
    pf, cst, yT = g["pf"], g["cst"], g["yT"]
    acc = convolved_rows(pf)
    with ExitStack() as es:
        sb = lambda n, s: es.enter_context(nc.sbuf_tensor(f"conv_{n}", s, F32))
        tok = sb("tok", [P, NT, GROUP])
        sq = sb("sq", [P, NT, GROUP])
        st = sb("st", [P, 3, NT])
        col = sb("col", [P, 3, 2])
        pw = sb("pw", [P, 2, GROUP])
        act_in = sb("lin", [P, 2, TOK])
        sil = sb("sil", [P, 2, TOK])
        ps = es.enter_context(nc.psum_tensor("conv_ps", [P, 4, 2 * BANK], F32))
        names = "loaded own turned tok_kept varied rooted normed back sig_done lin_done silued done kept"
        with stage(nc, "conv", names) as (block, loaded, own, turned, tok_kept, varied, rooted,
                                          normed, back, sig_done, lin_done, silued, done, kept):
            @block.sync
            def _(sp):
                one = lambda n: A[n][bass.ds(layer, 1), :].rearrange("a (c p) -> p (a c)", p=P)
                for n, v in enumerate(("conv_ln_g", "conv_ln_b", "conv_pw_b")):
                    sp.dma_start(col[:, n, :], one(v), allow_slow_non_contiguous=True).then_inc(loaded, 16)
                sp.dma_start(pw[:, :, :], A["conv_pw_w"][bass.ds(layer, 1)].rearrange("a (c p) n -> p (a c) n", p=P)).then_inc(loaded, 16)

            @block.scalar
            def _(act):
                for i in range(NT):
                    act.wait_ge(turned, i + 1)
                    nc.scalar.activation(tok[:, i, :], ps[:, i % 4, 0:GROUP], ACT.Copy).then_inc(tok_kept, 1)
                act.wait_ge(varied, 1)
                nc.scalar.activation(st[:, 1, :], st[:, 1, :], ACT.Sqrt).then_inc(rooted, 1)
                for c in range(2):
                    act.wait_ge(back, c + 1)
                    act.wait_ge(loaded, 16 * 4)
                    nc.scalar.activation(act_in[:, c, :], ps[:, c, 0:TOK], ACT.Identity, scale=col[:, 0, c:c + 1], bias=col[:, 1, c:c + 1]).then_inc(lin_done, 1)
                    nc.scalar.activation(sil[:, c, :], ps[:, c, 0:TOK], ACT.Sigmoid, scale=col[:, 0, c:c + 1], bias=col[:, 1, c:c + 1]).then_inc(sig_done, 1)
                for c in range(2):
                    act.wait_ge(done, c + 1)
                    nc.scalar.activation(yT[:, 2 + c, :], ps[:, 2 + c, 0:TOK], ACT.Identity, bias=col[:, 2, c:c + 1]).then_inc(kept, 1)

            @block.vector
            def _(dve):
                o = Own(dve, own)
                dve.wait_ge(tok_kept, NT)
                o.then(nc.vector.tensor_reduce(st[:, 0, :], tok[:, :, :], AX.X, ALU.add))
                o.then(nc.vector.tensor_scalar(st[:, 0, :], st[:, 0, :], 1.0 / GROUP, None, ALU.mult))
                o.then(nc.vector.tensor_tensor(tok[:, :, :], tok[:, :, :], st[:, 0, :].rearrange("p (t o) -> p t o", o=1)
                                               .broadcast_to([P, NT, GROUP]), ALU.subtract))
                o.then(nc.vector.tensor_tensor(sq[:, :, :], tok[:, :, :], tok[:, :, :], ALU.mult))
                o.then(nc.vector.tensor_reduce(st[:, 1, :], sq[:, :, :], AX.X, ALU.add))
                nc.vector.tensor_scalar(st[:, 1, :], st[:, 1, :], 1.0 / GROUP, EPS, ALU.mult, ALU.add).then_inc(varied, 1)
                dve.wait_ge(rooted, 1)
                o.then(nc.vector.reciprocal(st[:, 2, :], st[:, 1, :]))
                nc.vector.tensor_tensor(tok[:, :, :], tok[:, :, :], st[:, 2, :].rearrange("p (t o) -> p t o", o=1)
                                        .broadcast_to([P, NT, GROUP]), ALU.mult).then_inc(normed, 1)
                for c in range(2):
                    dve.wait_ge(sig_done, c + 1)
                    dve.wait_ge(lin_done, c + 1)
                    nc.vector.tensor_tensor(sil[:, c, :], sil[:, c, :], act_in[:, c, :], ALU.mult).then_inc(silued, 1)

            @block.tensor
            def _(pe):
                ident = cst[:, C_ID:C_ID + P]
                for i in range(NT):
                    if i >= 4:
                        pe.wait_ge(tok_kept, i - 3)
                    at = i * P + (PAD if i >= NTX else 0)
                    for c in range(2):
                        last = nc.tensor.transpose(ps[:, i % 4, c * P:(c + 1) * P], acc[:, c, at:at + P], ident)
                    last.then_inc(turned, 1)
                pe.wait_ge(normed, 1)
                for c in range(2):
                    for i in range(NT):
                        last = nc.tensor.transpose(ps[:, c, i * P:(i + 1) * P], tok[:, i, c * P:(c + 1) * P], ident)
                    last.then_inc(back, 1)
                pe.wait_ge(silued, 2)
                pe.wait_ge(loaded, 16 * 4)
                for c in range(2):
                    for t0, tw in ((0, SEQ), (SEQ, CTX)):
                        for k in range(2):
                            last = nc.tensor.matmul(ps[:, 2 + c, t0:t0 + tw], pw[:, k, c * P:(c + 1) * P], sil[:, k, t0:t0 + tw],
                                                    start=(k == 0), stop=(k == 1))
                    last.then_inc(done, 1)


def recurrence(nc, A, g, layer):
    pt, pf, cst, yT, cum = g["pt"], g["pf"], g["cst"], g["yT"], g["cum"]
    G = 2
    KC, VC, GC = 6, 1024, 1280
    q = pf[:, 4:6, :]
    kk = [pf[:, KC + 2 * d:KC + 2 * d + 2, :] for d in range(2)]
    scr = pf[:, 0:4, :].rearrange("p a t -> p (a t)").rearrange("p (g i h t) -> p g i h t", g=G, i=NT, h=2)
    ORDER = ([4, 5, 0, 1, 2, 3], [5, 4, 3, 2, 1, 0])
    NG = NT // TILES_A_MASK
    HALF = P // 2

    def group(d, lev, j):
        return (d * LEVELS + lev) * NG + j

    with ExitStack() as es:
        sb = lambda n, s: es.enter_context(nc.sbuf_tensor(f"rec_{n}", s, F32))
        e1, e2, e3 = (sb(n, [P, G, TOK]) for n in ("e1", "e2", "e3"))
        qe = sb("qe", [P, 2, G * NT, 2, HALF])
        ke = sb("ke", [P, 2, G, TOK])
        dec = sb("dec", [P, 2, G, NT])
        state = sb("state", [P, 2, NT, G, P])
        same = sb("same", [P, NT * 4])
        rs = sb("rs", [P, NT * 4])
        onorm = sb("onorm", [P, HEAD])
        pair = sb("pair", [P, 2])
        qc = [ke[:, d, :, :] for d in range(2)]
        ktok = [qe[:, d, :, :, :].rearrange("p a h t -> p (a h t)").rearrange("p (i c) -> p i c", c=GROUP) for d in range(2)]
        osum = kk[0].rearrange("p g t -> p (g t)").rearrange("p (i c) -> p i c", c=GROUP)
        ps_s = es.enter_context(nc.psum_tensor("rec_ps_s", [P, 2, 2, BANK], F32))
        ps_o = es.enter_context(nc.psum_tensor("rec_ps_o", [P, 2, BANK], F32))
        ps_u = es.enter_context(nc.psum_tensor("rec_ps_u", [P, 2, BANK], F32))
        names = ("loaded own own_p pair_set keys_zero cleared state_zero paired level_diff level_exp q_low q_high k_factors scored picked same_done "
                 "carry_diff carry_exp q_carried k_carried turned turned_kept updated state_used states_done out_done out_kept "
                 "varied rooted sig gate_out back back_kept")
        with stage(nc, "rec", names) as (block, loaded, own, own_p, pair_set, keys_zero, cleared, state_zero, paired, level_diff, level_exp, q_low, q_high, k_factors,
                                         scored, picked, same_done, carry_diff, carry_exp, q_carried, k_carried, turned, turned_kept,
                                         updated, state_used, states_done, out_done, out_kept, varied, rooted, sig, gate_out, back,
                                         back_kept):
            def by_tile(ap):
                return ap.rearrange("p g (i t) -> p (g i) t", t=P)

            cum_t = [cum[:, d, :, :, :].rearrange("p g i t -> p (g i) t") for d in range(2)]

            def half(ap, n, a):
                return ap.rearrange("p a (b x t) -> p a b x t", x=2, t=n)[:, :, :, a, :]

            def packed(ap, n):
                return ap.rearrange("p (a b t) -> p a b t", a=G * NT, t=n)

            def level_queries(eng, d, lev, hf):
                n = 1 << lev
                part = slice(HEAD * hf, HEAD * hf + HEAD)
                return eng.tensor_tensor(qe[part, lev % 2, :, hf, :].rearrange("p a (b t) -> p a b t", t=n), half(by_tile(q[part]), n, 1 - d),
                                         packed((e2, e3)[lev % 2][part, 1 - d, :], n), ALU.mult)

            @block.sync
            def _(sp):
                sp.dma_start(onorm[:, :], A["hgrn_onorm_g"][bass.ds(layer, 1), :].broadcast_to([P, HEAD])).then_inc(loaded, 16)

            @block.scalar
            def _(act):
                for d in range(2):
                    for lev in range(LEVELS):
                        step = d * LEVELS + lev
                        act.wait_ge(level_diff, step + 1)
                        if step >= 2:
                            used = max(s for s in range(step) if (s % LEVELS) % 2 == lev % 2) + 1
                            for sem in (q_low, q_high, k_factors):
                                act.wait_ge(sem, used)
                        nc.scalar.activation((e2, e3)[lev % 2][:, :, :], e1[:, :, :], ACT.Exp).then_inc(level_exp, 1)
                for sem in (q_low, q_high, k_factors):
                    act.wait_ge(sem, 2 * LEVELS)
                for d in range(2):
                    if d:
                        act.wait_ge(q_carried, 1)
                    nc.scalar.activation(by_tile(e2[:, :, :]), cum_t[d][:, :, 1 - d:1 - d + P], ACT.Exp).then_inc(carry_exp, 1)
                    nc.scalar.activation(dec[:, d, :, :], cum[:, d, :, :, P], ACT.Exp).then_inc(carry_exp, 1)
                    to_end = (e1, e3)[d]
                    act.wait_ge(carry_diff, d + 1)
                    nc.scalar.activation(to_end[:, :, :], to_end[:, :, :], ACT.Exp).then_inc(carry_exp, 1)
                for d in range(2):
                    for i in range(NT):
                        act.wait_ge(turned, NT * d + i + 1)
                        nc.scalar.activation(ktok[d][:, i, :], ps_s[:, i % 2, 0, 0:GROUP], ACT.Copy).then_inc(turned_kept, 1)
                act.wait_ge(q_carried, 2)
                nc.scalar.activation(e3[:, :, :].rearrange("p g (i c) -> p (g i) c", c=GROUP), pt[:, :, GC:GC + GROUP], ACT.Sigmoid).then_inc(sig, 1)
                act.wait_ge(varied, 1)
                nc.scalar.activation(rs[:, :], rs[:, :], ACT.Sqrt).then_inc(rooted, 1)
                for i in range(NT):
                    act.wait_ge(back, i + 1)
                    nc.scalar.activation(yT[:, 6:8, i * P:(i + 1) * P], ps_s[:, i % 2, 0, 0:2 * P].rearrange("p (a b) -> p a b", b=P), ACT.Copy).then_inc(back_kept, 1)

            @block.gpsimd
            def _(pool):
                nc.gpsimd.memset(pair[:, :], 0.0).then_inc(own_p, 1)
                pool.wait_ge(own_p, 1)
                for hf in range(2):
                    if hf:
                        pool.wait_ge(pair_set, 1)
                    nc.gpsimd.memset(pair[HEAD * hf:HEAD * hf + HEAD, hf:hf + 1], 1.0).then_inc(pair_set, 1)
                pool.wait_ge(pair_set, 2)
                nc.gpsimd.memset(ke[:, :, :, :], 0.0).then_inc(keys_zero, 1)
                pool.wait_ge(keys_zero, 1)
                pool.wait_ge(cleared, 2)
                for d in range(2):
                    for lev in range(LEVELS):
                        n = 1 << lev
                        step = d * LEVELS + lev
                        if step >= 2:
                            used = max(s for s in range(step) if (s % LEVELS) % 2 == lev % 2)
                            pool.wait_ge(scored, NG * (used + 1))
                        pool.wait_ge(level_exp, step + 1)
                        if step:
                            pool.wait_ge(k_factors, step)
                        level_queries(nc.gpsimd, d, lev, 1).then_inc(q_high, 1)
                        pool.wait_ge(q_high, step + 1)
                        nc.gpsimd.tensor_tensor(half(by_tile(ke[:, lev % 2, :, :]), n, d), half(by_tile(kk[d]), n, d),
                                                packed((e2, e3)[lev % 2][:, d, :], n), ALU.mult).then_inc(k_factors, 1)
                nc.gpsimd.memset(state[:, :, :, :, :], 0.0).then_inc(state_zero, 1)

            @block.vector
            def _(dve):
                o = Own(dve, own)
                tt = nc.vector.tensor_tensor

                def distances(d, lev):
                    n = 1 << lev
                    at = cum_t[d][:, :, 1 - d:1 - d + P]
                    mid = cum_t[d][:, :, 0:P].rearrange("p a (b t) -> p a b t", t=2 * n)[:, :, :, n:n + 1].broadcast_to([P, G * NT, P // (2 * n), n])
                    if d or lev:
                        dve.wait_ge(level_exp, LEVELS * d + lev)
                    o(tt(packed(e1[:, 0, :], n), mid, half(at, n, 0), ALU.subtract))
                    o(tt(packed(e1[:, 1, :], n), half(at, n, 1), mid, ALU.subtract))
                    o.settle()
                    dve.sem_inc(level_diff, 1)

                def targets(d, lev):
                    dve.wait_ge(level_exp, LEVELS * d + lev + 1)
                    level_queries(nc.vector, d, lev, 0).then_inc(q_low, 1)

                steps = [(d, lev) for d in range(2) for lev in range(LEVELS)]
                o.then(tt(e3[:, :, :], kk[0], kk[1], ALU.add))
                tt(e3[:, :, :], e3[:, :, :], q, ALU.mult).then_inc(paired, 1)
                distances(0, 0)
                nc.vector.memset(qe[:, :, :, :, :], 0.0).then_inc(cleared, 1)
                nc.vector.memset(scr, 0.0).then_inc(cleared, 1)
                dve.wait_ge(cleared, 2)
                dve.wait_ge(same_done, 1)
                o.then(nc.vector.tensor_copy(same[:, :], ps_u[:, 0, 0:4 * NT]))
                targets(0, 0)
                distances(0, 1)
                for s, (d, lev) in enumerate(steps):
                    n = 1 << lev
                    if s + 1 < len(steps):
                        if lev + 1 == LEVELS:
                            dve.wait_ge(scored, NG * (s + 1))
                        targets(*steps[s + 1])
                    if s + 2 < len(steps):
                        distances(*steps[s + 2])
                    for j in range(NG):
                        m = NG * s + j
                        dve.wait_ge(scored, m + 1)
                        if s:
                            dve.wait_ge(picked, m - NG + 1)
                        w = TILES_A_MASK
                        nb = w * P // n
                        src = ps_s[:, m % 2, :, 0:w * P].rearrange("p g (b t) -> p g b t", t=n)
                        dst = scr[:, :, j * w:(j + 1) * w, :, :].rearrange("p g i h (b x t) -> p g (i h b) x t", x=2, t=n)[:, :, :, 1 - d, :]
                        cm = C_LEV[d][lev]
                        mask = cst[:, cm:cm + nb].bitcast(U32).rearrange("p (a b t) -> p a b t", a=1, t=1)
                        nc.vector.copy_predicated(dst, mask.broadcast_to([P, 2, nb, n]), src).then_inc(picked, 1)
                for d in range(2):
                    to_start, to_end = e2[:, :, :], (e1, e3)[d][:, :, :]
                    tt(by_tile(to_end), cum_t[d][:, :, P:P + 1].broadcast_to([P, G * NT, P]), cum_t[d][:, :, 1 - d:1 - d + P],
                       ALU.subtract).then_inc(carry_diff, 1)
                for d in range(2):
                    dve.wait_ge(carry_exp, 3 * (d + 1))
                    to_start, to_end = e2[:, :, :], (e1, e3)[d][:, :, :]
                    tt(qc[d], q, (to_start, to_end)[d], ALU.mult).then_inc(q_carried, 1)
                    key = (to_end, to_start)[d]
                    tt(key, kk[d], key, ALU.mult).then_inc(k_carried, 1)
                dve.wait_ge(state_zero, 1)
                for d in range(2):
                    for n in range(NT - 1):
                        i, nxt = ORDER[d][n], ORDER[d][n + 1]
                        dve.wait_ge(updated, (NT - 1) * d + n + 1)
                        for hf in range(2):
                            part = slice(HEAD * hf, HEAD * hf + HEAD)
                            for gg in range(G):
                                src = ps_u[part, n % 2, gg * P + HEAD * hf:gg * P + HEAD * hf + HEAD]
                                new = state[part, d, nxt, gg, HEAD * hf:HEAD * hf + HEAD]
                                if n == 0:
                                    o(nc.vector.tensor_copy(new, src))
                                else:
                                    o(nc.vector.scalar_tensor_tensor(new, state[part, d, i, gg, HEAD * hf:HEAD * hf + HEAD],
                                                                     dec[part, d, gg, i:i + 1], src, ALU.mult, ALU.add))
                        o.settle()
                        dve.sem_inc(states_done, 1)
                heads = lambda ap: ap.rearrange("p i (h e) -> p (i h) e", e=HEAD)
                wide = lambda e: e[:, :, :].rearrange("p g (i c) -> p (g i) c", c=GROUP)
                split = lambda ap: ap.rearrange("p i (h e) -> p i h e", e=HEAD)
                o.then(tt(split(osum), split(pt[:, :, VC:VC + GROUP]), same[:, :].rearrange("p (i h o) -> p i h o", i=NT, o=1).broadcast_to([P, NT, 4, HEAD]), ALU.mult))
                for i in range(NT):
                    dve.wait_ge(out_done, i + 1)
                    o(tt(osum[:, i, :], osum[:, i, :], ps_o[:, i % 2, 0:GROUP], ALU.add))
                    o.settle()
                    dve.sem_inc(out_kept, 1)
                o.then(tt(wide(e1), osum, osum, ALU.mult))
                o.then(nc.vector.tensor_reduce(rs[:, :], heads(wide(e1)), AX.X, ALU.add))
                nc.vector.tensor_scalar(rs[:, :], rs[:, :], 1.0 / HEAD, EPS, ALU.mult, ALU.add).then_inc(varied, 1)
                dve.wait_ge(sig, 1)
                o.then(tt(wide(e3), wide(e3), pt[:, :, GC:GC + GROUP], ALU.mult))
                dve.wait_ge(loaded, 16)
                o.then(tt(heads(wide(e3)), heads(wide(e3)), onorm[:, :].rearrange("p (o e) -> p o e", o=1).broadcast_to([P, 4 * NT, HEAD]), ALU.mult))
                dve.wait_ge(rooted, 1)
                o.then(nc.vector.reciprocal(rs[:, :], rs[:, :]))
                o.then(tt(heads(osum), heads(osum), rs[:, :].rearrange("p (h o) -> p h o", o=1).broadcast_to([P, 4 * NT, HEAD]), ALU.mult))
                tt(osum, osum, wide(e3), ALU.mult).then_inc(gate_out, 1)

            @block.tensor
            def _(pe):
                ident = cst[:, C_ID:C_ID + P]
                pe.wait_ge(paired, 1)
                pe.wait_ge(pair_set, 2)
                for i in range(NT):
                    for gg in range(G):
                        last = nc.tensor.matmul(ps_u[:, 0, 4 * i + 2 * gg:4 * i + 2 * gg + 2], e3[:, gg, i * P:(i + 1) * P], pair[:, :], start=True, stop=True)
                last.then_inc(same_done, 1)
                for d in range(2):
                    for lev in range(LEVELS):
                        step = d * LEVELS + lev
                        for sem in (q_low, q_high, k_factors):
                            pe.wait_ge(sem, step + 1)
                        for j in range(NG):
                            m = group(d, lev, j)
                            if m >= 2:
                                pe.wait_ge(picked, m - 1)
                            for n in range(TILES_A_MASK):
                                i = j * TILES_A_MASK + n
                                for gg in range(G):
                                    last = nc.tensor.matmul(ps_s[:, m % 2, gg, n * P:(n + 1) * P], ke[:, lev % 2, gg, i * P:(i + 1) * P],
                                                            qe[:, lev % 2, gg * NT + i, :, :].rearrange("p h t -> p (h t)"), start=True, stop=True)
                            last.then_inc(scored, 1)
                pe.wait_ge(picked, NG * 2 * LEVELS)
                for d in range(2):
                    pe.wait_ge(k_carried, d + 1)
                    for i in range(NT):
                        if d or i >= 2:
                            pe.wait_ge(turned_kept, NT * d + i - 1)
                        for gg in range(G):
                            last = nc.tensor.transpose(ps_s[:, i % 2, 0, gg * P:(gg + 1) * P], (e1, e2)[d][:, gg, i * P:(i + 1) * P], ident)
                        last.then_inc(turned, 1)
                for d in range(2):
                    for n, i in enumerate(ORDER[d][:-1]):
                        m = (NT - 1) * d + n
                        pe.wait_ge(turned_kept, NT * (d + 1))
                        if m >= 2:
                            pe.wait_ge(states_done, m - 1 if n != 0 else m)
                        for gg in range(G):
                            last = nc.tensor.matmul(ps_u[:, n % 2, gg * P:(gg + 1) * P], ktok[d][:, i, gg * P:(gg + 1) * P],
                                                    pt[:, i, VC + gg * P:VC + (gg + 1) * P], start=True, stop=True)
                        last.then_inc(updated, 1)
                pe.wait_ge(states_done, 2 * (NT - 1))
                pe.wait_ge(q_carried, 2)
                for i in range(NT):
                    if i >= 2:
                        pe.wait_ge(out_kept, i - 1)
                    for gg in range(G):
                        for d in range(2):
                            if d:
                                for hf in range(2):
                                    c = gg * P + hf * HEAD
                                    nc.tensor.matmul(ps_o[:, i % 2, c:c + HEAD], scr[:, gg, i, hf, :], pt[:, i, VC + c:VC + c + HEAD],
                                                     start=False, stop=False)
                            last = nc.tensor.matmul(ps_o[:, i % 2, gg * P:(gg + 1) * P], qc[d][:, gg, i * P:(i + 1) * P], state[:, d, i, gg, :],
                                                    start=(d == 0), stop=(d == 1))
                    last.then_inc(out_done, 1)
                pe.wait_ge(gate_out, 1)
                for i in range(NT):
                    if i >= 2:
                        pe.wait_ge(back_kept, i - 1)
                    for a in range(2):
                        last = nc.tensor.transpose(ps_s[:, i % 2, 0, a * P:(a + 1) * P], osum[:, i, a * P:(a + 1) * P], ident)
                    last.then_inc(back, 1)


def gates_scalar(act, pf, scratch, step, sems):
    e1, e2, _, e4 = scratch
    own_a, exp_arg, first_ln, diff, lse_ln, k_arg, k_exp = sems
    d = step // 3
    if step % 3 == 0:
        act.wait_ge(exp_arg, d + 1)
        act.activation(e1[:, :, :], e1[:, :, :], ACT.Exp).then_inc(own_a, 1)
        act.wait_ge(own_a, 2 * d + 1)
        act.activation(e2[:, :, :], e1[:, :, :], ACT.Ln, bias=1.0).then_inc(first_ln, 1)
    elif step % 3 == 1:
        act.wait_ge(diff, d + 1)
        act.activation(e4[:, :, :], e4[:, :, :], ACT.Exp).then_inc(own_a, 1)
        act.wait_ge(own_a, 2 * d + 2)
        act.activation(e4[:, :, :], e4[:, :, :], ACT.Ln, bias=1.0).then_inc(lse_ln, 1)
    else:
        act.wait_ge(k_arg, d + 1)
        z = pf[:, 6 + 2 * d:8 + 2 * d, :]
        act.activation(z, z, ACT.Exp).then_inc(k_exp, 1)


def gates_vector(v, dve, o, layer, lb, lbl, pf, cst, cum, scratch, sems):
    e1, e2, e3, e4 = scratch
    exp_arg, first_ln, diff, lse_ln, k_arg, k_exp = sems
    tt = v.tensor_tensor
    o(v.memset(cum[:, :, :, :, 0], 0.0))
    o.then(v.tensor_copy(lbl[:, :, :], lb[:, bass.ds(layer, 1), :, :].rearrange("p a b c -> p (a b) c")))
    for d in range(2):
        z = pf[:, 6 + 2 * d:8 + 2 * d, :]
        o.then(v.tensor_scalar(e3[:, :, :], z, 0.0, None, ALU.min))
        o(v.scalar_tensor_tensor(e1[:, :, :], e3[:, :, :], 2.0, z, ALU.mult, ALU.subtract))
        o.then(tt(z, e3[:, :, :], z, ALU.subtract))
        dve.sem_inc(exp_arg, 1)
        dve.wait_ge(first_ln, d + 1)
        for gg in range(2):
            o(v.tensor_scalar(e1[:, gg, :], z[:, gg, :], lbl[:, 1, 2 * d + gg:2 * d + gg + 1], None, ALU.add))
        o.settle()
        o.then(tt(e4[:, :, :], e3[:, :, :], e1[:, :, :], ALU.subtract))
        v.scalar_tensor_tensor(e4[:, :, :], e4[:, :, :], -1.0, e4[:, :, :], ALU.mult, ALU.min).then_inc(diff, 1)
        tt(z, z, e2[:, :, :], ALU.subtract).then_inc(k_arg, 1)
        o.then(tt(e3[:, :, :], e3[:, :, :], e1[:, :, :], ALU.max))
        o.then(tt(e3[:, :, :], e3[:, :, :], e2[:, :, :], ALU.subtract))
        dve.wait_ge(lse_ln, d + 1)
        o.then(tt(e3[:, :, :], e3[:, :, :], e4[:, :, :], ALU.add))
        ones = cst[:, C_COL:C_COL + 1].broadcast_to([P, P])
        for gg in range(2):
            for i in range(NT):
                o(v.tensor_tensor_scan(cum[:, d, gg, i, 1:P + 1], ones, e3[:, gg, i * P:(i + 1) * P], 0.0, ALU.mult, ALU.add))
        dve.wait_ge(k_exp, d + 1)
        for gg in range(2):
            o(v.tensor_scalar(z[:, gg, :], z[:, gg, :], lbl[:, 2, 2 * d + gg:2 * d + gg + 1], None, ALU.mult))
        o.settle()


def gated_add(dve, o, g, gate, ps, i, h, tmp):
    x = g["x"]
    s = 0 if i < NTX else 1
    o.then(dve.tensor_tensor(tmp, ps, gate[:, s, h * BANK:(h + 1) * BANK], ALU.mult))
    return dve.tensor_tensor(x[:, i, h * BANK:(h + 1) * BANK], x[:, i, h * BANK:(h + 1) * BANK], tmp, ALU.add)


def out_projection(nc, A, g, layer):
    yT = g["yT"]
    jobs = [(h, i) for h in range(2) for i in range(NT)]
    with ExitStack() as es:
        w = es.enter_context(nc.sbuf_tensor("w_out_t", [P, 2, KT, BANK], F32))
        gate = es.enter_context(nc.sbuf_tensor("out_gate", [P, 2, D], F32))
        tmp = es.enter_context(nc.sbuf_tensor("out_tmp", [P, BANK], F32))
        pr = es.enter_context(nc.psum_tensor("out_ps_row", [P, 2, 2 * BANK], F32))
        ps = es.enter_context(nc.psum_tensor("out_ps", [P, 4, BANK], F32))
        with stage(nc, "outp", "w0 w1 spread gates own done added") as (block, w0, w1, spread, gates, own, done, added):
            w_in = (w0, w1)

            @block.sync
            def _(sp):
                for h in range(2):
                    sp.dma_start(w[:, h, :, :], A["w_out"][bass.ds(layer, 1), :, h * BANK:(h + 1) * BANK]
                                 .rearrange("a (k p) n -> p (a k) n", p=P)).then_inc(w_in[h], 16)

            @block.tensor
            def _(pe):
                for s in range(2):
                    broadcast_row(nc, g, pr[:, s, :], 2, s).then_inc(spread, 1)
                for n, (h, i) in enumerate(jobs):
                    if i == 0:
                        pe.wait_ge(w_in[h], 16)
                    if n >= 4:
                        pe.wait_ge(added, n - 3)
                    for k in range(KT):
                        last = nc.tensor.matmul(ps[:, n % 4, :], yT[:, k, i * P:(i + 1) * P], w[:, h, k, :], start=(k == 0), stop=(k == KT - 1))
                    last.then_inc(done, 1)

            @block.scalar
            def _(act):
                for s in range(2):
                    act.wait_ge(spread, s + 1)
                    nc.scalar.activation(gate[:, s, :], pr[:, s, :], ACT.Copy).then_inc(gates, 1)

            @block.vector
            def _(dve):
                o = Own(dve, own)
                dve.wait_ge(gates, 2)
                for n, (h, i) in enumerate(jobs):
                    dve.wait_ge(done, n + 1)
                    if n:
                        dve.wait_ge(added, n)
                    gated_add(nc.vector, o, g, gate, ps[:, n % 4, :], i, h, tmp[:, :]).then_inc(added, 1)


MAX_EXTRA = 64
N_VALS = 6
N_SLOT_TAB = N_EXP + MAX_EXTRA


def route_and_share(nc, A, g, layer, hT, gate, y_dram, r):
    cst = g["cst"]
    E = N_EXP
    SPANS = ((0, SEQ), (SEQ, CTX))
    jobs = [(i, h) for i in range(NT) for h in range(2)]
    with ExitStack() as es:
        sb = lambda n, s: es.enter_context(nc.sbuf_tensor(f"rt_{n}", s, F32))
        wr = sb("w", [P, KT, E])
        bias = sb("bias", [P, E])
        sc = sb("score", [P, NT, E])
        sel = sb("sel", [P, NT, E])
        best = sb("best", [P, NT, N_GRP, 8])
        gs = sb("gsum", [P, NT, N_GRP])
        gt = sb("gt", [P, NT, N_GRP, N_GRP])
        eq = sb("eq", [P, NT, N_GRP, N_GRP])
        keep = sb("keep", [P, NT, N_GRP])
        pen = sb("pen", [P, NT, N_GRP])
        top = sb("top", [P, NT, 8])
        rep = sb("rep", [P, NT, E])
        msk = sb("mask", [P, NT, E])
        den = sb("den", [P, NT])
        ones = sb("ones", [P, P])
        extra = sb("extra", [P, E])
        cumx = sb("cumx", [P, E])
        over = sb("over", [P, E])
        le = sb("le", [P, E])
        colx = sb("colx", [P, 3])
        dg = sb("dg", [P, 2, MAX_EXTRA])
        npair = sb("npair", [1, 4])
        wgu = sb("wgu", [P, KT, 2 * HID])
        wd = sb("wd", [P, 2, D])
        sig = sb("sig", [P, 2, TOK])
        hid = sb("hid", [P, 2, TOK])
        tmp = sb("tmp", [P, 2, BANK])
        zero = sb("zero", [P, D])
        ps_r = es.enter_context(nc.psum_tensor("rt_ps_r", [P, BANK], F32))
        ps_c = es.enter_context(nc.psum_tensor("rt_ps_c", [P, BANK], F32))
        ps_gu = es.enter_context(nc.psum_tensor("rt_ps_gu", [P, 4, BANK], F32))
        ps_y = es.enter_context(nc.psum_tensor("rt_ps_y", [P, 2, BANK], F32))
        names = ("router_in gu_in down_in zero_set zeroed ahead logits scored own chosen ranked extras listed spread gates gu_done sig_done "
                 "half_hid hid_done y_done y_used scaled")
        with stage(nc, "route", names) as (block, router_in, gu_in, down_in, zero_set, zeroed, ahead, logits, scored, own, chosen, ranked,
                                           extras, listed, spread, gates, gu_done, sig_done, half_hid, hid_done, y_done, y_used, scaled):
            @block.sync
            def _(sp):
                rows = lambda n: A[n][bass.ds(layer, 1)].rearrange("a (k p) n -> p (a k) n", p=P)
                sp.dma_start(wr[:, :, :], rows("router_w")).then_inc(router_in, 16)
                sp.dma_start(bias[:, :], A["router_bias"][bass.ds(layer, 1), :].broadcast_to([P, E])).then_inc(router_in, 16)
                for n, c in (("sh_w_gate", 0), ("sh_w_up", HID)):
                    sp.dma_start(wgu[:, :, c:c + HID], rows(n)).then_inc(gu_in, 16)
                sp.dma_start(wd[:, :, :], rows("sh_w_down")).then_inc(down_in, 16)
                sp.wait_ge(zero_set, 1)
                for i in range(NT + 1):
                    sp.dma_start(y_dram[i * P:(i + 1) * P, :], zero[:, :]).then_inc(zeroed, 16)
                for e in range(2):
                    one = lambda n: A[n][bass.ds(layer, 1), e:e + 1].rearrange("a e (k p) n -> p (a e k) n", p=P)
                    for n, c in (("exp_w_gate", 0), ("exp_w_up", HID)):
                        sp.dma_start(r["w_gu"][:, e, :, c:c + HID], one(n)).then_inc(ahead, 16)
                    sp.dma_start(r["w_down"][:, e, :, :], one("exp_w_down")).then_inc(ahead, 16)
                sp.wait_ge(zeroed, 16 * (NT + 1))
                sp.wait_ge(ahead, 16 * 6)

            @block.gpsimd
            def _(pool):
                nc.gpsimd.memset(zero[:, :], 0.0).then_inc(zero_set, 1)

            @block.scalar
            def _(act):
                act.wait_ge(logits, 1)
                nc.scalar.activation(sc[:, :, :].rearrange("p a b -> p (a b)"), ps_y[:, 0, 0:NT * E], ACT.Sigmoid).then_inc(scored, 1)
                for n, (t0, tw) in enumerate(SPANS):
                    act.wait_ge(gu_done, n + 1)
                    nc.scalar.activation(sig[:, :, t0:t0 + tw], ps_gu[:, 0:2, 0:tw], ACT.Sigmoid).then_inc(sig_done, 1)
                    act.wait_ge(spread, n + 1)
                    nc.scalar.activation(gate[:, n, :], ps_y[:, :, :].rearrange("p a b -> p (a b)"), ACT.Copy).then_inc(gates, 1)

            @block.tensor
            def _(pe):
                pe.wait_ge(router_in, 32)
                for i in range(NT):
                    for k in range(KT):
                        last = nc.tensor.matmul(ps_y[:, 0, i * E:(i + 1) * E], hT[:, k, i * P:(i + 1) * P], wr[:, k, :], start=(k == 0), stop=(k == KT - 1))
                last.then_inc(logits, 1)

                def hidden(n):
                    t0, tw = SPANS[n]
                    for m in range(4):
                        for k in range(KT):
                            last = nc.tensor.matmul(ps_gu[:, m, 0:tw], wgu[:, k, m * P:(m + 1) * P], hT[:, k, t0:t0 + tw], start=(k == 0), stop=(k == KT - 1))
                    last.then_inc(gu_done, 1)

                pe.wait_ge(gu_in, 32)
                hidden(0)
                pe.wait_ge(scored, 1)
                broadcast_row(nc, g, ps_y[:, :, :].rearrange("p a b -> p (a b)"), 5, 0).then_inc(spread, 1)
                pe.wait_ge(chosen, 1)
                for i in range(NT):
                    nc.tensor.matmul(ps_r[:, i * E:(i + 1) * E], cst[:, C_TRI:C_TRI + P], msk[:, i, :], start=True, stop=(i == 0))
                    for j in range(i):
                        nc.tensor.matmul(ps_r[:, i * E:(i + 1) * E], ones[:, :], msk[:, j, :], start=False, stop=(j == i - 1))
                for j in range(NT):
                    last = nc.tensor.matmul(ps_c[:, 0:E], ones[:, :], msk[:, j, :], start=(j == 0), stop=(j == NT - 1))
                last.then_inc(ranked, 1)
                pe.wait_ge(gates, 1)
                broadcast_row(nc, g, ps_y[:, :, :].rearrange("p a b -> p (a b)"), 5, 1).then_inc(spread, 1)
                pe.wait_ge(hid_done, 1)
                hidden(1)
                pe.wait_ge(down_in, 16)
                pe.wait_ge(gates, 2)
                for n, (i, h) in enumerate(jobs):
                    if i == NTX and h == 0:
                        pe.wait_ge(hid_done, 2)
                        pe.wait_ge(extras, 1)
                        nc.tensor.matmul(ps_c[:, E:E + 2 * MAX_EXTRA], ones[:, :], dg[:, :, :].rearrange("p a b -> p (a b)"), start=True, stop=True).then_inc(listed, 1)
                    if n >= 2:
                        pe.wait_ge(scaled, n - 1)
                    for a in range(2):
                        last = nc.tensor.matmul(ps_y[:, h, :], hid[:, a, i * P:(i + 1) * P], wd[:, a, h * BANK:(h + 1) * BANK], start=(a == 0), stop=(a == 1))
                    last.then_inc(y_done, 1)

            @block.vector
            def _(dve):
                x = g["x"]

                def hidden_values(n):
                    t0, tw = SPANS[n]
                    dve.wait_ge(sig_done, n + 1)
                    s_n = sig[:, :, t0:t0 + tw]
                    nc.vector.tensor_tensor(s_n, s_n, ps_gu[:, 0:2, 0:tw], ALU.mult).then_inc(half_hid, 1)
                    dve.wait_ge(half_hid, n + 1)
                    nc.vector.tensor_tensor(hid[:, :, t0:t0 + tw], s_n, ps_gu[:, 2:4, 0:tw], ALU.mult).then_inc(hid_done, 1)

                def add_results(n):
                    i, h = jobs[n]
                    s = 0 if i < NTX else 1
                    dve.wait_ge(y_done, n + 1)
                    if n >= 2:
                        dve.wait_ge(y_used, n - 1)
                    nc.vector.tensor_tensor(tmp[:, n % 2, :], ps_y[:, h, :], gate[:, s, h * BANK:(h + 1) * BANK], ALU.mult).then_inc(scaled, 1)
                    dve.wait_ge(scaled, n + 1)
                    nc.vector.tensor_tensor(x[:, i, h * BANK:(h + 1) * BANK], x[:, i, h * BANK:(h + 1) * BANK], tmp[:, n % 2, :], ALU.add).then_inc(y_used, 1)

                v = nc.vector
                o = Own(dve, own)
                o(v.memset(ones[:, :], 1.0))
                dve.wait_ge(scored, 1)
                dve.wait_ge(router_in, 32)
                o.then(v.tensor_tensor(sel[:, :, :], sc[:, :, :], bias[:, :].rearrange("p (o e) -> p o e", o=1).broadcast_to([P, NT, E]), ALU.add))
                for i in range(NT):
                    for q in range(N_GRP):
                        o(v.max(out=best[:, i, q, :], in_=sel[:, i, q * PER_GRP:(q + 1) * PER_GRP]))
                o.settle()
                o.then(v.tensor_tensor(gs[:, :, :], best[:, :, :, 0], best[:, :, :, 1], ALU.add))
                for i in range(NT):
                    other = gs[:, i, :].rearrange("p (o k) -> p o k", o=1).broadcast_to([P, N_GRP, N_GRP])
                    self_ = gs[:, i, :].rearrange("p (j o) -> p j o", o=1).broadcast_to([P, N_GRP, N_GRP])
                    o(v.tensor_tensor(gt[:, i, :, :], other, self_, ALU.is_gt))
                    o(v.tensor_tensor(eq[:, i, :, :], other, self_, ALU.is_equal))
                o.settle()
                low = cst[:, C_LOW:C_LOW + 64].rearrange("p (o n) -> p o n", o=1).broadcast_to([P, NT, 64])
                flat = lambda ap: ap.rearrange("p i a b -> p i (a b)")
                o.then(v.tensor_tensor(flat(eq[:, :, :, :]), flat(eq[:, :, :, :]), low, ALU.mult))
                o.then(v.tensor_tensor(gt[:, :, :, :], gt[:, :, :, :], eq[:, :, :, :], ALU.add))
                o.then(v.tensor_reduce(keep[:, :, :], gt[:, :, :, :], AX.X, ALU.add))
                o.then(v.tensor_scalar(keep[:, :, :], keep[:, :, :], 3.5, None, ALU.is_lt))
                o.then(v.tensor_scalar(pen[:, :, :], keep[:, :, :], -1.0, -NEG, ALU.add, ALU.mult))
                grp = lambda ap: ap.rearrange("p i (q e) -> p (i q) e", e=PER_GRP)
                wide = lambda ap: ap.rearrange("p i (q o) -> p (i q) o", o=1).broadcast_to([P, NT * N_GRP, PER_GRP])
                o.then(v.tensor_tensor(grp(sel[:, :, :]), grp(sel[:, :, :]), wide(keep[:, :, :]), ALU.mult))
                o.then(v.tensor_tensor(grp(sel[:, :, :]), grp(sel[:, :, :]), wide(pen[:, :, :]), ALU.add))
                for i in range(NT):
                    o(v.max(out=top[:, i, :], in_=sel[:, i, :]))
                o.settle()
                for i in range(NT):
                    o(v.match_replace(out=rep[:, i, :], in_to_replace=top[:, i, :], in_values=sel[:, i, :], imm_value=2 * NEG))
                o.settle()
                o.then(v.tensor_scalar(msk[:, :, :], rep[:, :, :], 1.5 * NEG, None, ALU.is_lt))
                o.then(v.tensor_tensor(sel[:, :, :], sc[:, :, :], msk[:, :, :], ALU.mult))
                o.then(v.tensor_reduce(den[:, :], sel[:, :, :], AX.X, ALU.add))
                o.then(v.reciprocal(den[:, :], den[:, :]))
                o.then(v.tensor_tensor(sel[:, :, :], sel[:, :, :], den[:, :].rearrange("p (t o) -> p t o", o=1).broadcast_to([P, NT, E]), ALU.mult))
                o.then(v.tensor_scalar(sel[:, :, :], sel[:, :, :], ROUTED_SCALE, None, ALU.mult))
                vals = r["vals"][:, :, :].rearrange("p t (e c) -> p t e c", c=N_VALS)
                for part in range(3):
                    o.then(v.tensor_copy(vals[:, :, :, 3 + part], sel[:, :, :]))
                    if part < 2:
                        o.then(v.tensor_tensor(sel[:, :, :], sel[:, :, :], vals[:, :, :, 3 + part], ALU.subtract))
                o.then(v.tensor_scalar(msk[:, NTX:NT, :], msk[:, NTX:NT, :], cst[:, bass.ds(layer + (C_COL + 10), 1)], None, ALU.mult))
                dve.sem_inc(chosen, 1)
                for c, at in ((0, C_COL + 16), (1, C_COL + 22)):
                    half = cst[:, at:at + NT].rearrange("p (t o) -> p t o", o=1).broadcast_to([P, NT, E])
                    o(v.tensor_copy(vals[:, :, :, c], half))
                o(v.memset(vals[:, :, :, 2], 1.0))
                hidden_values(0)
                dve.wait_ge(ranked, 1)
                rank = r["rank"]
                o.then(v.scalar_tensor_tensor(rank[:, :, :].rearrange("p a b -> p (a b)"), ps_r[:, 0:NT * E], 1.0,
                                              msk[:, :, :].rearrange("p a b -> p (a b)"), ALU.add, ALU.mult))
                o(v.tensor_scalar(rank[:, :, :], rank[:, :, :], -1.0, None, ALU.add))
                o.then(v.tensor_scalar(extra[:, :], ps_c[:, 0:E], float(P), None, ALU.is_gt))
                for m in range(2, NT):
                    o.then(v.tensor_scalar(over[:, :], ps_c[:, 0:E], float(m * P), None, ALU.is_gt))
                    o.then(v.tensor_tensor(extra[:, :], extra[:, :], over[:, :], ALU.add))
                o.then(v.tensor_tensor_scan(cumx[:, :], cst[:, C_COL:C_COL + 1].broadcast_to([P, E]), extra[:, :], 0.0, ALU.mult, ALU.add))
                row = cst[:, C_COL + 1:C_COL + 2]
                o.then(v.tensor_scalar(le[:, :], cumx[:, :], row, None, ALU.is_le))
                o.then(v.tensor_reduce(colx[:, 0:1], le[:, :], AX.X, ALU.add))
                o.then(v.tensor_tensor(le[:, :], le[:, :], extra[:, :], ALU.mult))
                o.then(v.tensor_reduce(colx[:, 1:2], le[:, :], AX.X, ALU.add))
                o.then(v.tensor_tensor(colx[:, 1:2], row, colx[:, 1:2], ALU.subtract))
                o.then(v.tensor_scalar(colx[:, 1:2], colx[:, 1:2], 1.0, float(P), ALU.add, ALU.mult))
                o.then(v.tensor_scalar(colx[:, 2:3], colx[:, 0:1], E - 0.5, 1e6, ALU.is_gt, ALU.mult))
                o.then(v.tensor_tensor(colx[:, 1:2], colx[:, 1:2], colx[:, 2:3], ALU.add))
                o.then(v.tensor_scalar(colx[:, 0:1], colx[:, 0:1], float(E - 1), None, ALU.min))
                for a in range(2):
                    o(v.tensor_scalar(dg[:, a, :], cst[:, C_ID:C_ID + MAX_EXTRA], colx[:, a:a + 1], None, ALU.mult))
                o.settle()
                dve.sem_inc(extras, 1)
                first, expert = r["first"], r["expert"]
                o(v.memset(first[:, 0:E], 0.0))
                o(v.tensor_copy(expert[:, 0:E], cst[0:1, C_IOTA:C_IOTA + E]))
                hidden_values(1)
                dve.wait_ge(gates, 2)
                for n in range(len(jobs) // 2):
                    add_results(n)
                dve.wait_ge(listed, 1)
                o(v.tensor_copy(expert[:, E:E + MAX_EXTRA], ps_c[0:1, E:E + MAX_EXTRA]))
                o(v.tensor_copy(first[:, E:E + MAX_EXTRA], ps_c[:, E + MAX_EXTRA:E + 2 * MAX_EXTRA]))
                o.then(v.tensor_copy(r["n_i"][:, 0:1], cumx[0:1, E - 1:E]))
                o.then(v.tensor_scalar(r["n_i"][:, 1:2], r["n_i"][:, 0:1], 1, None, ALU.bitwise_and))
                o.then(v.tensor_copy(npair[:, 0:2], r["n_i"][:, 0:2]))
                o.then(v.tensor_tensor(npair[:, 2:3], npair[:, 0:1], npair[:, 1:2], ALU.add))
                o.then(v.tensor_scalar(npair[:, 2:3], npair[:, 2:3], float(E), None, ALU.add))
                o.then(v.tensor_copy(r["n_i"][:, 2:3], npair[:, 2:3]))
                for n in range(len(jobs) // 2, len(jobs)):
                    add_results(n)


def routed_experts(nc, A, g, layer, r, h_dram, y_dram):
    cst = g["cst"]
    rank, vals, first, expert, n_i = r["rank"], r["vals"], r["first"], r["expert"], r["n_i"]
    wgu, wd = r["w_gu"], r["w_down"]
    with ExitStack() as es:
        sb = lambda n, s, dt=F32: es.enter_context(nc.sbuf_tensor(f"ex_{n}", s, dt))
        hot = sb("hot", [P, NT, P], BF16)
        slot = sb("slot", [P, 2, N_VALS])
        tok = sb("tok", [P, 2])
        miss = sb("miss", [P, 2])
        at_in = sb("at_in", [P, 2, 1], I32)
        at_out = sb("at_out", [P, 2, 1], I32)
        wt = sb("wt", [P, 2, 1])
        rows = sb("rows", [P, 2, D])
        rowsT = sb("rowsT", [P, 2, D])
        sig = sb("sig", [P, HID])
        hid = sb("hid", [P, HID])
        res = sb("res", [P, 2, D])
        pt = lambda n, s: es.enter_context(nc.psum_tensor(f"ex_ps_{n}", s, F32))
        ps_i = pt("i", [P, BANK])
        ps_x = pt("x", [P, 2 * BANK])
        ps_g = pt("g", [P, BANK])
        ps_up = pt("up", [P, BANK])
        ps_y = pt("y", [P, 2 * BANK])
        names = ("gu0 gu1 dn0 dn1 hot_done slots copied summed missed idx_ready out_ready taken turned rowsT_done g_done gu_done sig_done half_hid "
                 "hid_done y_done res_done out_free")
        with stage(nc, "experts", names, g["rows_sems"]) as (
                block, gu0, gu1, dn0, dn1, hot_done, slots, copied, summed, missed, idx_ready, out_ready, taken, turned, rowsT_done, g_done, gu_done,
                sig_done, half_hid, hid_done, y_done, res_done, out_free):
            gu_in, dn_in = (gu0, gu1), (dn0, dn1)
            gathered, scattered = g["rows_sems"][0:2], g["rows_sems"][2:4]

            def count(eng):
                return eng.value_load(n_i[0:1, 2:3], min_val=N_EXP, max_val=N_EXP + MAX_EXTRA - 4)

            def expert_of(eng, b):
                return eng.value_load(expert[0:1, bass.ds(b, 1)], min_val=0, max_val=N_EXP - 1)

            def blocks(eng, body):
                body(0, 0)
                body(1, 1)
                with eng.Fori(2, count(eng), 2) as b0:
                    body(b0, 0)
                    body(b0 + 1, 1)

            def wait(eng, sem, value):
                if not (isinstance(value, int) and value == 0):
                    eng.wait_ge(sem, value)

            def seen(b, a, units=16):
                return (b - a) * (units // 2) + units

            @block.sync
            def _(sp):
                def body(b, a):
                    e = expert_of(sp, b)
                    sp.wait_ge(gu_done, b - 1)
                    for n, c in (("exp_w_gate", 0), ("exp_w_up", HID)):
                        sp.dma_start(wgu[:, a, :, c:c + HID], A[n][bass.ds(layer, 1), bass.ds(e, 1)]
                                     .rearrange("a e (k p) n -> p (a e k) n", p=P)).then_inc(gu_in[a], 16)
                    sp.wait_ge(y_done, b - 1)
                    sp.dma_start(wd[:, a, :, :], A["exp_w_down"][bass.ds(layer, 1), bass.ds(e, 1)]
                                 .rearrange("a e (k p) n -> p (a e k) n", p=P)).then_inc(dn_in[a], 16)

                with sp.Fori(2, count(sp), 2) as b0:
                    body(b0, 0)
                    body(b0 + 1, 1)

            @block.gpsimd
            def _(pool):
                def gather(b, a):
                    pool.wait_ge(idx_ready, b + 1)
                    pool.sem_inc(taken, 1)
                    pool.indirect_dma_start(out=rows[:, a, :], out_offset=None, in_=h_dram[:, :],
                                            in_offset=bass.IndirectOffsetOnAxis(ap=at_in[:, a, :], axis=0)).then_inc(gathered[a], 16)

                def body(b, a):
                    pool.wait_ge(turned, b + 1)
                    gather(b + 2, a)
                    if not (isinstance(b, int) and b == 0):
                        pool.wait_ge(scattered[1 - a], seen(b - 1, 1 - a))
                        pool.sem_inc(out_free, 1)
                    pool.wait_ge(res_done, b + 1)
                    pool.sem_inc(taken, 1)
                    pool.indirect_dma_start(out=y_dram[:, :], out_offset=bass.IndirectOffsetOnAxis(ap=at_out[:, a, :], axis=0),
                                            in_=res[:, a, :], in_offset=None, compute_op=ALU.add).then_inc(scattered[a], 16)

                gather(0, 0)
                gather(1, 1)
                blocks(pool, body)
                n = count(pool)
                pool.wait_ge(scattered[1], n * 8)
                for a in range(2):
                    pool.wait_ge(gathered[a], n * 8 + 16)
                pool.sem_inc(taken, 1)
                pool.dma_reset(range(gathered[0].num, scattered[1].num + 1))

            @block.vector
            def _(dve):
                v = nc.vector

                def find(b):
                    e = expert_of(dve, b)
                    wait(dve, slots, b)
                    for i in range(NT):
                        last = v.tensor_scalar(hot[:, i, :], cst[:, C_IOTA:C_IOTA + P], first[:, bass.ds(b, 1)],
                                               rank[:, i, bass.ds(e, 1)], ALU.add, ALU.is_equal)
                    last.then_inc(hot_done, 1)

                def place_in(b, a):
                    dve.wait_ge(slots, b + 1)
                    v.tensor_copy(slot[:, a, :], ps_i[:, 0:N_VALS]).then_inc(copied, 1)
                    dve.wait_ge(copied, b + 1)
                    v.tensor_tensor(tok[:, a:a + 1], slot[:, a, 0:1], slot[:, a, 1:2], ALU.add).then_inc(summed, 1)
                    dve.wait_ge(summed, b + 1)
                    if not isinstance(b, int):
                        dve.wait_ge(gathered[a], seen(b - 2, a))
                    v.tensor_copy(at_in[:, a, :], tok[:, a:a + 1]).then_inc(idx_ready, 1)

                def place_out(b, a):
                    if not (isinstance(b, int) and b < 2):
                        dve.wait_ge(out_free, b - 1)
                    v.scalar_tensor_tensor(wt[:, a, :], slot[:, a, 3:4], slot[:, a, 4:5], slot[:, a, 5:6], ALU.add, ALU.add)
                    v.tensor_scalar(miss[:, a:a + 1], slot[:, a, 2:3], -1.0, 1.0, ALU.mult, ALU.add).then_inc(missed, 1)
                    dve.wait_ge(missed, b + 1)
                    v.scalar_tensor_tensor(at_out[:, a, :], miss[:, a:a + 1], cst[:, C_COL + 2:C_COL + 3], tok[:, a:a + 1],
                                           ALU.mult, ALU.add).then_inc(out_ready, 1)

                def body(b, a):
                    find(b + 2)
                    dve.wait_ge(sig_done, b + 1)
                    v.tensor_tensor(sig[:, :], sig[:, :], ps_g[:, 0:HID], ALU.mult).then_inc(half_hid, 1)
                    dve.wait_ge(half_hid, b + 1)
                    dve.wait_ge(gu_done, b + 1)
                    v.tensor_tensor(hid[:, :], sig[:, :], ps_up[:, 0:HID], ALU.mult).then_inc(hid_done, 1)
                    place_in(b + 2, a)
                    place_out(b + 1, 1 - a)

                for b in range(2):
                    find(b)
                    place_in(b, b)
                place_out(0, 0)
                blocks(dve, body)

            @block.scalar
            def _(act):
                def turn(b, a):
                    act.wait_ge(turned, b + 1)
                    nc.scalar.activation(rowsT[:, a, :], ps_x[:, :], ACT.Copy).then_inc(rowsT_done, 1)

                def body(b, a):
                    act.wait_ge(g_done, b + 1)
                    nc.scalar.activation(sig[:, :], ps_g[:, 0:HID], ACT.Sigmoid).then_inc(sig_done, 1)
                    turn(b + 1, 1 - a)
                    act.wait_ge(y_done, b + 1)
                    act.wait_ge(out_ready, b + 1)
                    nc.scalar.activation(res[:, a, :], ps_y[:, :], ACT.Copy, scale=wt[:, a, :]).then_inc(res_done, 1)

                turn(0, 0)
                blocks(act, body)

            @block.tensor
            def _(pe):
                ident = cst[:, C_ID:C_ID + P]

                def slots_of(b):
                    e = expert_of(pe, b)
                    pe.wait_ge(hot_done, b + 1)
                    wait(pe, copied, b)
                    for i in range(NT):
                        last = nc.tensor.matmul(ps_i[:, 0:N_VALS], hot[:, i, :], vals[:, i, bass.ds(e * N_VALS, N_VALS)], start=(i == 0), stop=(i == NT - 1))
                    last.then_inc(slots, 1)

                def turn(b, a):
                    pe.wait_ge(gathered[a], seen(b, a))
                    wait(pe, rowsT_done, b)
                    for k in range(KT):
                        last = nc.tensor.transpose(ps_x[:, k * P:(k + 1) * P], rows[:, a, k * P:(k + 1) * P], ident)
                    last.then_inc(turned, 1)

                def body(b, a):
                    if not isinstance(b, int):
                        pe.wait_ge(gu_in[a], (b - a) * 16)
                    pe.wait_ge(rowsT_done, b + 1)
                    wait(pe, hid_done, b)
                    for m in range(4):
                        for k in range(KT):
                            last = nc.tensor.matmul((ps_g, ps_up)[m // 2][:, m % 2 * P:(m % 2 + 1) * P], wgu[:, a, k, m * P:(m + 1) * P],
                                                    rowsT[:, a, k * P:(k + 1) * P], start=(k == 0), stop=(k == KT - 1))
                        if m == 1:
                            last.then_inc(g_done, 1)
                    last.then_inc(gu_done, 1)
                    turn(b + 1, 1 - a)
                    slots_of(b + 2)
                    pe.wait_ge(hid_done, b + 1)
                    if not isinstance(b, int):
                        pe.wait_ge(dn_in[a], (b - a) * 8)
                    wait(pe, res_done, b)
                    for h in range(2):
                        for m in range(2):
                            last = nc.tensor.matmul(ps_y[:, h * BANK:(h + 1) * BANK], hid[:, m * P:(m + 1) * P],
                                                    wd[:, a, m, h * BANK:(h + 1) * BANK], start=(m == 0), stop=(m == 1))
                    last.then_inc(y_done, 1)

                slots_of(0)
                slots_of(1)
                turn(0, 0)
                blocks(pe, body)


def combine(nc, A, g, layer, y_dram, gate):
    x = g["x"]
    with ExitStack() as es:
        y = es.enter_context(nc.sbuf_tensor("cb_y", [P, NT, D], F32))
        with stage(nc, "combine", "in0 in1 in2 in3 in4 in5 own") as (block, *arrived, own):
            @block.sync
            def _(sp):
                for i in range(NT):
                    sp.dma_start(y[:, i, :], y_dram[i * P:(i + 1) * P, :]).then_inc(arrived[i], 16)

            @block.vector
            def _(dve):
                o = Own(dve, own)
                for i in range(NT):
                    s = 0 if i < NTX else 1
                    dve.wait_ge(arrived[i], 16)
                    o.then(nc.vector.tensor_tensor(y[:, i, :], y[:, i, :], gate[:, s, :], ALU.mult))
                    o(nc.vector.tensor_tensor(x[:, i, :], x[:, i, :], y[:, i, :], ALU.add))


def moe(nc, A, g, layer, h_dram, y_dram):
    with ExitStack() as es:
        sb = lambda n, s, dt=F32: es.enter_context(nc.sbuf_tensor(f"moe_{n}", s, dt))
        gate = sb("gate", [P, 2, D])
        r = {"rank": sb("rank", [P, NT, N_EXP]), "vals": sb("vals", [P, NT, N_EXP * N_VALS], BF16), "first": sb("first", [P, N_SLOT_TAB]),
             "expert": sb("expert", [1, N_SLOT_TAB], I32), "n_i": sb("n_i", [1, 4], I32),
             "w_gu": sb("w_gu", [P, 2, KT, 2 * HID]), "w_down": sb("w_down", [P, 2, 2, D])}
        with nc.sbuf_tensor("h2T", [P, KT, TOK], F32) as hT:
            norm_rows(nc, A, g, layer, 3, "norm2_g", hT, h_dram)
            route_and_share(nc, A, g, layer, hT, gate, y_dram, r)
        routed_experts(nc, A, g, layer, r, h_dram, y_dram)
        combine(nc, A, g, layer, y_dram, gate)


_INS = ("x c ctx c_ctx w_mod b_mod norm1_g norm2_g w_in w_out gqa_q_gain gqa_k_gain win_q_gain win_k_gain win_sink "
        "conv_dw_w conv_dw_b conv_ln_g conv_ln_b conv_pw_w conv_pw_b hgrn_lb_logits hgrn_onorm_g router_w router_bias "
        "exp_w_gate exp_w_up exp_w_down sh_w_gate sh_w_up sh_w_down").split()


def kernel(**inputs):
    import concourse.bacc as bacc
    from concourse.bass_utils import run_bass_kernel_spmd

    nc = bacc.Bacc("TRN2", target_bir_lowering=False, num_devices=1)
    arrays = {f"in_{n}": np.ascontiguousarray(inputs[n]) for n in _INS}
    arrays["in_consts"] = shape_constants()
    A = {n[3:]: nc.dram_tensor(n, a.shape, mybir.dt.from_np(a.dtype), kind="ExternalInput").ap() for n, a in arrays.items()}
    out = nc.dram_tensor("out", (1, SEQ, D), F32, kind="ExternalOutput").ap()
    build(nc, A, out)
    got = run_bass_kernel_spmd(nc, [arrays], core_ids=[0])
    return got.results[0]["out"]
```
